# Optimizing a Trainium2 kernel written in Bass

```python
import jax, jax.numpy as jnp
from jax import lax
import numpy as np

D_MODEL = 1024
BATCH = 1
SEQ = 1024
DEPTH = 1
DEC_BATCH = 1
DEC_SEQ = 64
PAST_LEN = 512

CHUNK = 64
GMLP_CHUNK = 128
GMLP_WIDTH = 1024
GMLP_GROUPS = 8
GMLP_GROUP_DIM = GMLP_WIDTH // GMLP_GROUPS
N_HEADS = 16
N_KV_HEADS = 4
GQA_GROUP = N_HEADS // N_KV_HEADS
HEAD_DIM = 64
ATTN_WIDTH = N_HEADS * HEAD_DIM
KV_WIDTH = N_KV_HEADS * HEAD_DIM
WINDOW = 128
WIN_CHUNKS = WINDOW // CHUNK
D_FF = 2816
CONV_W = 3
EPS = 1e-6
NEG_INF = -1e30
SPLITS = [GMLP_WIDTH, 2 * GMLP_WIDTH, 2 * GMLP_WIDTH + ATTN_WIDTH,
          2 * GMLP_WIDTH + ATTN_WIDTH + KV_WIDTH, 2 * GMLP_WIDTH + ATTN_WIDTH + 2 * KV_WIDTH]
IN_COLS = 2 * GMLP_WIDTH + ATTN_WIDTH + 2 * KV_WIDTH + 2 * D_MODEL

kernel_name = 'hybrid_gmlp_swa_convffn_stream_step'

def rms_norm(x, g):
    xf = x.astype(jnp.float32)
    y = xf * lax.rsqrt(jnp.mean(xf * xf, axis=-1, keepdims=True) + EPS)
    return (y * g.astype(jnp.float32)).astype(x.dtype)

def layer_norm(x, g, b):
    xf = x.astype(jnp.float32)
    mu = jnp.mean(xf, axis=-1, keepdims=True)
    xc = xf - mu
    y = xc * lax.rsqrt(jnp.mean(xc * xc, axis=-1, keepdims=True) + EPS)
    return (y * g.astype(jnp.float32) + b.astype(jnp.float32)).astype(x.dtype)

def alibi_slopes():
    return jnp.exp2(-8.0 * jnp.arange(1, N_HEADS + 1, dtype=jnp.float32) / N_HEADS)

def gmlp_spatial(u, vn, w_s, b_s):
    B, S, _ = u.shape
    L = min(S, GMLP_CHUNK)
    nc = S // L
    idx = jnp.arange(L)
    mask = (idx[None, :] // CHUNK) <= (idx[:, None] // CHUNK)
    w = w_s[:, :L, :L] * mask[None].astype(w_s.dtype)
    vg = vn.reshape(B, nc, L, GMLP_GROUPS, GMLP_GROUP_DIM)
    s = jnp.einsum('gts,bnsgc->bntgc', w, vg) + b_s[:, :L].T[None, None, :, :, None]
    return u * s.reshape(B, S, GMLP_WIDTH)

def sink_attend(qc, kb, vb, dist, valid, sinks):
    s = jnp.einsum('bnqhgd,bnshd->bnhgqs', qc, kb).astype(jnp.float32) * (HEAD_DIM ** -0.5)
    slopes = alibi_slopes().reshape(N_KV_HEADS, GQA_GROUP, 1, 1)
    s = jnp.where(valid, s - slopes * dist.astype(jnp.float32), NEG_INF)
    sink = sinks.astype(jnp.float32).reshape(N_KV_HEADS, GQA_GROUP, 1, 1)
    m = jnp.maximum(jnp.max(s, axis=-1, keepdims=True), sink)
    e = jnp.exp(s - m)
    p = e / (jnp.sum(e, axis=-1, keepdims=True) + jnp.exp(sink - m))
    return jnp.einsum('bnhgqs,bnshd->bnqhgd', p.astype(vb.dtype), vb)

def swa_prompt(q, k, v, sinks):
    B, S = q.shape[0], q.shape[1]
    nc = S // CHUNK
    nb = WIN_CHUNKS + 1
    pad = ((0, 0), (WINDOW, 0), (0, 0), (0, 0))
    kc = jnp.pad(k, pad).reshape(B, nc + WIN_CHUNKS, CHUNK, N_KV_HEADS, HEAD_DIM)
    vc = jnp.pad(v, pad).reshape(B, nc + WIN_CHUNKS, CHUNK, N_KV_HEADS, HEAD_DIM)
    kb = jnp.concatenate([kc[:, i:i + nc] for i in range(nb)], axis=2)
    vb = jnp.concatenate([vc[:, i:i + nc] for i in range(nb)], axis=2)
    qc = q.reshape(B, nc, CHUNK, N_KV_HEADS, GQA_GROUP, HEAD_DIM)
    qi = jnp.arange(CHUNK)
    kj = jnp.arange(nb * CHUNK)
    dist = jnp.abs(qi[:, None] + WINDOW - kj[None, :])
    kpos = jnp.arange(nc)[:, None] * CHUNK - WINDOW + kj[None, :]
    valid = (kpos >= 0)[None, :, None, None, None, :]
    o = sink_attend(qc, kb, vb, dist, valid, sinks)
    return o.reshape(B, S, ATTN_WIDTH)

def swa_sample(q, k, v, cache_k, cache_v, sinks):
    B, n = q.shape[0], q.shape[1]
    w = cache_k.shape[1]
    kb = jnp.concatenate([cache_k, k], axis=1)[:, None]
    vb = jnp.concatenate([cache_v, v], axis=1)[:, None]
    qc = q.reshape(B, 1, n, N_KV_HEADS, GQA_GROUP, HEAD_DIM)
    dist = jnp.abs(jnp.arange(n)[:, None] + w - jnp.arange(w + n)[None, :])
    valid = jnp.ones((w + n,), dtype=bool)
    o = sink_attend(qc, kb, vb, dist, valid, sinks)
    return o.reshape(B, n, ATTN_WIDTH)

def conv_ffn(h, w_up, w_conv, b_conv, w_down, conv_state):
    B, S, _ = h.shape
    up = h @ w_up
    a, val = jnp.split(up, 2, axis=-1)
    hist = jnp.zeros((B, CONV_W - 1, D_FF), a.dtype) if conv_state is None else conv_state
    a_ext = jnp.concatenate([hist, a], axis=1)
    c = b_conv + sum(w_conv[i] * a_ext[:, i:i + S] for i in range(CONV_W))
    out = (jax.nn.gelu(c) * val) @ w_down
    return out, a_ext[:, -(CONV_W - 1):]

def trunk(x, params, caches):
    (ln_mix_g, w_in, ln_v_g, ln_v_b, w_s, b_s, attn_sinks, w_pa, w_pb, w_o,
     ln_ffn_g, w_up, w_conv, b_conv, w_down, ln_final_g) = params
    B, S, _ = x.shape
    new_k, new_v, new_conv, new_gv = [], [], [], []
    for l in range(DEPTH):
        h = rms_norm(x, ln_mix_g[l])
        proj = h @ w_in[l]
        u, vg, q, k, v, gates = jnp.split(proj, SPLITS, axis=-1)
        vn = layer_norm(jax.nn.gelu(vg), ln_v_g[l], ln_v_b[l])
        a_out = gmlp_spatial(jax.nn.gelu(u), vn, w_s[l], b_s[l])
        q = q.reshape(B, S, N_HEADS, HEAD_DIM)
        k = k.reshape(B, S, N_KV_HEADS, HEAD_DIM)
        v = v.reshape(B, S, N_KV_HEADS, HEAD_DIM)
        if caches is None:
            b_out = swa_prompt(q, k, v, attn_sinks[l])
            keep = min(WINDOW, S)
            new_k.append(k[:, S - keep:])
            new_v.append(v[:, S - keep:])
            conv_state = None
        else:
            b_out = swa_sample(q, k, v, caches[0][l], caches[1][l], attn_sinks[l])
            new_k.append(k)
            new_v.append(v)
            new_gv.append(vn)
            conv_state = caches[2][l]
        gate_a, gate_b = jnp.split(jax.nn.sigmoid(gates), 2, axis=-1)
        merged = gate_a * (a_out @ w_pa[l]) + gate_b * (b_out @ w_pb[l])
        x = x + merged @ w_o[l]
        f, conv_new = conv_ffn(rms_norm(x, ln_ffn_g[l]), w_up[l], w_conv[l], b_conv[l], w_down[l], conv_state)
        new_conv.append(conv_new)
        x = x + f
    y = rms_norm(x, ln_final_g)
    gv = jnp.stack(new_gv) if caches is not None else None
    return y, jnp.stack(new_k), jnp.stack(new_v), jnp.stack(new_conv), gv

def setup_inputs(seed: int = 0) -> dict:
    key = jax.random.key(seed)
    ks = jax.random.split(key, 24)
    f32 = jnp.float32
    rows = min(WINDOW, PAST_LEN)
    nrm = lambda k, shape, s: jax.random.normal(k, shape, f32) * s
    return {
        'x_prompt': nrm(ks[0], (BATCH, SEQ, D_MODEL), 1.0),
        'x_sample': nrm(ks[1], (DEC_BATCH, DEC_SEQ, D_MODEL), 1.0),
        'cache_k': nrm(ks[2], (DEPTH, DEC_BATCH, rows, N_KV_HEADS, HEAD_DIM), 1.0),
        'cache_v': nrm(ks[3], (DEPTH, DEC_BATCH, rows, N_KV_HEADS, HEAD_DIM), 1.0),
        'cache_conv': nrm(ks[4], (DEPTH, DEC_BATCH, CONV_W - 1, D_FF), 1.0),
        'ln_mix_g': 1.0 + nrm(ks[5], (DEPTH, D_MODEL), 0.02),
        'w_in': nrm(ks[6], (DEPTH, D_MODEL, IN_COLS), D_MODEL ** -0.5),
        'ln_v_g': 1.0 + nrm(ks[7], (DEPTH, GMLP_WIDTH), 0.02),
        'ln_v_b': nrm(ks[8], (DEPTH, GMLP_WIDTH), 0.02),
        'w_s': nrm(ks[9], (DEPTH, GMLP_GROUPS, GMLP_CHUNK, GMLP_CHUNK), GMLP_CHUNK ** -0.5),
        'b_s': 1.0 + nrm(ks[10], (DEPTH, GMLP_GROUPS, GMLP_CHUNK), 0.1),
        'attn_sinks': nrm(ks[11], (DEPTH, N_HEADS), 0.5),
        'w_pa': nrm(ks[12], (DEPTH, GMLP_WIDTH, D_MODEL), GMLP_WIDTH ** -0.5),
        'w_pb': nrm(ks[13], (DEPTH, ATTN_WIDTH, D_MODEL), ATTN_WIDTH ** -0.5),
        'w_o': nrm(ks[14], (DEPTH, D_MODEL, D_MODEL), D_MODEL ** -0.5),
        'ln_ffn_g': 1.0 + nrm(ks[15], (DEPTH, D_MODEL), 0.02),
        'w_up': nrm(ks[16], (DEPTH, D_MODEL, 2 * D_FF), D_MODEL ** -0.5),
        'w_conv': nrm(ks[17], (DEPTH, CONV_W, D_FF), CONV_W ** -0.5),
        'b_conv': nrm(ks[18], (DEPTH, D_FF), 0.02),
        'w_down': nrm(ks[19], (DEPTH, D_FF, D_MODEL), D_FF ** -0.5),
        'ln_final_g': 1.0 + nrm(ks[20], (D_MODEL,), 0.02),
    }

def reference(x_prompt, x_sample, cache_k, cache_v, cache_conv, ln_mix_g, w_in, ln_v_g, ln_v_b,
              w_s, b_s, attn_sinks, w_pa, w_pb, w_o, ln_ffn_g, w_up, w_conv, b_conv, w_down, ln_final_g):
    params = (ln_mix_g, w_in, ln_v_g, ln_v_b, w_s, b_s, attn_sinks, w_pa, w_pb, w_o,
              ln_ffn_g, w_up, w_conv, b_conv, w_down, ln_final_g)
    y_prompt, new_k_prompt, new_v_prompt, new_conv_prompt, _ = trunk(x_prompt, params, None)
    y_sample, new_k_sample, new_v_sample, new_conv_sample, new_gmlp_v_sample = trunk(
        x_sample, params, (cache_k, cache_v, cache_conv))
    return (y_prompt, y_sample, new_k_prompt, new_v_prompt, new_conv_prompt,
            new_k_sample, new_v_sample, new_conv_sample, new_gmlp_v_sample)


_drawn_inputs = setup_inputs


def setup_inputs(seed=0):
    import zlib

    import numpy as np

    out = dict(_drawn_inputs(seed))
    spreads = {}
    factors = {'ln_v_g': 8.113,
     'ln_v_b': 8.52,
     'attn_sinks': 4.075,
     'ln_ffn_g': 2.765,
     'b_conv': 5.543,
     'ln_final_g': 25.41,
     'cache_k': 3.927,
     'cache_v': 2.922,
     'b_s': 2.706}
    for name, (base, spread) in spreads.items():
        noise = np.random.default_rng([zlib.crc32(name.encode()), seed]).standard_normal(out[name].shape)
        drawn = base * np.exp(spread * noise) if base else spread * noise
        out[name] = __import__('jax').numpy.asarray(drawn.astype(out[name].dtype))
    for name, factor in factors.items():
        out[name] = (out[name] * factor).astype(out[name].dtype)
    return out
```

```python
from contextlib import ExitStack, contextmanager

import concourse.bass as bass
from concourse import mybir

F32 = mybir.dt.float32
F32R = mybir.dt.float32r
ALU = mybir.AluOpType
ACT = mybir.ActivationFunctionType

P = 128
D = 1024
KT = D // P
SEQ, DEC = 1024, 64
T = SEQ + DEC
NT = SEQ // P + 1
CACHE = 128
HEADS, KVH, HD = 16, 4, 64
FF = 2816
FT = FF // P
EPS = 1e-6
FFN_GROUP = 8
FAR = 2.56e32
NB = 364
U0, VG0, Q0, K0, GA0, GB0 = 0, 1024, 2048, 3072, 3584, 4608
EXT = T + 4
SAMP = SEQ + 4


ATT_TILE = 48


def rows_of(n):
    return P if n < NT - 1 else DEC


def keys_of(n):
    if n == 0:
        return 0, P, P
    return ((n - 1) * P, 2 * P, 0) if n < NT - 1 else (SEQ, CACHE + DEC, P - DEC)


def queries_of(n):
    return (n * P, 0) if n < NT - 1 else (T - P, P - DEC)


def key_tiles(n):
    if n == 0:
        return [(0, P)]
    return [(n - 1, P), (n, P)] if n < NT - 1 else [(NT - 1, CACHE), (NT, DEC)]


MIX = (["act", "act"], ["act", "group", "act", "group"], 3, ["group", "group"])
GATE = ([], ["act", "act"], KT // 2, [])
ATT = ([], ["act", "act", "group", "group"], (2, 2), [])
FFN = (["act", "dve", "act", "dve"], ["act", "dve", "group", "act", "dve", "group"], FT // 2 - 1,
       ["group", "group"])


class Count:

    def __init__(self):
        self.v, self.rate, self.i = {}, {}, 0

    def get(self, key, half=1):
        r = self.rate.get(key, 0) // half
        v = self.v.get(key, 0) // half
        return v + self.i * r if r else v

    def add(self, key, n=1):
        self.v[key] = self.v.get(key, 0) + n

    def slot(self, key="block"):
        return self.v.get(key, 0) % 2

    def block(self, kind):
        for _ in range(4 if kind == "group" else 1):
            self.tile(kind)
        self.add("block")

    def tile(self, kind):
        self.add(("freed", "act" if kind == "act" else "dve", self.slot("tile")))
        self.add("tile")

    @contextmanager
    def loop(self, eng, reps, kinds, **more):
        before = dict(self.v)
        dry = Count()
        for kind in kinds:
            dry.block(kind)
        for k, n in more.items():
            dry.add(k, n)
        assert not (dry.v.get("block", 0) % 2 or dry.v.get("tile", 0) % 2 or self.slot() or self.slot("tile"))
        self.rate = dry.v
        if isinstance(reps, tuple):
            with eng.Fori(0, reps[0]) as a:
                with eng.Fori(0, reps[1]) as b:
                    self.i = a * reps[1] + b
                    yield a, b
            reps = reps[0] * reps[1]
        else:
            with eng.Fori(0, reps) as i:
                self.i = i
                yield i
        for k, n in dry.v.items():
            assert self.v.get(k, 0) - before.get(k, 0) == n, (k, n)
            self.v[k] = before.get(k, 0) + n * reps
        self.rate, self.i = {}, 0


def program(nc, x_prompt, x_sample, cache_k, cache_v, cache_conv, ln_mix_g, w_in, ln_v_g, ln_v_b, w_s, b_s,
            attn_sinks, w_pa, w_pb, w_o, ln_ffn_g, w_up, w_conv, b_conv, w_down, ln_final_g,
            y_prompt, y_sample, new_k_prompt, new_v_prompt, new_conv_prompt, new_k_sample, new_v_sample,
            new_conv_sample, new_gmlp_v_sample, m1_spill):
    with ExitStack() as ctx:
        def sem(name):
            return ctx.enter_context(nc.semaphore(name))

        cursor = (nc.sbuf_base + 63) // 64 * 64

        def region(size):
            nonlocal cursor
            at = cursor
            cursor += (size + 63) // 64 * 64
            assert cursor <= nc.sbuf_usable_end, cursor
            return [at, at + size]

        def put(reg, name, shape, dt=F32, at=None):
            size = 4
            for s in shape[1:]:
                size *= s
            start = reg[0] + (reg[2] if len(reg) > 2 else 0) if at is None else reg[0] + at
            t = nc.alloc_sbuf_tensor_at(name, shape, dt, offset=start)
            assert start + size <= reg[1], (name, start + size - reg[1])
            if at is None:
                del reg[2:]
                reg.append(start - reg[0] + (size + 31) // 32 * 32)
            return t

        def again(reg):
            return reg[:2]

        r_h = region(2 * KT * T * 4)
        r_w = region(2 * 1024 * 4 * 3)
        r_s = region(NT * D * 4)
        r_a = region(KT * T * 4)
        r_g = region(3 * 2 * T * 4)
        r_t = region(16384)
        r_c = region(4416)

        h_hi = put(r_h, "h_hi", [P, KT, T], F32R)
        h_lo = put(r_h, "h_lo", [P, KT, T], F32R)
        h2_hi, h2_lo = h_hi, h_lo

        ident = put(r_c, "ident", [P, P])
        mean_mat = put(r_c, "mean_mat", [P, P])
        stat = put(r_c, "stat", [P, 3, 16])
        stat_y = put(r_c, "stat_y", [P, 3, 16])
        half_neg = put(r_c, "half_neg", [P, 1])
        ln_stats = put(r_c, "ln_stats", [P, 2, 2, 6])
        ln_mv = put(r_c, "ln_mv", [P, NT, 2])
        ln_rstd = put(r_c, "ln_rstd", [P, NT])
        slopes = put(r_c, "slopes", [P, HEADS])
        sinks = put(r_c, "sinks", [P, HEADS])
        sink_now = put(r_c, "sink_now", [P, 4])
        att_stat = put(r_c, "att_stat", [P, 2, 8, 4])
        conv_w = put(r_c, "conv_w", [P, 5, FT])
        ffn_c = put(r_c, "ffn_c", [P, FT + KT])
        conv_out = put(r_c, "conv_out", [P, 2, 2, FT])
        spare = put(r_c, "spare", [P, 4])

        r_w0 = again(r_w)
        xt = put(r_w0, "xt", [P, 2, D])
        xn = put(r_w0, "xn", [P, 2, D])
        mix_g = put(r_w0, "mix_g", [P, D])
        junk = put(r_w0, "junk", [P, D])
        raw = put(r_w, "raw", [P, 2, 1024])
        w_hi = put(r_w, "w_hi", [P, 2, 1024], F32R)
        w_lo = put(r_w, "w_lo", [P, 2, 1024], F32R)

        gs = put(r_s, "gs", [P, NT, D])
        r_v = [r_a[0], r_t[1]]
        wraw = put(r_v, "wraw", [P, KT, 256])
        wide_hi = put(r_v, "wide_hi", [P, 2, KT, 256], F32R)
        wide_lo = put(r_v, "wide_lo", [P, 2, KT, 256], F32R)
        lnv_g = put(r_v, "lnv_g", [P, D])
        lnv_b = put(r_v, "lnv_b", [P, D])
        ws_hi = put(r_v, "ws_hi", [P, KT, P], F32R)
        ws_lo = put(r_v, "ws_lo", [P, KT, P], F32R)
        bs = put(r_v, "bs", [P, KT, P])
        ws_raw = put(r_v, "ws_raw", [P, KT, P])
        tab_rows = put(r_v, "tab_rows", [P, 2, P])
        r_v2 = [r_a[0] + 8192, r_t[1]]
        vn_hi = put(r_v2, "vn_hi", [P, 2, D], F32R)
        vn_lo = put(r_v2, "vn_lo", [P, 2, D], F32R)

        acc = put(r_a, "acc", [P, KT, T])
        grp = put(r_g, "grp", [P, 2, T])
        grp_hi = put(r_g, "grp_hi", [P, 2, T], F32R)
        grp_lo = put(r_g, "grp_lo", [P, 2, T], F32R)
        xt2 = put(again(r_g), "xt2", [P, 2, D], at=2 * T * 4)
        gate = put(r_t, "gate", [P, 2, T])
        m1 = put(again(r_t), "m1", [P, 2, T])
        r_k = again(r_s)
        k_t = put(r_k, "k_t", [P, 2, T + CACHE])
        v_tok = put(r_k, "v_tok", [P, NT + 1, 256])
        k_now = put(r_k, "k_now", [P, T + CACHE])
        v_now = put(r_k, "v_now", [P, NT + 1, P])
        bias_now = put(r_k, "bias_now", [P, 4, 256])
        dist = put(r_k, "dist", [P, 256])
        r_t2 = again(r_t)
        sc_sb = put(r_t2, "sc_sb", [P, 3, 4, 256])
        pt_sb = put(r_t2, "pt_sb", [P, 2, 4, P])
        k_tok = put(again(r_t), "k_tok", [P, 3, 256])
        xres = put(again(r_s), "xres", [P, KT, T])
        r_f = again(r_a)
        a_ext = put(r_f, "a_ext", [P, 2, EXT])
        conv = put(r_f, "conv", [P, 2, EXT])
        sq = put(again(r_a), "sq", [P, KT, T])
        r_n = again(r_t)
        rb = put(r_n, "rb", [P, T])
        hn = put(r_n, "hn", [P, 2, T])
        r_y = again(r_t)
        fin_g = put(r_y, "fin_g", [P, D])
        r_y2 = again(r_a)
        y_sb = put(r_y2, "y_sb", [P, 2, D])
        y_junk = put(r_y2, "y_junk", [P, D])
        conv_rows = put(r_y2, "conv_rows", [2 * FT, 2, P])

        pset = [ctx.enter_context(nc.psum_tensor(f"pset{i}", [P, 3, 512], F32)) for i in range(2)]
        pex = ctx.enter_context(nc.psum_tensor("pex", [P, 2, 512], F32))

        s_ident = sem("s_ident")
        s_tab_in = sem("s_tab_in")
        s_row_in = sem("s_row_in")
        s_tab_t = sem("s_tab_t")
        s_tab = sem("s_tab")
        s_ws_hi = sem("s_ws_hi")
        s_ws = sem("s_ws")
        s_dist = sem("s_dist")
        s_distf = sem("s_distf")
        s_x_in = [sem(f"s_x_in{i}") for i in range(2)]
        s_sq = sem("s_sq")
        s_var = sem("s_var")
        s_rstd = sem("s_rstd")
        s_xn = sem("s_xn")
        s_xnt = sem("s_xnt")
        s_h_hi = sem("s_h_hi")
        s_h = sem("s_h")
        s_wide_in = sem("s_wide_in")
        s_kv_w = sem("s_kv_w")
        s_wide_hi = sem("s_wide_hi")
        s_wide = sem("s_wide")
        s_vt = sem("s_vt")
        s_vt_free = sem("s_vt_free")
        s_ln = sem("s_ln")
        s_ln_mv = sem("s_ln_mv")
        s_ln_v = sem("s_ln_v")
        s_ln_r = sem("s_ln_r")
        s_ln_a = sem("s_ln_a")
        s_vn = sem("s_vn")
        s_vn_hi = sem("s_vn_hi")
        s_vn_lo = sem("s_vn_lo")
        s_mixed = sem("s_mixed")
        s_s = sem("s_s")
        s_out = sem("s_out")
        s_vnout = sem("s_vnout")
        s_load = [sem(f"s_load{i}") for i in range(2)]
        s_w_hi = sem("s_w_hi")
        s_w = sem("s_w")
        s_tile = sem("s_tile")
        s_freed = {("freed", e, s): sem(f"s_freed_{e}{s}") for e in ("act", "dve") for s in range(2)}
        s_zero = sem("s_zero")
        s_prod = sem("s_prod")
        s_grp_hi = sem("s_grp_hi")
        s_grp = sem("s_grp")
        s_m1 = sem("s_m1")
        s_spill = sem("s_spill")
        s_ktr = sem("s_ktr")
        s_kt = sem("s_kt")
        s_cache = sem("s_cache")
        s_kv_out = sem("s_kv_out")
        s_now = sem("s_now")
        s_bias = sem("s_bias")
        s_q = sem("s_q")
        s_sc = sem("s_sc")
        s_smax = sem("s_smax")
        s_neg = sem("s_neg")
        s_exp = sem("s_exp")
        s_den = sem("s_den")
        s_p = sem("s_p")
        s_ptr = sem("s_ptr")
        s_pt = sem("s_pt")
        s_o = sem("s_o")
        s_b_hi = sem("s_b_hi")
        s_b = sem("s_b")
        s_x2_in = [sem(f"s_x2_in{i}") for i in range(2)]
        s_x2t = sem("s_x2t")
        s_x2 = sem("s_x2")
        s_m1_in = [sem(f"s_m1_in{i}") for i in range(2)]
        s_gb = sem("s_gb")
        s_sq2 = sem("s_sq2")
        s_ms = sem("s_ms")
        s_r0 = sem("s_r0")
        s_r1 = sem("s_r1")
        s_r2 = sem("s_r2")
        s_hn = sem("s_hn")
        s_hn_hi = sem("s_hn_hi")
        s_h2 = sem("s_h2")
        s_zext = sem("s_zext")
        s_c0 = sem("s_c0")
        s_c1 = sem("s_c1")
        s_conv = sem("s_conv")
        s_gelu = sem("s_gelu")
        s_tail = sem("s_tail")
        s_tail_t = sem("s_tail_t")
        s_tail_r = sem("s_tail_r")
        s_yt = sem("s_yt")
        s_ysq = sem("s_ysq")
        s_yv = sem("s_yv")
        s_yr = sem("s_yr")
        s_y = sem("s_y")
        s_y_out = [sem(f"s_y_out{i}") for i in range(2)]
        s_fin_g = sem("s_fin_g")

        def k_tiles(w):
            return w[0].rearrange("(k p) c -> p k c", p=P)

        w_in_v, w_up_v = k_tiles(w_in), k_tiles(w_up)
        w_pb_v = w_pb[0].rearrange("(h r) c -> r h c", r=HD)

        def token_rows(n):
            return x_prompt[0, n * P:(n + 1) * P, :] if n < NT - 1 else x_sample[0]

        def halves(t):
            return t[:, 0:2 * NB].rearrange("p (b n) -> p b n", b=2), t[:, 2 * NB:T]

        def pieces(s):
            return pset[s][:, 0:2, 0:NB], pset[s][:, 2, 0:T - 2 * NB]

        def row128(v):
            return v.rearrange("(a n) -> a n", a=1).broadcast_to([P, v.shape[0]])

        block = ctx.enter_context(nc.Block())

        @block.sync
        def _(sp):
            def wide(w, c0):
                if w:
                    sp.wait_ge(s_wide, w)
                sp.dma_start(wraw[:], w_in_v[:, :, bass.ds(c0, 256)]).then_inc(s_wide_in, 16)

            def load_x(n):
                if n >= 2:
                    sp.wait_ge(s_xn, n - 1)
                sp.dma_start(xt[0:rows_of(n), n % 2, :], token_rows(n)).then_inc(s_x_in[n % 2], 16)

            sp.dma_start(mix_g[:], row128(ln_mix_g[0])).then_inc(s_row_in, 16)
            load_x(0)
            load_x(1)
            wide(0, VG0)
            for n in range(2, NT):
                load_x(n)
            sp.dma_start(tab_rows[0:3 * FT, 0, :], w_conv[0].rearrange("i (f p) -> (i f) p", p=P)).then_inc(s_tab_in, 16)
            sp.dma_start(tab_rows[3 * FT:5 * FT, 0, :], cache_conv[0, 0].rearrange("i (f p) -> (i f) p", p=P)).then_inc(s_tab_in, 16)
            sp.dma_start(tab_rows[0:FT, 1, :], b_conv[0].rearrange("(f p) -> f p", p=P)).then_inc(s_tab_in, 16)
            sp.dma_start(tab_rows[FT:FT + KT, 1, :], ln_ffn_g[0].rearrange("(f p) -> f p", p=P)).then_inc(s_tab_in, 16)
            sp.dma_start(ws_raw[:], w_s[0].rearrange("g t s -> t g s")).then_inc(s_tab_in, 16)
            for w in range(1, 4):
                wide(w, VG0 + 256 * w)
            sp.dma_start(lnv_g[:], row128(ln_v_g[0])).then_inc(s_row_in, 16)
            sp.dma_start(lnv_b[:], row128(ln_v_b[0])).then_inc(s_row_in, 16)
            sp.dma_start(bs[:], b_s.rearrange("a g t -> a (g t)").broadcast_to([P, D])).then_inc(s_row_in, 16)
            sp.dma_start(sinks[:], attn_sinks.broadcast_to([P, HEADS])).then_inc(s_row_in, 16)

            c = Count()

            def load(srcs):
                s = c.slot()
                if c.v.get("block", 0) >= 2 or c.rate:
                    sp.wait_ge(s_w, c.get("block") - 1)
                else:
                    sp.wait_ge(s_h, NT)
                for place, src in srcs:
                    sp.dma_start(place(raw[:, s, :]), src).then_inc(s_load[s], 16)

            def part(h, k):
                return lambda slot: slot[64 * h:64 * h + 64].rearrange("p (k c) -> p k c", k=k)

            def proj(view, c0):
                load([(part(h, KT), view[64 * h:64 * h + 64, :, bass.ds(c0, P)]) for h in range(2)])

            def group(w, j, b):
                view = k_tiles(w)
                load([(part(h, 2), view[64 * h:64 * h + 64, bass.ds(2 * j, 2), 512 * b:512 * b + 512])
                      for h in range(2)])

            def load_m1(m, k):
                if not isinstance(m, int):
                    sp.wait_ge(s_prod, m + (KT - 1))
                sp.dma_start(m1[:, k, :], m1_spill[bass.ds(m, 1)].rearrange("a p t -> (a p) t"))\
                  .then_inc(s_m1_in[k], 16)

            def load_residual():
                sp.wait_ge(s_tile, c.get("tile") - 1)
                for k in range(2):
                    load_m1(k, k)
                for n in range(NT):
                    if n >= 2:
                        sp.wait_ge(s_x2t, n - 1)
                    sp.dma_start(xt2[0:rows_of(n), n % 2, :], token_rows(n)).then_inc(s_x2_in[n % 2], 16)

            def mix(c0, w, with_m1):
                pro, body, reps, epi = MIX
                for k in range(2):
                    proj(w_in_v, c0 + P * k)
                    if k == 1 and with_m1:
                        load_residual()
                    c.block(pro[k])
                with c.loop(sp, reps, body) as i:
                    for k in range(2):
                        if with_m1:
                            load_m1(i * 2 + (2 + k), k)
                        proj(w_in_v, i * 256 + (c0 + 256 + P * k))
                        c.block(body[2 * k])
                        group(w, i, k)
                        c.block(body[2 * k + 1])
                for b in range(2):
                    group(w, reps, b)
                    c.block(epi[b])

            mix(U0, w_pa, False)
            with c.loop(sp, GATE[2], GATE[1]) as i:
                for k in range(2):
                    proj(w_in_v, i * 256 + (GA0 + P * k))
                    c.block("act")
            with c.loop(sp, ATT[2], ATT[1]) as (pair, half):
                for k in range(2):
                    load([(lambda slot, h=h: slot.rearrange("p (k c) -> p k c", k=KT)[:, :, 64 * h:64 * h + 64],
                           w_in_v[:, :, bass.ds(pair * 512 + half * 128 + (Q0 + 256 * h + 64 * k), HD)])
                          for h in range(2)])
                    c.block("act")
                for b in range(2):
                    load([(part(h, 2), w_pb_v[:, bass.ds(pair * 8 + half * 2 + 4 * h, 2), 512 * b:512 * b + 512])
                          for h in range(2)])
                    c.block("group")
            mix(GB0, w_o, True)
            pro, body, reps, epi = FFN
            for k in range(2):
                proj(w_up_v, P * k)
                c.block(pro[0])
                proj(w_up_v, FF + P * k)
                c.block(pro[1])
            with c.loop(sp, reps, body) as i:
                for k in range(2):
                    proj(w_up_v, i * 256 + (256 + P * k))
                    c.block(body[0])
                    proj(w_up_v, i * 256 + (FF + 256 + P * k))
                    c.block(body[1])
                    group(w_down, i, k)
                    c.block(body[2])
            for b in range(2):
                group(w_down, reps, b)
                c.block(epi[b])
            sp.dma_start(fin_g[:], row128(ln_final_g)).then_inc(s_fin_g, 16)
            sp.wait_ge(s_tail_r, 2)
            for q, out in enumerate((new_conv_prompt, new_conv_sample)):
                sp.dma_start(out[0, 0].rearrange("i (f p) -> (i f) p", p=P), conv_rows[:, q, :]).then_inc(s_out, 16)
            for n in range(NT):
                sp.wait_ge(s_y, n + 1)
                dst = y_prompt[0, n * P:(n + 1) * P, :] if n < NT - 1 else y_sample[0]
                sp.dma_start(dst, y_sb[0:rows_of(n), n % 2, :]).then_inc(s_y_out[n % 2], 16)
            sp.wait_ge(s_out, 32)
            sp.wait_ge(s_y_out[0], 16 * 5)
            sp.wait_ge(s_y_out[1], 16 * 4)
            sp.wait_ge(s_vnout, 16)
            sp.wait_ge(s_kv_out, 64)
            sp.wait_ge(s_spill, 16 * KT)

        @block.gpsimd
        def _(pool):
            pool.memset(ident[:], 0.0).then_inc(s_zero, 1)
            pool.memset(half_neg[:], -0.5).then_inc(s_zero, 1)
            pool.memset(mean_mat[:], 1.0 / D).then_inc(s_zero, 1)
            for i in range(HEADS):
                last = pool.memset(slopes[:, i:i + 1], -2.0 ** (-8.0 * (i + 1) / HEADS))
            last.then_inc(s_zero, 1)
            pool.wait_ge(s_zero, 4)
            pool.affine_select(out=ident[:], in_=ident[:], compare_op=ALU.not_equal, fill=1.0, base=0,
                               pattern=[[-1, P]], channel_multiplier=1).then_inc(s_ident, 1)

            def rstd(n, table, s_in, s_mid, s_end, done):
                r = rows_of(n)
                pool.wait_ge(s_in, n + 1)
                pool.tensor_scalar(table[0:r, 1, n:n + 1], table[0:r, 0, n:n + 1], 1.0 / D, EPS, ALU.mult,
                                   ALU.add).then_inc(s_mid, 1)
                pool.wait_ge(s_mid, n + 1)
                pool.tensor_tensor(table[0:r, 2, n:n + 1], table[0:r, 1, n:n + 1], half_neg[0:r, :],
                                   ALU.pow).then_inc(s_end, 1)

            for n in range(NT):
                rstd(n, stat, s_sq, s_var, s_rstd, n)

            for n in range(NT):
                r = rows_of(n)
                pool.wait_ge(s_ln_mv, n + 1)
                pool.tensor_scalar(ln_rstd[0:r, n:n + 1], ln_mv[0:r, n, 1:2], 1.0, EPS, ALU.mult,
                                   ALU.add).then_inc(s_ln_v, 1)
                pool.wait_ge(s_ln_v, n + 1)
                pool.tensor_tensor(ln_rstd[0:r, n:n + 1], ln_rstd[0:r, n:n + 1], half_neg[0:r, :],
                                   ALU.pow).then_inc(s_ln_r, 1)
            for n in range(NT):
                r = rows_of(n)
                pool.wait_ge(s_vn_hi, n + 1)
                pool.tensor_tensor(vn_lo[0:r, n % 2, :], gs[0:r, n, :], vn_hi[0:r, n % 2, :].bitcast(F32),
                                   ALU.subtract).then_inc(s_vn_lo, 1)
            pool.wait_ge(s_s, NT)
            pool.memset(acc[:], 0.0).then_inc(s_zero, 1)

            with pool.Fori(0, KT) as i:
                pool.wait_ge(s_m1, i + 3)
                pool.dma_start(m1_spill[bass.ds(i, 1)].rearrange("a p t -> (a p) t"),
                               acc[:, bass.ds(i, 1), :].rearrange("p a t -> p (a t)")).then_inc(s_spill, 16)
            pool.wait_ge(s_spill, 16 * KT)
            pool.dma_start(wraw[:], w_in_v[:, :, K0:K0 + 256]).then_inc(s_kv_w, 16)
            pool.dma_start(k_tok[:, 2, :], cache_k[0, 0].rearrange("t h d -> t (h d)")).then_inc(s_cache, 16)
            pool.dma_start(v_tok[:, NT - 1, :], cache_v[0, 0].rearrange("t h d -> t (h d)")).then_inc(s_cache, 16)
            pool.wait_ge(s_wide, 5)
            pool.dma_start(wraw[:], w_in_v[:, :, K0 + 256:K0 + 512]).then_inc(s_kv_w, 16)

            pool.wait_ge(s_grp, 4)
            pool.wait_ge(s_prod, 2 * 4)
            pool.iota(dist[:].bitcast(mybir.dt.int32), [[-1, 256]], base=P, channel_multiplier=1).then_inc(s_dist, 1)
            pool.wait_ge(s_distf, 2)
            pool.affine_select(out=dist[0:64, :], in_=dist[0:64, :], compare_op=ALU.is_ge, fill=FAR, base=191,
                               pattern=[[-1, 256]], channel_multiplier=0).then_inc(s_dist, 1)
            pool.affine_select(out=dist[64:P, :], in_=dist[64:P, :], compare_op=ALU.is_ge, fill=FAR, base=-64,
                               pattern=[[1, 256]], channel_multiplier=0).then_inc(s_dist, 1)
            pool.wait_ge(s_dist, 3)
            pool.wait_ge(s_vt, 6 * NT)
            pool.memset(acc[:], 0.0).then_inc(s_zero, 1)
            pool.wait_ge(s_kt, NT + 1)
            pool.wait_ge(s_vt_free, 6 * NT + 3)
            pool.wait_ge(s_cache, 32)
            with pool.Fori(0, 2) as pair:
                pool.wait_ge(s_tile, pair * 20 + ATT_TILE)
                pool.tensor_copy(k_now[:], k_t[:, bass.ds(pair, 1), :].rearrange("p a c -> p (a c)")).then_inc(s_now, 1)
                pool.tensor_copy(v_now[:, 0:NT, :], v_tok[:, 0:NT, bass.ds(pair * P, P)]).then_inc(s_now, 1)
                pool.tensor_copy(v_now[0:DEC, NT, :], v_tok[0:DEC, NT, bass.ds(pair * P, P)]).then_inc(s_now, 1)

            pool.wait_ge(s_h2, KT)
            pool.memset(a_ext[:, :, 0:2], 0.0).then_inc(s_zext, 1)

            def keep_tail(f, k):
                src = a_ext[:, k, :]
                at = bass.ds(f, 1)
                pool.tensor_copy(conv_out[:, 0, :, at], src[:, SEQ:SEQ + 2].unsqueeze(2))
                pool.tensor_copy(conv_out[:, 1, :, at], src[:, EXT - 2:EXT].unsqueeze(2)).then_inc(s_tail, 1)

            for k in range(2):
                pool.wait_ge(s_c0, k + 1)
                keep_tail(k, k)
            with pool.Fori(0, FFN[2]) as i:
                for k in range(2):
                    pool.wait_ge(s_c0, i * 2 + (k + 3))
                    keep_tail(i * 2 + (k + 2), k)
            for n in range(NT):
                rstd(n, stat_y, s_ysq, s_yv, s_yr, n)

        @block.scalar
        def _(act):
            copy = ACT.Copy
            act.sem_inc(s_freed["freed", "act", 0], 1)
            act.sem_inc(s_freed["freed", "act", 1], 1)
            act.sem_inc(s_vt_free, 3)

            def h_hi_part(n):
                r = rows_of(n)
                act.wait_ge(s_xnt, n + 1)
                for b in range(2):
                    last = act.activation(h_hi[:, 4 * b:4 * b + 4, n * P:n * P + r],
                                          pset[n % 2][:, b, :].rearrange("p (k t) -> p k t", k=4)[:, :, 0:r], copy)
                last.then_inc(s_h_hi, 1)

            for n in range(NT):
                r = rows_of(n)
                act.wait_ge(s_x_in[n % 2], 16 * (n // 2 + 1))
                if n >= 1:
                    act.wait_ge(s_sq, n)
                act.activation(junk[0:r, :], xt[0:r, n % 2, :], ACT.Square,
                               accum_out=stat[0:r, 0, n:n + 1]).then_inc(s_sq, 1)
                if n >= 1:
                    h_hi_part(n - 1)
            h_hi_part(NT - 1)
            act.wait_ge(s_tab_t, 1)
            act.activation(conv_w[:].rearrange("p i f -> p (i f)"), pex[:, 0, 0:5 * FT], copy)
            act.activation(ffn_c[:], pex[:, 0, P:P + FT + KT], copy).then_inc(s_tab, 1)
            for b in range(2):
                act.wait_ge(s_tab_t, 2 + b)
                act.activation(ws_hi[:, 4 * b:4 * b + 4, :],
                               pex[:, 1 - b, :].rearrange("p (k t) -> p k t", k=4), copy).then_inc(s_ws_hi, 1)

            def wide_hi_part(w, slot, arrived=s_wide_in, before=0):
                act.wait_ge(arrived, (w - before) * 16 + 16)
                act.activation(wide_hi[:, slot], wraw[:], copy).then_inc(s_wide_hi, 1)

            with act.Fori(0, 2) as i:
                for k in range(2):
                    wide_hi_part(i * 2 + k, k)
                for k in range(2):
                    for n in range(NT):
                        r = rows_of(n)
                        act.wait_ge(s_vt, i * 18 + (9 * k + n + 1))
                        act.activation(gs[0:r, n, bass.ds(i * 512 + 256 * k, 256)], pset[0][0:r, n % 3, 0:256],
                                       ACT.Gelu_apprx_tanh).then_inc(s_vt_free, 1)

            c = Count()

            def split_hi(ahead=1):
                s = (c.slot() + ahead) % 2
                act.wait_ge(s_load[s], c.get("block", 2) * 32 + ((c.slot() + ahead) // 2 * 32 + 32))
                if c.v.get("tile", 0):
                    act.wait_ge(s_tile, c.get("tile"))
                act.activation(w_hi[:, s, :], raw[:, s, :], copy).then_inc(s_w_hi, 1)

            def group_hi(g):
                act.wait_ge(s_prod, g * 2 + 2)
                act.wait_ge(s_tile, c.get("tile"))
                act.activation(grp_hi[:], grp[:], copy).then_inc(s_grp_hi, 1)

            def evacuate(dst, func, **kw):
                act.wait_ge(s_tile, c.get("tile") + 1)
                s = c.slot("tile")
                for d, q in zip(halves(dst), pieces(s)):
                    last = act.activation(d, q, func, **kw)
                last.then_inc(s_freed["freed", "act", s], 1)

            def mix(project, between=None, after=None):
                pro, body, reps, epi = MIX
                for k in range(2):
                    split_hi()
                    project(k)
                    c.block(pro[k])
                if between:
                    between()
                with c.loop(act, reps, body, g=1):
                    for k in range(2):
                        split_hi()
                        if k == 0:
                            group_hi(c.get("g"))
                            act.wait_ge(s_grp, c.get("g") + 1)
                        project(k)
                        c.block("act")
                        split_hi()
                        c.block("group")
                    c.add("g")
                split_hi()
                group_hi(c.get("g"))
                if after:
                    after(0)
                c.block("group")
                c.add("g")
                split_hi()
                if after:
                    after(1)
                c.block("group")

            def values_hi():
                for n in range(NT):
                    r = rows_of(n)
                    act.wait_ge(s_vn, n + 1)
                    if n >= 2:
                        act.wait_ge(s_mixed, n - 1)
                    act.activation(vn_hi[0:r, n % 2, :], gs[0:r, n, :], copy).then_inc(s_vn_hi, 1)
                    if n == NT - 1:
                        act.dma_start(new_gmlp_v_sample[0, 0], gs[0:DEC, n, :]).then_inc(s_vnout, 16)

            split_hi(0)
            mix(lambda k: evacuate(grp[:, k, :], ACT.Gelu_apprx_tanh), between=values_hi)

            with c.loop(act, GATE[2], GATE[1], m=2):
                for k in range(2):
                    split_hi()
                    act.wait_ge(s_m1, c.get("m") + 1)
                    evacuate(gate[:, k, :], ACT.Sigmoid)
                    c.block("act")
                    c.add("m")

            for w in range(4, 6):
                wide_hi_part(w, w % 2, s_kv_w, 4)
            for n in range(NT):
                r = rows_of(n)
                act.wait_ge(s_vt, 4 * NT + n + 1)
                if n >= 2:
                    act.wait_ge(s_ktr, n - 1)
                act.activation(k_tok[0:r, n % 2, :], pset[0][0:r, n % 3, 0:256], copy).then_inc(s_vt_free, 1)
            for n in range(NT):
                r, slot = rows_of(n), n if n < NT - 1 else NT
                act.wait_ge(s_vt, 5 * NT + n + 1)
                act.activation(v_tok[0:r, slot, :], pset[0][0:r, n % 3, 0:256], copy).then_inc(s_vt_free, 1)
            act.wait_ge(s_vt_free, 6 * NT + 3)
            for dst, src in ((new_k_prompt, k_tok[:, (NT - 2) % 2, :]), (new_k_sample, k_tok[0:DEC, (NT - 1) % 2, :]),
                             (new_v_prompt, v_tok[:, NT - 2, :]), (new_v_sample, v_tok[0:DEC, NT, :])):
                act.dma_start(dst[0, 0].rearrange("t h d -> t (h d)"), src).then_inc(s_kv_out, 16)

            with c.loop(act, ATT[2], ATT[1], att=NT):
                for k in range(2):
                    split_hi()
                    evacuate(grp[:, k, :], copy, scale=HD ** -0.5)
                    c.block("act")
                for step in range(NT + 3):
                    if step < NT:
                        n, a = step, att_stat[:, step % 2]
                        w = keys_of(n)[1]
                        act.wait_ge(s_neg, c.get("att") + n + 1)
                        for e in range(4):
                            act.activation(sc_sb[:, n % 3, e, 0:w], sc_sb[:, n % 3, e, 0:w], ACT.Exp,
                                           bias=a[:, 1, e:e + 1], accum_out=a[:, 3, e:e + 1])
                        act.activation(a[:, 4, :], a[:, 2, :], ACT.Exp).then_inc(s_exp, 1)
                    if step >= 3:
                        n, r, q0 = step - 3, rows_of(step - 3), queries_of(step - 3)[1]
                        act.wait_ge(s_o, c.get("att") + n + 1)
                        act.activation(grp_hi[:, :, n * P:n * P + r],
                                       pset[n % 2][:, 2, 0:256].rearrange("p (k q) -> p k q", k=2)[:, :, q0:P],
                                       copy).then_inc(s_b_hi, 1)
                    if 2 <= step <= NT + 1:
                        n = step - 2
                        act.wait_ge(s_ptr, c.get("att") + n + 1)
                        for j, (_, rows) in enumerate(key_tiles(n)):
                            last = act.activation(pt_sb[0:rows, j, :, :],
                                                  pset[0][0:rows, j, :].rearrange("p (e q) -> p e q", e=4)[:, :, :], copy)
                        last.then_inc(s_pt, 1)
                c.add("att", NT)
                for b in range(2):
                    split_hi()
                    c.block("group")

            for n in range(NT):
                r = rows_of(n)
                act.wait_ge(s_x2t, n + 1)
                for b in range(2):
                    last = act.activation(xres[:, 4 * b:4 * b + 4, n * P:n * P + r],
                                          pset[n % 2][:, b, :].rearrange("p (k t) -> p k t", k=4)[:, :, 0:r], copy)
                last.then_inc(s_x2, 1)

            def squares(b):
                for q in range(4):
                    kt, key = 4 * b + q, ("freed", "dve", q % 2)
                    act.wait_ge(s_freed[key], c.get(key) + q // 2 + 2)
                    act.activation(sq[:, kt, :], xres[:, kt, :], ACT.Square).then_inc(s_sq2, 1)

            mix(lambda k: evacuate(grp[:, k, :], ACT.Sigmoid), after=squares)

            act.wait_ge(s_r0, 1)
            act.activation(rb[:], rb[:], ACT.Sqrt).then_inc(s_r1, 1)
            for kt in range(KT):
                act.wait_ge(s_hn, kt + 1)
                act.activation(h2_hi[:, kt, :], hn[:, kt % 2, :], copy).then_inc(s_hn_hi, 1)

            def up_gate(k, first):
                f, key = c.get("f"), ("freed", "act", c.slot("tile"))
                if not first:
                    act.wait_ge(s_conv, f - 1)
                    act.wait_ge(s_tail, f - 1)
                at = bass.ds(f, 1)
                act.activation(a_ext[:, k, SEQ + 2:SEQ + 4], conv_w[:, 3:5, at].rearrange("p i f -> p (i f)"), copy)
                act.wait_ge(s_tile, c.get("tile") + 1)
                p0, p1 = pieces(key[2])
                act.activation(a_ext[:, k, 2:2 + 2 * NB].rearrange("p (b n) -> p b n", b=2), p0, copy)
                act.activation(a_ext[:, k, 2 + 2 * NB:2 + SEQ], p1[:, 0:SEQ - 2 * NB], copy)
                act.activation(a_ext[:, k, SAMP:EXT], p1[:, SEQ - 2 * NB:], copy).then_inc(s_freed[key], 1)
                act.wait_ge(s_freed[key], c.get(key) + 2)
                act.wait_ge(s_prod, f + (2 * FFN_GROUP - 1) if not first else 2 * FFN_GROUP)
                act.activation(conv[:, k, 2:EXT], a_ext[:, k, 2:EXT], ACT.Identity, bias=ffn_c[:, at],
                               scale=conv_w[:, 2, at]).then_inc(s_c0, 1)

            def up_value():
                f = c.get("f")
                act.wait_ge(s_conv, f + 1)
                k = c.slot("f")
                act.activation(conv[:, k, 2:EXT], conv[:, k, 2:EXT], ACT.Gelu_apprx_tanh).then_inc(s_gelu, 1)

            pro, body, reps, epi = FFN
            for k in range(2):
                split_hi()
                up_gate(k, True)
                c.block("act")
                split_hi()
                up_value()
                c.block("dve")
                c.add("f")
            with c.loop(act, reps, body, g=1, f=2):
                for k in range(2):
                    split_hi()
                    if k == 0:
                        group_hi(c.get("g"))
                    up_gate(k, False)
                    c.block("act")
                    split_hi()
                    up_value()
                    c.block("dve")
                    split_hi()
                    c.block("group")
                    c.add("f")
                c.add("g")
            split_hi()
            group_hi(c.get("g"))
            c.block("group")
            c.block("group")

            act.wait_ge(s_tail_t, 1)
            act.activation(conv_rows[:].rearrange("r q p -> r (q p)"), pex[0:2 * FT, 0, 0:2 * P], copy).then_inc(s_tail_r, 2)
            for n in range(NT):
                r = rows_of(n)
                act.wait_ge(s_yt, n + 1)
                if n >= 1:
                    act.wait_ge(s_ysq, n)
                act.activation(y_junk[0:r, :].rearrange("p (b c) -> p b c", b=2), pset[n % 2][0:r, 0:2, :], ACT.Square,
                               accum_out=stat_y[0:r, 0, n:n + 1]).then_inc(s_ysq, 1)

        @block.vector
        def _(dve):
            for key, n in ((s_freed["freed", "dve", 0], 1), (s_freed["freed", "dve", 1], 1), (s_m1, 2)):
                dve.sem_inc(key, n)

            def h_lo_part(n):
                r = rows_of(n)
                dve.wait_ge(s_h_hi, n + 1)
                for b in range(2):
                    at = (slice(None), slice(4 * b, 4 * b + 4), slice(n * P, n * P + r))
                    last = dve.tensor_tensor(h_lo[at], pset[n % 2][:, b, :].rearrange("p (k t) -> p k t", k=4)[:, :, 0:r],
                                             h_hi[at].bitcast(F32), ALU.subtract)
                last.then_inc(s_h, 1)

            dve.wait_ge(s_row_in, 16)
            for n in range(NT):
                r = rows_of(n)
                dve.wait_ge(s_rstd, n + 1)
                dve.wait_ge(s_x_in[n % 2], 16 * (n // 2 + 1))
                if n >= 2:
                    dve.wait_ge(s_xnt, n - 1)
                dve.scalar_tensor_tensor(xn[0:r, n % 2, :], xt[0:r, n % 2, :], stat[0:r, 2, n:n + 1], mix_g[0:r, :],
                                         ALU.mult, ALU.mult).then_inc(s_xn, 1)
                if n >= 1:
                    h_lo_part(n - 1)
            h_lo_part(NT - 1)
            for b in range(2):
                dve.wait_ge(s_ws_hi, b + 1)
                dve.tensor_tensor(ws_lo[:, 4 * b:4 * b + 4, :], pex[:, 1 - b, :].rearrange("p (k t) -> p k t", k=4),
                                  ws_hi[:, 4 * b:4 * b + 4, :].bitcast(F32), ALU.subtract).then_inc(s_ws, 1)
            dve.wait_ge(s_ws, 2)
            dve.memset(ws_hi[64:P, :, 0:64].bitcast(F32), 0.0)
            dve.memset(ws_lo[64:P, :, 0:64].bitcast(F32), 0.0).then_inc(s_ws, 1)

            def wide_lo_part(w, slot):
                dve.wait_ge(s_wide_hi, w + 1)
                dve.tensor_tensor(wide_lo[:, slot], wraw[:], wide_hi[:, slot].bitcast(F32), ALU.subtract).then_inc(s_wide, 1)

            with dve.Fori(0, 2) as i:
                for k in range(2):
                    wide_lo_part(i * 2 + k, k)

            c = Count()

            def split_lo(ahead=1):
                s = (c.slot() + ahead) % 2
                dve.wait_ge(s_w_hi, c.get("block") + (ahead + 1))
                dve.tensor_tensor(w_lo[:, s, :], raw[:, s, :], w_hi[:, s, :].bitcast(F32), ALU.subtract).then_inc(s_w, 1)

            def group_lo(g):
                dve.wait_ge(s_grp_hi, g + 1)
                dve.tensor_tensor(grp_lo[:], grp[:], grp_hi[:].bitcast(F32), ALU.subtract).then_inc(s_grp, 1)

            def add_group(dst, b):
                for q in range(4):
                    dve.wait_ge(s_tile, c.get("tile") + 1)
                    s = c.slot("tile")
                    for d, v in zip(halves(dst[:, 4 * b + q, :]), pieces(s)):
                        last = dve.tensor_tensor(d, v, d, ALU.add)
                    last.then_inc(s_freed["freed", "dve", s], 1)
                    c.tile("group")
                c.add("block")

            def evacuated(k):
                key = ("freed", "act", c.slot("tile"))
                dve.wait_ge(s_freed[key], c.get(key) + 2)

            def mix(project, dst, between=None):
                pro, body, reps, epi = MIX
                for k in range(2):
                    split_lo()
                    if not between:
                        project(k)
                    c.block(pro[k])
                    c.add("kt")
                if between:
                    between()
                with c.loop(dve, reps, body, g=1, kt=2):
                    for k in range(2):
                        split_lo()
                        if k == 0:
                            group_lo(c.get("g"))
                        project(k)
                        c.block("act")
                        c.add("kt")
                        split_lo()
                        add_group(dst, k)
                    c.add("g")
                split_lo()
                group_lo(c.get("g"))
                add_group(dst, 0)
                c.add("g")
                split_lo()
                add_group(dst, 1)

            def values():
                dve.wait_ge(s_row_in, 16 * 5)
                for n in range(NT):
                    r = rows_of(n)
                    dve.wait_ge(s_vt_free, 3 * NT + n + 1 + 3)
                    if n >= 1:
                        dve.wait_ge(s_ln_mv, n)
                    for b in range(2):
                        last = dve.bn_stats(ln_stats[0:r, 0, b, :], gs[0:r, n, 512 * b:512 * b + 512])
                    last.then_inc(s_ln, 1)
                    dve.wait_ge(s_ln, n + 1)
                    dve.bn_aggr(ln_mv[0:r, n, :], ln_stats[0:r, 0]).then_inc(s_ln_mv, 1)
                    dve.wait_ge(s_ln_mv, n + 1)
                    dve.scalar_tensor_tensor(gs[0:r, n, :], gs[0:r, n, :], ln_mv[0:r, n, 0:1], lnv_g[0:r, :],
                                             ALU.subtract, ALU.mult).then_inc(s_ln_a, 1)
                    dve.wait_ge(s_ln_a, n + 1)
                    dve.wait_ge(s_ln_r, n + 1)
                    dve.scalar_tensor_tensor(gs[0:r, n, :], gs[0:r, n, :], ln_rstd[0:r, n:n + 1], lnv_b[0:r, :],
                                             ALU.mult, ALU.add).then_inc(s_vn, 1)

            def mixed():
                for n in range(NT):
                    r = rows_of(n)
                    src = pex if n % 2 == 0 else pset[1]
                    dve.wait_ge(s_mixed, n + 1)
                    if n == NT - 1:
                        dve.wait_ge(s_vnout, 16)
                    for b in range(2):
                        last = dve.tensor_tensor(
                            gs[:, n, 512 * b:512 * b + 512].rearrange("p (g t) -> p g t", g=4)[:, :, 0:r],
                            src[:, b, :].rearrange("p (g t) -> p g t", g=4)[:, :, 0:r],
                            bs[:, 4 * b:4 * b + 4, 0:r], ALU.add)
                    last.then_inc(s_s, 1)
                dve.wait_ge(s_s, NT)
                for k in range(2):
                    product(k, k)
                dve.wait_ge(s_zero, 5)

            def product(k, kt):
                at = kt * P
                p = grp[:, k, 0:SEQ].rearrange("p (n t) -> p n t", t=P)
                dve.tensor_tensor(p, p, gs[:, 0:NT - 1, bass.ds(at, P)], ALU.mult)
                p = grp[:, k, SEQ:T]
                dve.tensor_tensor(p, p, gs[:, NT - 1, bass.ds(at, DEC)], ALU.mult).then_inc(s_prod, 1)

            def project_u(k):
                evacuated(k)
                product(k, c.get("kt"))

            values()
            split_lo(0)
            mix(project_u, acc, between=mixed)

            with c.loop(dve, GATE[2], GATE[1], m=2):
                for k in range(2):
                    split_lo()
                    evacuated(k)
                    a = acc[:, bass.ds(c.get("m"), 1), :].rearrange("p a t -> p (a t)")
                    dve.tensor_tensor(a, a, gate[:, k, :], ALU.mult).then_inc(s_m1, 1)
                    c.block("act")
                    c.add("m")

            for w in range(4, 6):
                wide_lo_part(w, w % 2)
            for n in range(NT + 1):
                r = (rows_of(n) if n < NT else CACHE)
                col = n * P if n < NT - 1 else (SEQ + CACHE if n == NT - 1 else SEQ)
                dve.wait_ge(s_ktr, n + 1)
                dve.tensor_copy(k_t[:, :, col:col + r],
                                pex[:, n % 2, 0:256].rearrange("p (k t) -> p k t", k=2)[:, :, 0:r]).then_inc(s_kt, 1)
            dve.wait_ge(s_dist, 1)
            dve.tensor_copy(bias_now[:, 0, :], dist[:].bitcast(mybir.dt.int32)).then_inc(s_distf, 1)
            dve.wait_ge(s_distf, 1)
            dve.scalar_tensor_tensor(dist[:], bias_now[:, 0, :], -1.0, bias_now[:, 0, :], ALU.mult,
                                     ALU.max).then_inc(s_distf, 1)

            dve.wait_ge(s_dist, 3)
            dve.wait_ge(s_zero, 6)
            dve.wait_ge(s_kv_out, 64)
            with c.loop(dve, ATT[2], ATT[1], att=NT, den=2 * NT) as (pair, half):
                for k in range(2):
                    split_lo()
                    c.block("act")
                for e in range(4):
                    at = bass.ds(pair * 8 + half * 2 + (4 * (e // 2) + e % 2), 1)
                    dve.tensor_scalar(bias_now[:, e, :], dist[:], slopes[:, at], None, ALU.mult)
                    last = dve.tensor_copy(sink_now[:, e:e + 1], sinks[:, at])
                last.then_inc(s_bias, 1)
                dve.wait_ge(s_bias, c.i + 1)
                for step in range(NT + 4):
                    if step < NT:
                        n, a = step, att_stat[:, step % 2]
                        w, b0 = keys_of(n)[1], keys_of(n)[2]
                        src = pex if n % 2 == 0 else pset[1]
                        if n >= 3:
                            dve.wait_ge(s_ptr, c.get("att") + (n - 2))
                        dve.wait_ge(s_sc, c.get("att") + n + 1)
                        dve.tensor_copy(spare[:, 3:4], sink_now[:, 0:1])
                        for e in range(4):
                            last = dve.tensor_tensor_reduce(
                                sc_sb[:, n % 3, e, 0:w], src[:, e // 2, 256 * (e % 2):256 * (e % 2) + w],
                                bias_now[:, e, b0:b0 + w], 1.0, sink_now[:, e:e + 1], ALU.add, ALU.max,
                                a[:, 0, e:e + 1])
                        last.then_inc(s_smax, 1)
                        dve.wait_ge(s_smax, c.get("att") + n + 1)
                        dve.tensor_scalar(a[:, 1, :], a[:, 0, :], -1.0, None, ALU.mult)
                        dve.tensor_tensor(a[:, 2, :], sink_now[:, :], a[:, 0, :], ALU.subtract).then_inc(s_neg, 1)
                    if 1 <= step <= NT:
                        n, a = step - 1, att_stat[:, (step - 1) % 2]
                        w = keys_of(n)[1]
                        dve.wait_ge(s_exp, c.get("att") + n + 1)
                        dve.tensor_tensor(a[:, 5, :], a[:, 3, :], a[:, 4, :], ALU.add).then_inc(s_den, 1)
                        dve.wait_ge(s_den, c.get("den") + 1)
                        dve.reciprocal(a[:, 6, :], a[:, 5, :]).then_inc(s_den, 1)
                        dve.wait_ge(s_den, c.get("den") + 2)
                        c.add("den", 2)
                        for e in range(4):
                            p = sc_sb[:, n % 3, e, 0:w]
                            last = dve.tensor_scalar(p, p, a[:, 6, e:e + 1], None, ALU.mult)
                        last.then_inc(s_p, 1)
                    if step >= 4:
                        n, r, q0 = step - 4, rows_of(step - 4), queries_of(step - 4)[1]
                        dve.wait_ge(s_b_hi, c.get("att") + n + 1)
                        at = (slice(None), slice(None), slice(n * P, n * P + r))
                        dve.tensor_tensor(grp_lo[at], pset[n % 2][:, 2, 0:256].rearrange("p (k q) -> p k q", k=2)[:, :, q0:P],
                                          grp_hi[at].bitcast(F32), ALU.subtract).then_inc(s_b, 1)
                c.add("att", NT)
                for b in range(2):
                    split_lo()
                    add_group(acc, b)

            c.v["kt"] = 0

            def merge(k):
                evacuated(k)
                a = acc[:, bass.ds(c.get("kt"), 1), :].rearrange("p a t -> p (a t)")
                dve.tensor_tensor(grp[:, k, :], grp[:, k, :], a, ALU.mult).then_inc(s_gb, 1)
                dve.wait_ge(s_gb, c.get("kt") + 1)
                dve.wait_ge(s_m1_in[k], c.get("kt", 2) * 16 + 16)
                dve.tensor_tensor(grp[:, k, :], grp[:, k, :], m1[:, k, :], ALU.add).then_inc(s_prod, 1)

            mix(merge, xres)

            dve.wait_ge(s_ms, KT)
            for d, v in zip(halves(rb[:]), pieces(0)):
                last = dve.tensor_scalar(d, v, 1.0, EPS, ALU.mult, ALU.add)
            last.then_inc(s_r0, 1)
            dve.wait_ge(s_r1, 1)
            dve.reciprocal(rb[:], rb[:]).then_inc(s_r2, 1)
            dve.wait_ge(s_r2, 1)

            def h2_lo_part(kt):
                dve.wait_ge(s_hn_hi, kt + 1)
                dve.tensor_tensor(h2_lo[:, kt, :], hn[:, kt % 2, :], h2_hi[:, kt, :].bitcast(F32),
                                  ALU.subtract).then_inc(s_h2, 1)

            for kt in range(KT):
                if kt >= 2:
                    dve.wait_ge(s_h2, kt - 1)
                dve.scalar_tensor_tensor(hn[:, kt % 2, :], xres[:, kt, :], ffn_c[:, FT + kt:FT + kt + 1], rb[:],
                                         ALU.mult, ALU.mult).then_inc(s_hn, 1)
                if kt >= 1:
                    h2_lo_part(kt - 1)
            h2_lo_part(KT - 1)

            def up_gate(k):
                f = c.get("f")
                at = bass.ds(f, 1)
                dve.wait_ge(s_c0, f + 1)
                cv = conv[:, k, 2:EXT]
                dve.scalar_tensor_tensor(cv, a_ext[:, k, 1:EXT - 1], conv_w[:, 1, at], cv, ALU.mult, ALU.add).then_inc(s_c1, 1)
                dve.wait_ge(s_c1, f + 1)
                dve.scalar_tensor_tensor(cv, a_ext[:, k, 0:EXT - 2], conv_w[:, 0, at], cv, ALU.mult, ALU.add).then_inc(s_conv, 1)

            def up_value(k):
                f, s = c.get("f"), c.slot("tile")
                dve.wait_ge(s_gelu, f + 1)
                dve.wait_ge(s_tile, c.get("tile") + 1)
                p0, p1 = pieces(s)
                g = grp[:, k, :]
                dve.tensor_tensor(g[:, 0:2 * NB].rearrange("p (b n) -> p b n", b=2), p0,
                                  conv[:, k, 2:2 + 2 * NB].rearrange("p (b n) -> p b n", b=2), ALU.mult)
                dve.tensor_tensor(g[:, 2 * NB:SEQ], p1[:, 0:SEQ - 2 * NB], conv[:, k, 2 + 2 * NB:2 + SEQ], ALU.mult)
                dve.tensor_tensor(g[:, SEQ:T], p1[:, SEQ - 2 * NB:], conv[:, k, SAMP:EXT],
                                  ALU.mult).then_inc(s_freed["freed", "dve", s], 1)
                dve.tensor_copy(spare[:, 3:4], half_neg[:]).then_inc(s_prod, 1)

            dve.wait_ge(s_zext, 1)
            pro, body, reps, epi = FFN
            for k in range(2):
                split_lo()
                up_gate(k)
                c.block("act")
                split_lo()
                up_value(k)
                c.block("dve")
                c.add("f")
            with c.loop(dve, reps, body, g=1, f=2):
                for k in range(2):
                    split_lo()
                    if k == 0:
                        group_lo(c.get("g"))
                    up_gate(k)
                    c.block("act")
                    split_lo()
                    up_value(k)
                    c.block("dve")
                    split_lo()
                    add_group(xres, k)
                    c.add("f")
                c.add("g")
            split_lo()
            group_lo(c.get("g"))
            add_group(xres, 0)
            add_group(xres, 1)

            dve.wait_ge(s_fin_g, 16)
            for n in range(NT):
                r = rows_of(n)
                dve.wait_ge(s_yr, n + 1)
                if n >= 2:
                    dve.wait_ge(s_y_out[n % 2], 16 * (n // 2))
                dve.scalar_tensor_tensor(y_sb[0:r, n % 2, :].rearrange("p (b c) -> p b c", b=2), pset[n % 2][0:r, 0:2, :],
                                         stat_y[0:r, 2, n:n + 1], fin_g[0:r, :].rearrange("p (b c) -> p b c", b=2),
                                         ALU.mult, ALU.mult).then_inc(s_y, 1)

        @block.tensor
        def _(pe):
            pe.wait_ge(s_ident, 1)
            for n in range(NT):
                r = rows_of(n)
                pe.wait_ge(s_xn, n + 1)
                if n >= 2:
                    pe.wait_ge(s_h, n - 1)
                for kt in range(KT):
                    last = pe.transpose(pset[n % 2][:, kt // 4, kt % 4 * P:kt % 4 * P + r],
                                        xn[0:r, n % 2, kt * P:kt * P + P], ident[0:r, 0:r])
                last.then_inc(s_xnt, 1)
            pe.wait_ge(s_tab_in, 16 * 5)
            pe.transpose(pex[:, 0, 0:5 * FT], tab_rows[0:5 * FT, 0, :], ident[0:5 * FT, 0:5 * FT])
            pe.transpose(pex[:, 0, P:P + FT + KT], tab_rows[0:FT + KT, 1, :], ident[0:FT + KT, 0:FT + KT]).then_inc(s_tab_t, 1)
            for b in range(2):
                if b == 1:
                    pe.wait_ge(s_tab, 1)
                for g in range(4):
                    last = pe.transpose(pex[:, 1 - b, g * P:g * P + P], ws_raw[:, 4 * b + g, :], ident[:])
                last.then_inc(s_tab_t, 1)

            def products(out, lhs, rhs, first=True, last=True):
                for n, (a, b) in enumerate(((0, 0), (0, 1), (1, 0))):
                    mm = pe.matmul(out, lhs[a], rhs[b], start=first and n == 0, stop=last and n == 2)
                return mm

            def wide_tiles(q0, slot, after=None):
                for n in range(NT):
                    r = rows_of(n)
                    pe.wait_ge(s_vt_free, q0 + (n + 1))
                    for kt in range(KT):
                        last = products(pset[0][0:r, n % 3, 0:256],
                                        [h[:, kt, n * P:n * P + r] for h in (h_hi, h_lo)],
                                        [v[:, slot, kt, :] for v in (wide_hi, wide_lo)], kt == 0, kt == KT - 1)
                    last.then_inc(s_vt, 1)
                    if after and n:
                        after(n - 1)

            pe.wait_ge(s_h, NT)
            with pe.Fori(0, 2) as i:
                for k in range(2):
                    pe.wait_ge(s_wide, i * 2 + (k + 1))
                    wide_tiles(i * 18 + 9 * k, k)

            c = Count()
            TB = [(b, b * NB, min(T, b * NB + NB)) for b in range(3)]
            PASSES = ((0, 0), (0, 1), (1, 0))
            w_pair = (w_hi, w_lo)

            def set_free():
                s = c.slot("tile")
                for e in ("act", "dve"):
                    key = ("freed", e, s)
                    pe.wait_ge(s_freed[key], c.get(key) + 1)
                return s

            def project(kind, x_pair, ready=None):
                pe.wait_ge(s_w, c.get("block") + 1)
                ws, s = c.slot(), set_free()
                for kt in range(KT):
                    if ready is not None:
                        pe.wait_ge(ready, kt + 1)
                    for n, (a, b) in enumerate(PASSES):
                        for blk, t0, t1 in TB:
                            last = pe.matmul(pset[s][:, blk, 0:t1 - t0], w_pair[a][:, ws, kt * P:kt * P + P],
                                             x_pair[b][:, kt, t0:t1], start=kt == 0 and n == 0,
                                             stop=kt == KT - 1 and n == 2)
                last.then_inc(s_tile, 1)
                c.block(kind)

            def group(ready, value):
                pe.wait_ge(s_w, c.get("block") + 1)
                pe.wait_ge(ready, value)
                ws = c.slot()
                for q in range(4):
                    s = set_free()
                    for k in range(2):
                        for n, (a, b) in enumerate(PASSES):
                            for blk, t0, t1 in TB:
                                last = pe.matmul(pset[s][:, blk, 0:t1 - t0],
                                                 w_pair[a][:, ws, 512 * k + P * q:512 * k + P * q + P],
                                                 (grp_hi, grp_lo)[b][:, k, t0:t1], start=k == 0 and n == 0,
                                                 stop=k == 1 and n == 2)
                    last.then_inc(s_tile, 1)
                    c.tile("group")
                c.add("block")

            def mix(between=None):
                pro, body, reps, epi = MIX
                for k in range(2):
                    project(pro[k], (h_hi, h_lo))
                if between:
                    between()
                with c.loop(pe, reps, body, g=1):
                    for k in range(2):
                        project("act", (h_hi, h_lo))
                        group(s_grp, c.get("g") + 1)
                    c.add("g")
                for b in range(2):
                    group(s_grp, c.get("g") + 1)
                c.add("g")

            def spatial():
                pe.wait_ge(s_ws, 3)
                key = ("freed", "act", 1)
                pe.wait_ge(s_freed[key], c.get(key) + 1)
                for n in range(NT):
                    r = rows_of(n)
                    dst = pex if n % 2 == 0 else pset[1]
                    pe.wait_ge(s_vn_lo, n + 1)
                    if n >= 2:
                        pe.wait_ge(s_s, n - 1)
                    for g in range(KT):
                        last = products(dst[:, g // 4, g % 4 * P:g % 4 * P + r],
                                        [v[0:r, n % 2, g * P:g * P + P] for v in (vn_hi, vn_lo)],
                                        [v[0:r, g, 0:r] for v in (ws_hi, ws_lo)])
                    last.then_inc(s_mixed, 1)
                pe.wait_ge(s_s, NT)

            mix(between=spatial)
            with c.loop(pe, GATE[2], GATE[1]):
                for k in range(2):
                    project("act", (h_hi, h_lo))

            for s in range(2):
                key = ("freed", "act", s)
                pe.wait_ge(s_freed[key], c.get(key) + 1)
            def transpose_k(n):
                r = rows_of(n) if n < NT else CACHE
                if n < NT:
                    pe.wait_ge(s_vt_free, 4 * NT + n + 1 + 3)
                else:
                    pe.wait_ge(s_cache, 32)
                if n >= 2:
                    pe.wait_ge(s_kt, n - 1)
                for p in range(2):
                    last = pe.transpose(pex[:, n % 2, p * P:p * P + r],
                                        k_tok[0:r, n % 2 if n < NT else 2, p * P:p * P + P], ident[0:r, 0:r])
                last.then_inc(s_ktr, 1)

            pe.wait_ge(s_wide, 5)
            wide_tiles(4 * NT, 0, transpose_k)
            transpose_k(NT - 1)
            transpose_k(NT)
            pe.wait_ge(s_wide, 6)
            wide_tiles(5 * NT, 1)
            pe.wait_ge(s_vt_free, 6 * NT + 3)
            pe.wait_ge(s_kt, NT + 1)

            with c.loop(pe, ATT[2], ATT[1], att=NT) as (pair, half):
                for k in range(2):
                    project("act", (h_hi, h_lo))
                for s in range(2):
                    key = ("freed", "act", s)
                    pe.wait_ge(s_freed[key], c.get(key) + 1)
                pe.wait_ge(s_now, pair * 3 + 3)
                for step in range(NT + 3):
                    if step < NT:
                        n, q0 = step, queries_of(step)[0]
                        k0, w, _ = keys_of(n)
                        dst = pex if n % 2 == 0 else pset[1]
                        if n >= 2:
                            pe.wait_ge(s_smax, c.get("att") + (n - 1))
                        for e in range(4):
                            h, k = e // 2, e % 2
                            last = pe.matmul(dst[:, h, 256 * k:256 * k + w],
                                             grp[64 * h:64 * h + 64, k, q0:q0 + P],
                                             k_now[64 * h:64 * h + 64, k0:k0 + w], start=True, stop=True)
                        last.then_inc(s_sc, 1)
                    if step >= 3:
                        n = step - 3
                        pe.wait_ge(s_pt, c.get("att") + n + 1)
                        if n >= 2:
                            pe.wait_ge(s_b, c.get("att") + (n - 1))
                        tiles = key_tiles(n)
                        for h in range(2):
                            for j, (slot, rows) in enumerate(tiles):
                                last = pe.matmul(
                                    pset[n % 2][64 * h:64 * h + 64, 2, 0:256].rearrange("p (k q) -> p k q", k=2)[:, :, :],
                                    v_now[0:rows, slot, 64 * h:64 * h + 64],
                                    pt_sb[0:rows, j, 2 * h:2 * h + 2, :],
                                    start=j == 0, stop=j == len(tiles) - 1)
                        last.then_inc(s_o, 1)
                    if 2 <= step <= NT + 1:
                        n = step - 2
                        pe.wait_ge(s_p, c.get("att") + n + 1)
                        for j, (_, rows) in enumerate(key_tiles(n)):
                            for e in range(4):
                                last = pe.transpose(pset[0][0:rows, j, e * P:e * P + P],
                                                    sc_sb[:, n % 3, e, j * P:j * P + rows], ident[:])
                        last.then_inc(s_ptr, 1)
                c.add("att", NT)
                for b in range(2):
                    group(s_b, c.get("att"))

            for s in range(2):
                key = ("freed", "dve", s)
                pe.wait_ge(s_freed[key], c.get(key) + 1)
            for n in range(NT):
                r = rows_of(n)
                pe.wait_ge(s_x2_in[n % 2], 16 * (n // 2 + 1))
                if n >= 2:
                    pe.wait_ge(s_x2, n - 1)
                for kt in range(KT):
                    last = pe.transpose(pset[n % 2][:, kt // 4, kt % 4 * P:kt % 4 * P + r],
                                        xt2[0:r, n % 2, kt * P:kt * P + P], ident[0:r, 0:r])
                last.then_inc(s_x2t, 1)
            pe.wait_ge(s_x2, NT)
            mix()

            key = ("freed", "dve", 0)
            pe.wait_ge(s_freed[key], c.get(key) + 1)
            for kt in range(KT):
                pe.wait_ge(s_sq2, kt + 1)
                for blk, t0, t1 in TB:
                    last = pe.matmul(pset[0][:, blk, 0:t1 - t0], mean_mat[:], sq[:, kt, t0:t1],
                                     start=kt == 0, stop=kt == KT - 1)
                last.then_inc(s_ms, 1)

            pro, body, reps, epi = FFN
            for n, kind in enumerate(pro):
                project(kind, (h2_hi, h2_lo), s_h2 if n == 0 else None)
            with c.loop(pe, reps, body, g=1):
                for kind in body:
                    if kind == "group":
                        group(s_grp, c.get("g") + 1)
                    else:
                        project(kind, (h2_hi, h2_lo))
                c.add("g")
            for b in range(2):
                group(s_grp, c.get("g") + 1)

            pe.wait_ge(s_tail, FT)
            for q in range(2):
                last = pe.transpose(pex[0:2 * FT, 0, q * P:q * P + P], conv_out[:, q].rearrange("p i f -> p (i f)"), ident[:])
            last.then_inc(s_tail_t, 1)
            for s in range(2):
                key = ("freed", "dve", s)
                pe.wait_ge(s_freed[key], c.get(key) + 1)
            for n in range(NT):
                r = rows_of(n)
                if n >= 2:
                    pe.wait_ge(s_y, n - 1)
                for kt in range(KT):
                    last = pe.transpose(pset[n % 2][0:r, kt // 4, kt % 4 * P:kt % 4 * P + P],
                                        xres[:, kt, n * P:n * P + r], ident[:])
                last.then_inc(s_yt, 1)


_INS = ["x_prompt", "x_sample", "cache_k", "cache_v", "cache_conv", "ln_mix_g", "w_in", "ln_v_g", "ln_v_b", "w_s",
        "b_s", "attn_sinks", "w_pa", "w_pb", "w_o", "ln_ffn_g", "w_up", "w_conv", "b_conv", "w_down", "ln_final_g"]
_OUTS = [(1, SEQ, D), (1, DEC, D), (1, 1, 128, KVH, HD), (1, 1, 128, KVH, HD), (1, 1, 2, FF),
         (1, 1, DEC, KVH, HD), (1, 1, DEC, KVH, HD), (1, 1, 2, FF), (1, 1, DEC, D)]


def kernel(**inputs):
    import numpy as _np
    import concourse.bacc as _bacc
    from concourse import mybir as _mybir
    from concourse.bass_utils import run_bass_kernel_spmd as _run

    nc = _bacc.Bacc("TRN2", target_bir_lowering=False, num_devices=1)
    arrays, args = {}, []
    for name in _INS:
        a = _np.ascontiguousarray(inputs[name])
        arrays[f"in_{name}_dram"] = a
        args.append(nc.dram_tensor(f"in_{name}_dram", a.shape, _mybir.dt.from_np(a.dtype), kind="ExternalInput").ap())
    for i, shape in enumerate(_OUTS):
        args.append(nc.dram_tensor(f"out_{i}_dram", shape, _mybir.dt.float32, kind="ExternalOutput").ap())
    args.append(nc.dram_tensor("m1_spill", (KT, P, T), _mybir.dt.float32, kind="Internal").ap())
    program(nc, *args)
    r = _run(nc, [arrays], core_ids=[0])
    return tuple(r.results[0][f"out_{i}_dram"] for i in range(len(_OUTS)))
```

```python
from contextlib import ExitStack, contextmanager

import concourse.bass as bass
from concourse import mybir

F32 = mybir.dt.float32
F32R = mybir.dt.float32r
ALU = mybir.AluOpType
ACT = mybir.ActivationFunctionType

P = 128
D = 1024
KT = D // P
SEQ, DEC = 1024, 64
T = SEQ + DEC
NT = SEQ // P + 1
CACHE = 128
HEADS, KVH, HD = 16, 4, 64
FF = 2816
FT = FF // P
EPS = 1e-6
FFN_GROUP = 8
FAR = 2.56e32
NB = 364
U0, VG0, Q0, K0, GA0, GB0 = 0, 1024, 2048, 3072, 3584, 4608
EXT = T + 4
SAMP = SEQ + 4


ATT_TILE = 48


def rows_of(n):
    return P if n < NT - 1 else DEC


def keys_of(n):
    if n == 0:
        return 0, P, P
    return ((n - 1) * P, 2 * P, 0) if n < NT - 1 else (SEQ, CACHE + DEC, P - DEC)


def queries_of(n):
    return (n * P, 0) if n < NT - 1 else (T - P, P - DEC)


def key_tiles(n):
    if n == 0:
        return [(0, P)]
    return [(n - 1, P), (n, P)] if n < NT - 1 else [(NT - 1, CACHE), (NT, DEC)]


MIX = (["act", "act"], ["act", "group", "act", "group"], 3, ["group", "group"])
GATE = (["act", "act"], ["act", "act"], KT // 2 - 2, ["act", "act"])
ATT = ([], ["act", "act", "group", "group"], (2, 2), [])
FFN = (["act", "dve", "act", "dve"], ["act", "dve", "group", "act", "dve", "group"], FT // 2 - 1,
       ["group", "group"])


class Count:

    def __init__(self):
        self.v, self.rate, self.i = {}, {}, 0

    def get(self, key, half=1):
        r = self.rate.get(key, 0) // half
        v = self.v.get(key, 0) // half
        return v + self.i * r if r else v

    def add(self, key, n=1):
        self.v[key] = self.v.get(key, 0) + n

    def slot(self, key="block"):
        return self.v.get(key, 0) % 2

    def block(self, kind):
        for _ in range(4 if kind == "group" else 1):
            self.tile(kind)
        self.add("block")

    def tile(self, kind):
        self.add(("freed", "act" if kind == "act" else "dve", self.slot("tile")))
        self.add("tile")

    @contextmanager
    def loop(self, eng, reps, kinds, **more):
        before = dict(self.v)
        dry = Count()
        for kind in kinds:
            dry.block(kind)
        for k, n in more.items():
            dry.add(k, n)
        assert not (dry.v.get("block", 0) % 2 or dry.v.get("tile", 0) % 2 or self.slot() or self.slot("tile"))
        self.rate = dry.v
        if isinstance(reps, tuple):
            with eng.Fori(0, reps[0]) as a:
                with eng.Fori(0, reps[1]) as b:
                    self.i = a * reps[1] + b
                    yield a, b
            reps = reps[0] * reps[1]
        else:
            with eng.Fori(0, reps) as i:
                self.i = i
                yield i
        for k, n in dry.v.items():
            assert self.v.get(k, 0) - before.get(k, 0) == n, (k, n)
            self.v[k] = before.get(k, 0) + n * reps
        self.rate, self.i = {}, 0


def program(nc, x_prompt, x_sample, cache_k, cache_v, cache_conv, ln_mix_g, w_in, ln_v_g, ln_v_b, w_s, b_s,
            attn_sinks, w_pa, w_pb, w_o, ln_ffn_g, w_up, w_conv, b_conv, w_down, ln_final_g,
            y_prompt, y_sample, new_k_prompt, new_v_prompt, new_conv_prompt, new_k_sample, new_v_sample,
            new_conv_sample, new_gmlp_v_sample, m1_spill):
    with ExitStack() as ctx:
        def sem(name):
            return ctx.enter_context(nc.semaphore(name))

        cursor = (nc.sbuf_base + 63) // 64 * 64

        def region(size):
            nonlocal cursor
            at = cursor
            cursor += (size + 63) // 64 * 64
            assert cursor <= nc.sbuf_usable_end, cursor
            return [at, at + size]

        def put(reg, name, shape, dt=F32, at=None):
            size = 4
            for s in shape[1:]:
                size *= s
            start = reg[0] + (reg[2] if len(reg) > 2 else 0) if at is None else reg[0] + at
            t = nc.alloc_sbuf_tensor_at(name, shape, dt, offset=start)
            assert start + size <= reg[1], (name, start + size - reg[1])
            if at is None:
                del reg[2:]
                reg.append(start - reg[0] + (size + 31) // 32 * 32)
            return t

        def again(reg):
            return reg[:2]

        r_h = region(2 * KT * T * 4)
        r_w = region(2 * 1024 * 4 * 3)
        r_s = region(NT * D * 4)
        r_a = region(KT * T * 4)
        r_g = region(3 * 2 * T * 4)
        r_t = region(16384)
        r_c = region(4416)

        h_hi = put(r_h, "h_hi", [P, KT, T], F32R)
        h_lo = put(r_h, "h_lo", [P, KT, T], F32R)
        h2_hi, h2_lo = h_hi, h_lo

        ident = put(r_c, "ident", [P, P])
        mean_mat = put(r_c, "mean_mat", [P, P])
        stat = put(r_c, "stat", [P, 3, 16])
        stat_y = put(r_c, "stat_y", [P, 3, 16])
        half_neg = put(r_c, "half_neg", [P, 1])
        ln_stats = put(r_c, "ln_stats", [P, 2, 2, 6])
        ln_mv = put(r_c, "ln_mv", [P, NT, 2])
        ln_rstd = put(r_c, "ln_rstd", [P, NT])
        slopes = put(r_c, "slopes", [P, HEADS])
        sinks = put(r_c, "sinks", [P, HEADS])
        sink_now = put(r_c, "sink_now", [P, 4])
        att_stat = put(r_c, "att_stat", [P, 2, 8, 4])
        conv_w = put(r_c, "conv_w", [P, 5, FT])
        ffn_c = put(r_c, "ffn_c", [P, FT + KT])
        conv_out = put(r_c, "conv_out", [P, 2, 2, FT])
        spare = put(r_c, "spare", [P, 4])

        r_w0 = again(r_w)
        xt_a = put(r_w0, "xt_a", [P, 2, D])
        xn = put(r_w0, "xn", [P, 2, D])
        mix_g = put(r_w0, "mix_g", [P, D])
        junk = put(r_w0, "junk", [P, D])
        raw = put(r_w, "raw", [P, 2, 1024])
        w_hi = put(r_w, "w_hi", [P, 2, 1024], F32R)
        w_lo = put(r_w, "w_lo", [P, 2, 1024], F32R)

        gs = put(r_s, "gs", [P, NT, D])
        r_v = [r_a[0], r_t[1]]
        wraw = put(r_v, "wraw", [P, KT, 256])
        wide_hi = put(r_v, "wide_hi", [P, 2, KT, 256], F32R)
        wide_lo = put(r_v, "wide_lo", [P, 2, KT, 256], F32R)
        ws_raw = put(r_v, "ws_raw", [P, KT, P])
        lnv_g = put(r_v, "lnv_g", [P, D])
        lnv_b = put(r_v, "lnv_b", [P, D])
        ws_t = put(r_v, "ws_t", [P, KT, P])
        bs = put(r_v, "bs", [P, KT, P])
        tab_rows = put(r_v, "tab_rows", [P, 2, P])
        xt_b = put(r_v, "xt_b", [P, 2, D])
        r_kw = again(r_g)
        kv_raw = put(r_kw, "kv_raw", [P, KT, 256])
        k_pair = (put(r_kw, "k_hi", [P, KT, 256], F32R), put(r_kw, "k_lo", [P, KT, 256], F32R))
        r_vw = again(r_a)
        v_pair = (put(r_vw, "v_hi", [P, KT, 256], F32R), put(r_vw, "v_lo", [P, KT, 256], F32R))

        acc = put(r_a, "acc", [P, KT, T])
        grp = put(r_g, "grp", [P, 2, T])
        grp_hi = put(r_g, "grp_hi", [P, 2, T], F32R)
        grp_lo = put(r_g, "grp_lo", [P, 2, T], F32R)
        xt2 = put(again(r_g), "xt2", [P, 2, D], at=2 * T * 4)
        gate = put(r_t, "gate", [P, 2, T])
        m1 = put(again(r_t), "m1", [P, 2, T])
        r_k = again(r_s)
        k_t = put(r_k, "k_t", [P, 2, T + CACHE])
        v_tok = put(r_k, "v_tok", [P, NT + 1, 256])
        k_now = put(r_k, "k_now", [P, T + CACHE])
        v_now = put(r_k, "v_now", [P, NT + 1, P])
        bias_now = put(r_k, "bias_now", [P, 4, 256])
        dist = put(r_k, "dist", [P, 256])
        r_t2 = again(r_t)
        sc_sb = put(r_t2, "sc_sb", [P, 3, 4, 256])
        pt_sb = put(r_t2, "pt_sb", [P, 2, 4, P])
        k_tok = put(again(r_t), "k_tok", [P, 3, 256], at=2 * T * 4)
        xres = put(again(r_s), "xres", [P, KT, T])
        r_f = again(r_a)
        a_ext = put(r_f, "a_ext", [P, 2, EXT])
        conv = put(r_f, "conv", [P, 2, EXT])
        sq = put(again(r_a), "sq", [P, KT, T])
        r_n = again(r_t)
        rb = put(r_n, "rb", [P, T])
        hn = put(r_n, "hn", [P, 2, T])
        r_y = again(r_t)
        fin_g = put(r_y, "fin_g", [P, D])
        r_y2 = again(r_a)
        y_sb = put(r_y2, "y_sb", [P, 2, D])
        y_junk = put(r_y2, "y_junk", [P, D])
        conv_rows = put(r_y2, "conv_rows", [2 * FT, 2, P])

        pset = [ctx.enter_context(nc.psum_tensor(f"pset{i}", [P, 3, 512], F32)) for i in range(2)]
        pex = ctx.enter_context(nc.psum_tensor("pex", [P, 2, 512], F32))

        s_ident = sem("s_ident")
        s_tab_in = sem("s_tab_in")
        s_row_in = sem("s_row_in")
        s_tab_t = sem("s_tab_t")
        s_tab = sem("s_tab")
        s_ws_t = sem("s_ws_t")
        s_ws = sem("s_ws")
        s_dist = sem("s_dist")
        s_distf = sem("s_distf")
        s_x_in = [sem(f"s_x_in{i}") for i in range(4)]
        s_sq = sem("s_sq")
        s_var = sem("s_var")
        s_rstd = sem("s_rstd")
        s_xn = sem("s_xn")
        s_xnt = sem("s_xnt")
        s_h_hi = sem("s_h_hi")
        s_h = sem("s_h")
        s_wide_in = sem("s_wide_in")
        s_kv_w = sem("s_kv_w")
        s_wide_hi = sem("s_wide_hi")
        s_wide = sem("s_wide")
        s_vt = sem("s_vt")
        s_vt_free = sem("s_vt_free")
        s_ln = sem("s_ln")
        s_ln_mv = sem("s_ln_mv")
        s_ln_v = sem("s_ln_v")
        s_ln_r = sem("s_ln_r")
        s_ln_a = sem("s_ln_a")
        s_vn = sem("s_vn")
        s_mixed = sem("s_mixed")
        s_s = sem("s_s")
        s_out = sem("s_out")
        s_vnout = sem("s_vnout")
        s_load = [sem(f"s_load{i}") for i in range(2)]
        s_w_hi = sem("s_w_hi")
        s_w = sem("s_w")
        s_tile = sem("s_tile")
        s_freed = {("freed", e, s): sem(f"s_freed_{e}{s}") for e in ("act", "dve") for s in range(2)}
        s_zero = sem("s_zero")
        s_prod = sem("s_prod")
        s_grp_hi = sem("s_grp_hi")
        s_grp = sem("s_grp")
        s_m1 = sem("s_m1")
        s_spill = sem("s_spill")
        s_ktr = sem("s_ktr")
        s_kt = sem("s_kt")
        s_cache = sem("s_cache")
        s_kv_out = sem("s_kv_out")
        s_now = sem("s_now")
        s_bias = sem("s_bias")
        s_q = sem("s_q")
        s_sc = sem("s_sc")
        s_smax = sem("s_smax")
        s_neg = sem("s_neg")
        s_exp = sem("s_exp")
        s_den = sem("s_den")
        s_p = sem("s_p")
        s_ptr = sem("s_ptr")
        s_pt = sem("s_pt")
        s_o = sem("s_o")
        s_b_hi = sem("s_b_hi")
        s_b = sem("s_b")
        s_x2_in = [sem(f"s_x2_in{i}") for i in range(2)]
        s_x2t = sem("s_x2t")
        s_x2 = sem("s_x2")
        s_m1_in = [sem(f"s_m1_in{i}") for i in range(2)]
        s_gb = sem("s_gb")
        s_sq2 = sem("s_sq2")
        s_ms = sem("s_ms")
        s_r0 = sem("s_r0")
        s_r1 = sem("s_r1")
        s_r2 = sem("s_r2")
        s_hn = sem("s_hn")
        s_hn_hi = sem("s_hn_hi")
        s_h2 = sem("s_h2")
        s_zext = sem("s_zext")
        s_c0 = sem("s_c0")
        s_c1 = sem("s_c1")
        s_conv = sem("s_conv")
        s_gelu = sem("s_gelu")
        s_tail = sem("s_tail")
        s_tail_t = sem("s_tail_t")
        s_tail_r = sem("s_tail_r")
        s_yt = sem("s_yt")
        s_ysq = sem("s_ysq")
        s_yv = sem("s_yv")
        s_yr = sem("s_yr")
        s_y = sem("s_y")
        s_y_out = [sem(f"s_y_out{i}") for i in range(2)]
        s_fin_g = sem("s_fin_g")

        def k_tiles(w):
            return w[0].rearrange("(k p) c -> p k c", p=P)

        w_in_v, w_up_v = k_tiles(w_in), k_tiles(w_up)
        w_pb_v = w_pb[0].rearrange("(h r) c -> r h c", r=HD)

        def token_rows(n):
            return x_prompt[0, n * P:(n + 1) * P, :] if n < NT - 1 else x_sample[0]

        def x_slot(n):
            return (xt_a, xt_b)[n % 4 // 2][0:rows_of(n), n % 2, :]

        def v_bank(n):
            return (pex[:, 0], pex[:, 1], pset[1][:, 2])[n % 3]

        def halves(t):
            return t[:, 0:2 * NB].rearrange("p (b n) -> p b n", b=2), t[:, 2 * NB:T]

        def pieces(s):
            return pset[s][:, 0:2, 0:NB], pset[s][:, 2, 0:T - 2 * NB]

        def row128(v):
            return v.rearrange("(a n) -> a n", a=1).broadcast_to([P, v.shape[0]])

        block = ctx.enter_context(nc.Block())

        @block.sync
        def _(sp):
            def wide(w, c0):
                if w:
                    sp.wait_ge(s_wide, w)
                sp.dma_start(wraw[:], w_in_v[:, :, bass.ds(c0, 256)]).then_inc(s_wide_in, 16)

            def load_x(n):
                if n >= 4:
                    sp.wait_ge(s_xn, n - 3)
                sp.dma_start(x_slot(n), token_rows(n)).then_inc(s_x_in[n % 4], 16)

            load_x(0)
            sp.dma_start(mix_g[:], row128(ln_mix_g[0])).then_inc(s_row_in, 16)
            load_x(1)
            wide(0, VG0)
            for n in range(2, NT):
                load_x(n)
            sp.dma_start(tab_rows[0:3 * FT, 0, :], w_conv[0].rearrange("i (f p) -> (i f) p", p=P)).then_inc(s_tab_in, 16)
            sp.dma_start(tab_rows[3 * FT:5 * FT, 0, :], cache_conv[0, 0].rearrange("i (f p) -> (i f) p", p=P)).then_inc(s_tab_in, 16)
            sp.dma_start(tab_rows[0:FT, 1, :], b_conv[0].rearrange("(f p) -> f p", p=P)).then_inc(s_tab_in, 16)
            sp.dma_start(tab_rows[FT:FT + KT, 1, :], ln_ffn_g[0].rearrange("(f p) -> f p", p=P)).then_inc(s_tab_in, 16)
            sp.dma_start(ws_raw[:], w_s[0].rearrange("g t s -> t g s")).then_inc(s_tab_in, 16)
            wide(1, VG0 + 256)
            sp.dma_start(lnv_g[:], row128(ln_v_g[0])).then_inc(s_row_in, 16)
            sp.dma_start(lnv_b[:], row128(ln_v_b[0])).then_inc(s_row_in, 16)
            sp.dma_start(bs[:], b_s.rearrange("a g t -> a (g t)").broadcast_to([P, D])).then_inc(s_row_in, 16)
            sp.dma_start(sinks[:], attn_sinks.broadcast_to([P, HEADS])).then_inc(s_row_in, 16)
            for w in range(2, 4):
                wide(w, VG0 + 256 * w)

            c = Count()

            def load(srcs):
                s = c.slot()
                if c.v.get("block", 0) >= 2 or c.rate:
                    sp.wait_ge(s_w, c.get("block") - 1)
                else:
                    sp.wait_ge(s_h, NT)
                for place, src in srcs:
                    sp.dma_start(place(raw[:, s, :]), src).then_inc(s_load[s], 16)

            def part(h, k):
                return lambda slot: slot[64 * h:64 * h + 64].rearrange("p (k c) -> p k c", k=k)

            def proj(view, c0):
                load([(part(h, KT), view[64 * h:64 * h + 64, :, bass.ds(c0, P)]) for h in range(2)])

            def group(w, j, b):
                view = k_tiles(w)
                load([(part(h, 2), view[64 * h:64 * h + 64, bass.ds(2 * j, 2), 512 * b:512 * b + 512])
                      for h in range(2)])

            def load_m1(m, k):
                if not isinstance(m, int):
                    sp.wait_ge(s_prod, m + (KT - 1))
                sp.dma_start(m1[:, k, :], m1_spill[bass.ds(m, 1)].rearrange("a p t -> (a p) t"))\
                  .then_inc(s_m1_in[k], 16)

            def load_residual():
                sp.wait_ge(s_tile, c.get("tile") - 1)
                for k in range(2):
                    load_m1(k, k)
                for n in range(NT):
                    if n >= 2:
                        sp.wait_ge(s_x2t, n - 1)
                    sp.dma_start(xt2[0:rows_of(n), n % 2, :], token_rows(n)).then_inc(s_x2_in[n % 2], 16)

            def mix(c0, w, with_m1, early=()):
                pro, body, reps, epi = MIX
                for k in range(2):
                    proj(w_in_v, c0 + P * k)
                    if k == 1 and with_m1:
                        load_residual()
                    c.block(pro[k])
                with c.loop(sp, reps, body) as i:
                    for k in range(2):
                        if with_m1:
                            load_m1(i * 2 + (2 + k), k)
                        proj(w_in_v, i * 256 + (c0 + 256 + P * k))
                        c.block(body[2 * k])
                        group(w, i, k)
                        c.block(body[2 * k + 1])
                for c1 in early:
                    proj(w_in_v, c1)
                    c.block("act")
                for b in range(2):
                    group(w, reps, b)
                    c.block(epi[b])

            mix(U0, w_pa, False, early=(GA0, GA0 + P))
            with c.loop(sp, GATE[2], GATE[1]) as i:
                for k in range(2):
                    proj(w_in_v, i * 256 + (GA0 + P * (2 + k)))
                    c.block("act")
            for k in range(2):
                proj(w_in_v, GA0 + P * (KT - 2 + k))
                c.block("act")
            with c.loop(sp, ATT[2], ATT[1]) as (pair, half):
                for k in range(2):
                    load([(lambda slot, h=h: slot.rearrange("p (k c) -> p k c", k=KT)[:, :, 64 * h:64 * h + 64],
                           w_in_v[:, :, bass.ds(pair * 512 + half * 128 + (Q0 + 256 * h + 64 * k), HD)])
                          for h in range(2)])
                    c.block("act")
                for b in range(2):
                    load([(part(h, 2), w_pb_v[:, bass.ds(pair * 8 + half * 2 + 4 * h, 2), 512 * b:512 * b + 512])
                          for h in range(2)])
                    c.block("group")
            mix(GB0, w_o, True)
            pro, body, reps, epi = FFN
            for k in range(2):
                proj(w_up_v, P * k)
                c.block(pro[0])
                proj(w_up_v, FF + P * k)
                c.block(pro[1])
            with c.loop(sp, reps, body) as i:
                for k in range(2):
                    proj(w_up_v, i * 256 + (256 + P * k))
                    c.block(body[0])
                    proj(w_up_v, i * 256 + (FF + 256 + P * k))
                    c.block(body[1])
                    group(w_down, i, k)
                    c.block(body[2])
            for b in range(2):
                group(w_down, reps, b)
                c.block(epi[b])
            sp.dma_start(fin_g[:], row128(ln_final_g)).then_inc(s_fin_g, 16)
            sp.wait_ge(s_tail_r, 2)
            for q, out in enumerate((new_conv_prompt, new_conv_sample)):
                sp.dma_start(out[0, 0].rearrange("i (f p) -> (i f) p", p=P), conv_rows[:, q, :]).then_inc(s_out, 16)
            for n in range(NT):
                sp.wait_ge(s_y, n + 1)
                dst = y_prompt[0, n * P:(n + 1) * P, :] if n < NT - 1 else y_sample[0]
                sp.dma_start(dst, y_sb[0:rows_of(n), n % 2, :]).then_inc(s_y_out[n % 2], 16)
            sp.wait_ge(s_out, 32)
            sp.wait_ge(s_y_out[0], 16 * 5)
            sp.wait_ge(s_y_out[1], 16 * 4)
            sp.wait_ge(s_vnout, 16)
            sp.wait_ge(s_kv_out, 64)
            sp.wait_ge(s_spill, 16 * KT)

        @block.gpsimd
        def _(pool):
            pool.memset(ident[:], 0.0).then_inc(s_zero, 1)
            pool.memset(half_neg[:], -0.5).then_inc(s_zero, 1)
            pool.memset(mean_mat[:], 1.0 / D).then_inc(s_zero, 1)
            for i in range(HEADS):
                last = pool.memset(slopes[:, i:i + 1], -2.0 ** (-8.0 * (i + 1) / HEADS))
            last.then_inc(s_zero, 1)
            pool.wait_ge(s_zero, 4)
            pool.affine_select(out=ident[:], in_=ident[:], compare_op=ALU.not_equal, fill=1.0, base=0,
                               pattern=[[-1, P]], channel_multiplier=1).then_inc(s_ident, 1)

            def rstd(n, table, s_in, s_mid, s_end, done):
                r = rows_of(n)
                pool.wait_ge(s_in, n + 1)
                pool.tensor_scalar(table[0:r, 1, n:n + 1], table[0:r, 0, n:n + 1], 1.0 / D, EPS, ALU.mult,
                                   ALU.add).then_inc(s_mid, 1)
                pool.wait_ge(s_mid, n + 1)
                pool.tensor_tensor(table[0:r, 2, n:n + 1], table[0:r, 1, n:n + 1], half_neg[0:r, :],
                                   ALU.pow).then_inc(s_end, 1)

            for n in range(NT):
                rstd(n, stat, s_sq, s_var, s_rstd, n)

            for n in range(NT):
                r = rows_of(n)
                pool.wait_ge(s_ln_mv, n + 1)
                pool.tensor_scalar(ln_rstd[0:r, n:n + 1], ln_mv[0:r, n, 1:2], 1.0, EPS, ALU.mult,
                                   ALU.add).then_inc(s_ln_v, 1)
                pool.wait_ge(s_ln_v, n + 1)
                pool.tensor_tensor(ln_rstd[0:r, n:n + 1], ln_rstd[0:r, n:n + 1], half_neg[0:r, :],
                                   ALU.pow).then_inc(s_ln_r, 1)
            pool.wait_ge(s_tile, 1)
            pool.memset(acc[:], 0.0).then_inc(s_zero, 1)

            pool.wait_ge(s_tile, ATT_TILE - KT + 2)
            pool.wait_ge(s_prod, 2 * 4)
            pool.dma_start(kv_raw[:], w_in_v[:, :, K0:K0 + 256]).then_inc(s_kv_w, 16)
            pool.dma_start(k_tok[:, 2, :], cache_k[0, 0].rearrange("t h d -> t (h d)")).then_inc(s_cache, 16)
            pool.dma_start(v_tok[:, NT - 1, :], cache_v[0, 0].rearrange("t h d -> t (h d)")).then_inc(s_cache, 16)

            for half in range(2):
                with pool.Fori(0, KT // 2) as i:
                    pool.wait_ge(s_m1, i + (3 + half * KT // 2))
                    pool.dma_start(m1_spill[bass.ds(i + half * KT // 2, 1)].rearrange("a p t -> (a p) t"),
                                   acc[:, bass.ds(i + half * KT // 2, 1), :].rearrange("p a t -> p (a t)"))\
                        .then_inc(s_spill, 16)
                pool.wait_ge(s_spill, 16 * (half + 1) * KT // 2)
                if half == 0:
                    pool.wait_ge(s_wide, 5)
                    pool.dma_start(kv_raw[:], w_in_v[:, :, K0 + 256:K0 + 512]).then_inc(s_kv_w, 16)

            pool.wait_ge(s_grp, 4)
            pool.wait_ge(s_prod, 2 * 4)
            pool.iota(dist[:].bitcast(mybir.dt.int32), [[-1, 256]], base=P, channel_multiplier=1).then_inc(s_dist, 1)
            pool.wait_ge(s_distf, 2)
            pool.affine_select(out=dist[0:64, :], in_=dist[0:64, :], compare_op=ALU.is_ge, fill=FAR, base=191,
                               pattern=[[-1, 256]], channel_multiplier=0).then_inc(s_dist, 1)
            pool.affine_select(out=dist[64:P, :], in_=dist[64:P, :], compare_op=ALU.is_ge, fill=FAR, base=-64,
                               pattern=[[1, 256]], channel_multiplier=0).then_inc(s_dist, 1)
            pool.wait_ge(s_dist, 3)
            pool.wait_ge(s_vt, 6 * NT)
            pool.memset(acc[:], 0.0).then_inc(s_zero, 1)
            pool.wait_ge(s_kt, NT + 1)
            pool.wait_ge(s_vt_free, 6 * NT + 3)
            pool.wait_ge(s_cache, 32)
            with pool.Fori(0, 2) as pair:
                pool.wait_ge(s_tile, pair * 20 + ATT_TILE)
                pool.tensor_copy(k_now[:], k_t[:, bass.ds(pair, 1), :].rearrange("p a c -> p (a c)")).then_inc(s_now, 1)
                pool.tensor_copy(v_now[:, 0:NT, :], v_tok[:, 0:NT, bass.ds(pair * P, P)]).then_inc(s_now, 1)
                pool.tensor_copy(v_now[0:DEC, NT, :], v_tok[0:DEC, NT, bass.ds(pair * P, P)]).then_inc(s_now, 1)

            pool.wait_ge(s_h2, KT)
            pool.memset(a_ext[:, :, 0:2], 0.0).then_inc(s_zext, 1)

            def keep_tail(f, k):
                src = a_ext[:, k, :]
                at = bass.ds(f, 1)
                pool.tensor_copy(conv_out[:, 0, :, at], src[:, SEQ:SEQ + 2].unsqueeze(2))
                pool.tensor_copy(conv_out[:, 1, :, at], src[:, EXT - 2:EXT].unsqueeze(2)).then_inc(s_tail, 1)

            for k in range(2):
                pool.wait_ge(s_c0, k + 1)
                keep_tail(k, k)
            with pool.Fori(0, FFN[2]) as i:
                for k in range(2):
                    pool.wait_ge(s_c0, i * 2 + (k + 3))
                    keep_tail(i * 2 + (k + 2), k)
            for n in range(NT):
                rstd(n, stat_y, s_ysq, s_yv, s_yr, n)

        @block.scalar
        def _(act):
            copy = ACT.Copy
            act.sem_inc(s_freed["freed", "act", 0], 1)
            act.sem_inc(s_freed["freed", "act", 1], 1)
            act.sem_inc(s_vt_free, 3)

            def h_hi_part(n):
                r = rows_of(n)
                act.wait_ge(s_xnt, n + 1)
                for b in range(2):
                    last = act.activation(h_hi[:, 4 * b:4 * b + 4, n * P:n * P + r],
                                          pset[n % 2][:, b, :].rearrange("p (k t) -> p k t", k=4)[:, :, 0:r], copy)
                last.then_inc(s_h_hi, 1)

            def wide_hi_part(w, dst, src=wraw, arrived=s_wide_in, before=0):
                act.wait_ge(arrived, (w - before) * 16 + 16)
                act.activation(dst, src[:], copy).then_inc(s_wide_hi, 1)

            def vg(w, n):
                r = rows_of(n)
                act.wait_ge(s_vt, w * NT + n + 1)
                act.activation(gs[0:r, n, 256 * w:256 * w + 256], v_bank(n)[0:r, 0:256],
                               ACT.Gelu_apprx_tanh).then_inc(s_vt_free, 1)

            for n in range(NT + 3):
                if n < NT:
                    r = rows_of(n)
                    act.wait_ge(s_x_in[n % 4], 16 * (n // 4 + 1))
                    if n >= 1:
                        act.wait_ge(s_sq, n)
                    act.activation(junk[0:r, :], x_slot(n), ACT.Square,
                                   accum_out=stat[0:r, 0, n:n + 1]).then_inc(s_sq, 1)
                if 1 <= n <= NT:
                    h_hi_part(n - 1)
                if n == 2:
                    wide_hi_part(0, wide_hi[:, 0])
                if n == NT - 2:
                    wide_hi_part(1, wide_hi[:, 1])
                if n >= 3:
                    vg(0, n - 3)
            act.wait_ge(s_tab_t, 1)
            act.activation(conv_w[:].rearrange("p i f -> p (i f)"), pset[1][:, 0, 0:5 * FT], copy)
            act.activation(ffn_c[:], pset[1][:, 0, P:P + FT + KT], copy)
            for b in range(2):
                last = act.activation(ws_t[:, 4 * b:4 * b + 4, :], pset[0][:, b, :].rearrange("p (k t) -> p k t", k=4), copy)
            last.then_inc(s_ws_t, 1)

            c = Count()

            def split_hi(ahead=1):
                s = (c.slot() + ahead) % 2
                act.wait_ge(s_load[s], c.get("block", 2) * 32 + ((c.slot() + ahead) // 2 * 32 + 32))
                if c.v.get("tile", 0):
                    act.wait_ge(s_tile, c.get("tile"))
                act.activation(w_hi[:, s, :], raw[:, s, :], copy).then_inc(s_w_hi, 1)

            def group_hi(g):
                act.wait_ge(s_prod, g * 2 + 2)
                act.wait_ge(s_tile, c.get("tile"))
                act.activation(grp_hi[:], grp[:], copy).then_inc(s_grp_hi, 1)

            def evacuate(dst, func, **kw):
                act.wait_ge(s_tile, c.get("tile") + 1)
                s = c.slot("tile")
                for d, q in zip(halves(dst), pieces(s)):
                    last = act.activation(d, q, func, **kw)
                last.then_inc(s_freed["freed", "act", s], 1)

            def mix(project, between=None, after=None, early=None, first=1):
                pro, body, reps, epi = MIX
                for k in range(2):
                    if k >= 1 - first:
                        split_hi()
                    project(k)
                    c.block(pro[k])
                if between:
                    between()
                with c.loop(act, reps, body, g=1):
                    for k in range(2):
                        split_hi()
                        if k == 0:
                            group_hi(c.get("g"))
                            act.wait_ge(s_grp, c.get("g") + 1)
                        project(k)
                        c.block("act")
                        split_hi()
                        c.block("group")
                    c.add("g")
                split_hi()
                group_hi(c.get("g"))
                if early:
                    for k in range(2):
                        early(k)
                        c.block("act")
                        split_hi()
                if after:
                    after(0)
                c.block("group")
                c.add("g")
                split_hi()
                if after:
                    after(1)
                c.block("group")

            def values_out():
                act.wait_ge(s_vn, NT)
                act.dma_start(new_gmlp_v_sample[0, 0], gs[0:DEC, NT - 1, :]).then_inc(s_vnout, 16)

            for w in range(1, 4):
                if w < 3:
                    wide_hi_part(w + 1, wide_hi[:, (w + 1) % 2])
                else:
                    split_hi(0)
                    split_hi(1)
                for n in range(NT):
                    vg(w, n)
            c.v["m"] = 0

            def gate_a(k):
                act.wait_ge(s_m1, c.get("m") + 1)
                evacuate(gate[:, k, :], ACT.Sigmoid)
                c.add("m")

            mix(lambda k: evacuate(grp[:, k, :], ACT.Gelu_apprx_tanh), between=values_out, early=gate_a, first=0)

            with c.loop(act, GATE[2], GATE[1], m=2):
                for k in range(2):
                    split_hi()
                    gate_a(k)
                    c.block("act")
            wide_hi_part(4, k_pair[0][:], kv_raw, s_kv_w, 4)
            for k in range(2):
                split_hi()
                gate_a(k)
                c.block("act")
                if k == 0:
                    wide_hi_part(5, v_pair[0][:], kv_raw, s_kv_w, 4)

            for n in range(NT):
                r = rows_of(n)
                act.wait_ge(s_vt, 4 * NT + n + 1)
                if n >= 2:
                    act.wait_ge(s_ktr, n - 1)
                act.activation(k_tok[0:r, n % 2, :], pset[0][0:r, n % 3, 0:256], copy).then_inc(s_vt_free, 1)
            for n in range(NT):
                r, slot = rows_of(n), n if n < NT - 1 else NT
                act.wait_ge(s_vt, 5 * NT + n + 1)
                act.activation(v_tok[0:r, slot, :], pset[0][0:r, n % 3, 0:256], copy).then_inc(s_vt_free, 1)
            act.wait_ge(s_vt_free, 6 * NT + 3)
            for dst, src in ((new_k_prompt, k_tok[:, (NT - 2) % 2, :]), (new_k_sample, k_tok[0:DEC, (NT - 1) % 2, :]),
                             (new_v_prompt, v_tok[:, NT - 2, :]), (new_v_sample, v_tok[0:DEC, NT, :])):
                act.dma_start(dst[0, 0].rearrange("t h d -> t (h d)"), src).then_inc(s_kv_out, 16)

            with c.loop(act, ATT[2], ATT[1], att=NT):
                for k in range(2):
                    split_hi()
                    evacuate(grp[:, k, :], copy, scale=HD ** -0.5)
                    c.block("act")
                for step in range(NT + 3):
                    if step < NT:
                        n, a = step, att_stat[:, step % 2]
                        w = keys_of(n)[1]
                        act.wait_ge(s_neg, c.get("att") + n + 1)
                        for e in range(4):
                            act.activation(sc_sb[:, n % 3, e, 0:w], sc_sb[:, n % 3, e, 0:w], ACT.Exp,
                                           bias=a[:, 1, e:e + 1], accum_out=a[:, 3, e:e + 1])
                        act.activation(a[:, 4, :], a[:, 2, :], ACT.Exp).then_inc(s_exp, 1)
                    if step >= 3:
                        n, r, q0 = step - 3, rows_of(step - 3), queries_of(step - 3)[1]
                        act.wait_ge(s_o, c.get("att") + n + 1)
                        act.activation(grp_hi[:, :, n * P:n * P + r],
                                       pset[n % 2][:, 2, 0:256].rearrange("p (k q) -> p k q", k=2)[:, :, q0:P],
                                       copy).then_inc(s_b_hi, 1)
                    if 2 <= step <= NT + 1:
                        n = step - 2
                        act.wait_ge(s_ptr, c.get("att") + n + 1)
                        for j, (_, rows) in enumerate(key_tiles(n)):
                            last = act.activation(pt_sb[0:rows, j, :, :],
                                                  pset[0][0:rows, j, :].rearrange("p (e q) -> p e q", e=4)[:, :, :], copy)
                        last.then_inc(s_pt, 1)
                c.add("att", NT)
                for b in range(2):
                    split_hi()
                    c.block("group")

            for n in range(NT):
                r = rows_of(n)
                act.wait_ge(s_x2t, n + 1)
                for b in range(2):
                    last = act.activation(xres[:, 4 * b:4 * b + 4, n * P:n * P + r],
                                          pset[n % 2][:, b, :].rearrange("p (k t) -> p k t", k=4)[:, :, 0:r], copy)
                last.then_inc(s_x2, 1)

            def squares(b):
                for q in range(4):
                    kt, key = 4 * b + q, ("freed", "dve", q % 2)
                    act.wait_ge(s_freed[key], c.get(key) + q // 2 + 2)
                    act.activation(sq[:, kt, :], xres[:, kt, :], ACT.Square).then_inc(s_sq2, 1)

            mix(lambda k: evacuate(grp[:, k, :], ACT.Sigmoid), after=squares)

            act.wait_ge(s_r0, 1)
            act.activation(rb[:], rb[:], ACT.Sqrt).then_inc(s_r1, 1)
            for kt in range(KT):
                act.wait_ge(s_hn, kt + 1)
                act.activation(h2_hi[:, kt, :], hn[:, kt % 2, :], copy).then_inc(s_hn_hi, 1)

            def up_gate(k, first):
                f, key = c.get("f"), ("freed", "act", c.slot("tile"))
                if not first:
                    act.wait_ge(s_conv, f - 1)
                    act.wait_ge(s_tail, f - 1)
                at = bass.ds(f, 1)
                act.activation(a_ext[:, k, SEQ + 2:SEQ + 4], conv_w[:, 3:5, at].rearrange("p i f -> p (i f)"), copy)
                act.wait_ge(s_tile, c.get("tile") + 1)
                p0, p1 = pieces(key[2])
                act.activation(a_ext[:, k, 2:2 + 2 * NB].rearrange("p (b n) -> p b n", b=2), p0, copy)
                act.activation(a_ext[:, k, 2 + 2 * NB:2 + SEQ], p1[:, 0:SEQ - 2 * NB], copy)
                act.activation(a_ext[:, k, SAMP:EXT], p1[:, SEQ - 2 * NB:], copy).then_inc(s_freed[key], 1)
                act.wait_ge(s_freed[key], c.get(key) + 2)
                act.wait_ge(s_prod, f + (2 * FFN_GROUP - 1) if not first else 2 * FFN_GROUP)
                act.activation(conv[:, k, 2:EXT], a_ext[:, k, 2:EXT], ACT.Identity, bias=ffn_c[:, at],
                               scale=conv_w[:, 2, at]).then_inc(s_c0, 1)

            def up_value():
                f = c.get("f")
                act.wait_ge(s_conv, f + 1)
                k = c.slot("f")
                act.activation(conv[:, k, 2:EXT], conv[:, k, 2:EXT], ACT.Gelu_apprx_tanh).then_inc(s_gelu, 1)

            pro, body, reps, epi = FFN
            for k in range(2):
                split_hi()
                up_gate(k, True)
                c.block("act")
                split_hi()
                up_value()
                c.block("dve")
                c.add("f")
            with c.loop(act, reps, body, g=1, f=2):
                for k in range(2):
                    split_hi()
                    if k == 0:
                        group_hi(c.get("g"))
                    up_gate(k, False)
                    c.block("act")
                    split_hi()
                    up_value()
                    c.block("dve")
                    split_hi()
                    c.block("group")
                    c.add("f")
                c.add("g")
            split_hi()
            group_hi(c.get("g"))
            c.block("group")
            c.block("group")

            act.wait_ge(s_tail_t, 1)
            act.activation(conv_rows[:].rearrange("r q p -> r (q p)"), pex[0:2 * FT, 0, 0:2 * P], copy).then_inc(s_tail_r, 2)
            for n in range(NT):
                r = rows_of(n)
                act.wait_ge(s_yt, n + 1)
                if n >= 1:
                    act.wait_ge(s_ysq, n)
                act.activation(y_junk[0:r, :].rearrange("p (b c) -> p b c", b=2), pset[n % 2][0:r, 0:2, :], ACT.Square,
                               accum_out=stat_y[0:r, 0, n:n + 1]).then_inc(s_ysq, 1)

        @block.vector
        def _(dve):
            for key, n in ((s_freed["freed", "dve", 0], 1), (s_freed["freed", "dve", 1], 1), (s_m1, 2)):
                dve.sem_inc(key, n)

            def h_lo_part(n):
                r = rows_of(n)
                dve.wait_ge(s_h_hi, n + 1)
                for b in range(2):
                    at = (slice(None), slice(4 * b, 4 * b + 4), slice(n * P, n * P + r))
                    last = dve.tensor_tensor(h_lo[at], pset[n % 2][:, b, :].rearrange("p (k t) -> p k t", k=4)[:, :, 0:r],
                                             h_hi[at].bitcast(F32), ALU.subtract)
                last.then_inc(s_h, 1)

            dve.wait_ge(s_row_in, 16)
            def wide_lo_part(w, dst, hi, src=wraw):
                dve.wait_ge(s_wide_hi, w + 1)
                dve.tensor_tensor(dst, src[:], hi.bitcast(F32), ALU.subtract).then_inc(s_wide, 1)

            for n in range(NT):
                r = rows_of(n)
                dve.wait_ge(s_rstd, n + 1)
                dve.wait_ge(s_x_in[n % 4], 16 * (n // 4 + 1))
                if n >= 2:
                    dve.wait_ge(s_xnt, n - 1)
                dve.scalar_tensor_tensor(xn[0:r, n % 2, :], x_slot(n), stat[0:r, 2, n:n + 1], mix_g[0:r, :],
                                         ALU.mult, ALU.mult).then_inc(s_xn, 1)
                if n >= 1:
                    h_lo_part(n - 1)
                if n == 2:
                    wide_lo_part(0, wide_lo[:, 0], wide_hi[:, 0])
                if n == NT - 2:
                    wide_lo_part(1, wide_lo[:, 1], wide_hi[:, 1])
            h_lo_part(NT - 1)
            dve.wait_ge(s_ws_t, 1)
            dve.memset(ws_t[64:P, :, 0:64], 0.0).then_inc(s_ws, 1)
            for w in range(2, 4):
                wide_lo_part(w, wide_lo[:, w % 2], wide_hi[:, w % 2])

            c = Count()

            def split_lo(ahead=1):
                s = (c.slot() + ahead) % 2
                dve.wait_ge(s_w_hi, c.get("block") + (ahead + 1))
                dve.tensor_tensor(w_lo[:, s, :], raw[:, s, :], w_hi[:, s, :].bitcast(F32), ALU.subtract).then_inc(s_w, 1)

            def group_lo(g):
                dve.wait_ge(s_grp_hi, g + 1)
                dve.tensor_tensor(grp_lo[:], grp[:], grp_hi[:].bitcast(F32), ALU.subtract).then_inc(s_grp, 1)

            def add_group(dst, b):
                for q in range(4):
                    dve.wait_ge(s_tile, c.get("tile") + 1)
                    s = c.slot("tile")
                    for d, v in zip(halves(dst[:, 4 * b + q, :]), pieces(s)):
                        last = dve.tensor_tensor(d, v, d, ALU.add)
                    last.then_inc(s_freed["freed", "dve", s], 1)
                    c.tile("group")
                c.add("block")

            def evacuated(k):
                key = ("freed", "act", c.slot("tile"))
                dve.wait_ge(s_freed[key], c.get(key) + 2)

            def mix(project, dst, between=None, early=None, first=1):
                pro, body, reps, epi = MIX
                for k in range(2):
                    if k >= 1 - first:
                        split_lo()
                    if not between:
                        project(k)
                    c.block(pro[k])
                    c.add("kt")
                if between:
                    between()
                with c.loop(dve, reps, body, g=1, kt=2):
                    for k in range(2):
                        split_lo()
                        if k == 0:
                            group_lo(c.get("g"))
                        project(k)
                        c.block("act")
                        c.add("kt")
                        split_lo()
                        add_group(dst, k)
                    c.add("g")
                split_lo()
                group_lo(c.get("g"))
                if early:
                    for k in range(2):
                        early(k)
                        c.block("act")
                        split_lo()
                add_group(dst, 0)
                c.add("g")
                split_lo()
                add_group(dst, 1)

            def values():
                dve.wait_ge(s_row_in, 16 * 5)
                for n in range(NT):
                    r = rows_of(n)
                    dve.wait_ge(s_vt_free, 3 * NT + n + 1 + 3)
                    if n >= 1:
                        dve.wait_ge(s_ln_mv, n)
                    for b in range(2):
                        last = dve.bn_stats(ln_stats[0:r, 0, b, :], gs[0:r, n, 512 * b:512 * b + 512])
                    last.then_inc(s_ln, 1)
                    dve.wait_ge(s_ln, n + 1)
                    dve.bn_aggr(ln_mv[0:r, n, :], ln_stats[0:r, 0]).then_inc(s_ln_mv, 1)
                    dve.wait_ge(s_ln_mv, n + 1)
                    dve.scalar_tensor_tensor(gs[0:r, n, :], gs[0:r, n, :], ln_mv[0:r, n, 0:1], lnv_g[0:r, :],
                                             ALU.subtract, ALU.mult).then_inc(s_ln_a, 1)
                    dve.wait_ge(s_ln_a, n + 1)
                    dve.wait_ge(s_ln_r, n + 1)
                    dve.scalar_tensor_tensor(gs[0:r, n, :], gs[0:r, n, :], ln_rstd[0:r, n:n + 1], lnv_b[0:r, :],
                                             ALU.mult, ALU.add).then_inc(s_vn, 1)

            def mixed():
                for n in range(NT):
                    r = rows_of(n)
                    src = (pex, *pset)[n % 3]
                    dve.wait_ge(s_mixed, n + 1)
                    if n == NT - 1:
                        dve.wait_ge(s_vnout, 16)
                    for b in range(2):
                        last = dve.tensor_tensor(
                            gs[:, n, 512 * b:512 * b + 512].rearrange("p (g t) -> p g t", g=4)[:, :, 0:r],
                            src[:, b, :].rearrange("p (g t) -> p g t", g=4)[:, :, 0:r],
                            bs[:, 4 * b:4 * b + 4, 0:r], ALU.add)
                    last.then_inc(s_s, 1)
                dve.wait_ge(s_s, NT)
                for k in range(2):
                    product(k, k)
                dve.wait_ge(s_zero, 5)

            def product(k, kt):
                at = kt * P
                p = grp[:, k, 0:SEQ].rearrange("p (n t) -> p n t", t=P)
                dve.tensor_tensor(p, p, gs[:, 0:NT - 1, bass.ds(at, P)], ALU.mult)
                p = grp[:, k, SEQ:T]
                dve.tensor_tensor(p, p, gs[:, NT - 1, bass.ds(at, DEC)], ALU.mult).then_inc(s_prod, 1)

            def project_u(k):
                evacuated(k)
                product(k, c.get("kt"))

            split_lo(0)
            split_lo(1)
            values()
            gate_in = []

            def gate_early(k):
                key = ("freed", "act", c.slot("tile"))
                gate_in.append((s_freed[key], c.get(key) + 2))

            mix(project_u, acc, between=mixed, early=gate_early, first=0)

            def gated(m, k):
                a = acc[:, bass.ds(m, 1), :].rearrange("p a t -> p (a t)")
                dve.tensor_tensor(a, a, gate[:, k, :], ALU.mult).then_inc(s_m1, 1)

            for k, (key, value) in enumerate(gate_in):
                dve.wait_ge(key, value)
                gated(k, k)
            c.v["m"] = 2
            with c.loop(dve, GATE[2], GATE[1], m=2):
                for k in range(2):
                    split_lo()
                    evacuated(k)
                    gated(c.get("m"), k)
                    c.block("act")
                    c.add("m")
            wide_lo_part(4, k_pair[1][:], k_pair[0][:], kv_raw)
            for k in range(2):
                split_lo()
                evacuated(k)
                gated(c.get("m"), k)
                c.block("act")
                c.add("m")
                if k == 0:
                    wide_lo_part(5, v_pair[1][:], v_pair[0][:], kv_raw)

            for n in range(NT + 1):
                r = (rows_of(n) if n < NT else CACHE)
                col = n * P if n < NT - 1 else (SEQ + CACHE if n == NT - 1 else SEQ)
                dve.wait_ge(s_ktr, n + 1)
                dve.tensor_copy(k_t[:, :, col:col + r],
                                pex[:, n % 2, 0:256].rearrange("p (k t) -> p k t", k=2)[:, :, 0:r]).then_inc(s_kt, 1)
            dve.wait_ge(s_dist, 1)
            dve.tensor_copy(bias_now[:, 0, :], dist[:].bitcast(mybir.dt.int32)).then_inc(s_distf, 1)
            dve.wait_ge(s_distf, 1)
            dve.scalar_tensor_tensor(dist[:], bias_now[:, 0, :], -1.0, bias_now[:, 0, :], ALU.mult,
                                     ALU.max).then_inc(s_distf, 1)

            dve.wait_ge(s_dist, 3)
            dve.wait_ge(s_zero, 6)
            dve.wait_ge(s_kv_out, 64)
            with c.loop(dve, ATT[2], ATT[1], att=NT, den=2 * NT) as (pair, half):
                for k in range(2):
                    split_lo()
                    c.block("act")
                for e in range(4):
                    at = bass.ds(pair * 8 + half * 2 + (4 * (e // 2) + e % 2), 1)
                    dve.tensor_scalar(bias_now[:, e, :], dist[:], slopes[:, at], None, ALU.mult)
                    last = dve.tensor_copy(sink_now[:, e:e + 1], sinks[:, at])
                last.then_inc(s_bias, 1)
                dve.wait_ge(s_bias, c.i + 1)
                for step in range(NT + 4):
                    if step < NT:
                        n, a = step, att_stat[:, step % 2]
                        w, b0 = keys_of(n)[1], keys_of(n)[2]
                        src = pex if n % 2 == 0 else pset[1]
                        if n >= 3:
                            dve.wait_ge(s_ptr, c.get("att") + (n - 2))
                        dve.wait_ge(s_sc, c.get("att") + n + 1)
                        dve.tensor_copy(spare[:, 3:4], sink_now[:, 0:1])
                        for e in range(4):
                            last = dve.tensor_tensor_reduce(
                                sc_sb[:, n % 3, e, 0:w], src[:, e // 2, 256 * (e % 2):256 * (e % 2) + w],
                                bias_now[:, e, b0:b0 + w], 1.0, sink_now[:, e:e + 1], ALU.add, ALU.max,
                                a[:, 0, e:e + 1])
                        last.then_inc(s_smax, 1)
                        dve.wait_ge(s_smax, c.get("att") + n + 1)
                        dve.tensor_scalar(a[:, 1, :], a[:, 0, :], -1.0, None, ALU.mult)
                        dve.tensor_tensor(a[:, 2, :], sink_now[:, :], a[:, 0, :], ALU.subtract).then_inc(s_neg, 1)
                    if 1 <= step <= NT:
                        n, a = step - 1, att_stat[:, (step - 1) % 2]
                        w = keys_of(n)[1]
                        dve.wait_ge(s_exp, c.get("att") + n + 1)
                        dve.tensor_tensor(a[:, 5, :], a[:, 3, :], a[:, 4, :], ALU.add).then_inc(s_den, 1)
                        dve.wait_ge(s_den, c.get("den") + 1)
                        dve.reciprocal(a[:, 6, :], a[:, 5, :]).then_inc(s_den, 1)
                        dve.wait_ge(s_den, c.get("den") + 2)
                        c.add("den", 2)
                        for e in range(4):
                            p = sc_sb[:, n % 3, e, 0:w]
                            last = dve.tensor_scalar(p, p, a[:, 6, e:e + 1], None, ALU.mult)
                        last.then_inc(s_p, 1)
                    if step >= 4:
                        n, r, q0 = step - 4, rows_of(step - 4), queries_of(step - 4)[1]
                        dve.wait_ge(s_b_hi, c.get("att") + n + 1)
                        at = (slice(None), slice(None), slice(n * P, n * P + r))
                        dve.tensor_tensor(grp_lo[at], pset[n % 2][:, 2, 0:256].rearrange("p (k q) -> p k q", k=2)[:, :, q0:P],
                                          grp_hi[at].bitcast(F32), ALU.subtract).then_inc(s_b, 1)
                c.add("att", NT)
                for b in range(2):
                    split_lo()
                    add_group(acc, b)

            c.v["kt"] = 0

            def merge(k):
                evacuated(k)
                a = acc[:, bass.ds(c.get("kt"), 1), :].rearrange("p a t -> p (a t)")
                dve.tensor_tensor(grp[:, k, :], grp[:, k, :], a, ALU.mult).then_inc(s_gb, 1)
                dve.wait_ge(s_gb, c.get("kt") + 1)
                dve.wait_ge(s_m1_in[k], c.get("kt", 2) * 16 + 16)
                dve.tensor_tensor(grp[:, k, :], grp[:, k, :], m1[:, k, :], ALU.add).then_inc(s_prod, 1)

            mix(merge, xres)

            dve.wait_ge(s_ms, KT)
            for d, v in zip(halves(rb[:]), pieces(0)):
                last = dve.tensor_scalar(d, v, 1.0, EPS, ALU.mult, ALU.add)
            last.then_inc(s_r0, 1)
            dve.wait_ge(s_r1, 1)
            dve.reciprocal(rb[:], rb[:]).then_inc(s_r2, 1)
            dve.wait_ge(s_r2, 1)

            def h2_lo_part(kt):
                dve.wait_ge(s_hn_hi, kt + 1)
                dve.tensor_tensor(h2_lo[:, kt, :], hn[:, kt % 2, :], h2_hi[:, kt, :].bitcast(F32),
                                  ALU.subtract).then_inc(s_h2, 1)

            for kt in range(KT):
                if kt >= 2:
                    dve.wait_ge(s_h2, kt - 1)
                dve.scalar_tensor_tensor(hn[:, kt % 2, :], xres[:, kt, :], ffn_c[:, FT + kt:FT + kt + 1], rb[:],
                                         ALU.mult, ALU.mult).then_inc(s_hn, 1)
                if kt >= 1:
                    h2_lo_part(kt - 1)
            h2_lo_part(KT - 1)

            def up_gate(k):
                f = c.get("f")
                at = bass.ds(f, 1)
                dve.wait_ge(s_c0, f + 1)
                cv = conv[:, k, 2:EXT]
                dve.scalar_tensor_tensor(cv, a_ext[:, k, 1:EXT - 1], conv_w[:, 1, at], cv, ALU.mult, ALU.add).then_inc(s_c1, 1)
                dve.wait_ge(s_c1, f + 1)
                dve.scalar_tensor_tensor(cv, a_ext[:, k, 0:EXT - 2], conv_w[:, 0, at], cv, ALU.mult, ALU.add).then_inc(s_conv, 1)

            def up_value(k):
                f, s = c.get("f"), c.slot("tile")
                dve.wait_ge(s_gelu, f + 1)
                dve.wait_ge(s_tile, c.get("tile") + 1)
                p0, p1 = pieces(s)
                g = grp[:, k, :]
                dve.tensor_tensor(g[:, 0:2 * NB].rearrange("p (b n) -> p b n", b=2), p0,
                                  conv[:, k, 2:2 + 2 * NB].rearrange("p (b n) -> p b n", b=2), ALU.mult)
                dve.tensor_tensor(g[:, 2 * NB:SEQ], p1[:, 0:SEQ - 2 * NB], conv[:, k, 2 + 2 * NB:2 + SEQ], ALU.mult)
                dve.tensor_tensor(g[:, SEQ:T], p1[:, SEQ - 2 * NB:], conv[:, k, SAMP:EXT],
                                  ALU.mult).then_inc(s_freed["freed", "dve", s], 1)
                dve.tensor_copy(spare[:, 3:4], half_neg[:]).then_inc(s_prod, 1)

            dve.wait_ge(s_zext, 1)
            pro, body, reps, epi = FFN
            for k in range(2):
                split_lo()
                up_gate(k)
                c.block("act")
                split_lo()
                up_value(k)
                c.block("dve")
                c.add("f")
            with c.loop(dve, reps, body, g=1, f=2):
                for k in range(2):
                    split_lo()
                    if k == 0:
                        group_lo(c.get("g"))
                    up_gate(k)
                    c.block("act")
                    split_lo()
                    up_value(k)
                    c.block("dve")
                    split_lo()
                    add_group(xres, k)
                    c.add("f")
                c.add("g")
            split_lo()
            group_lo(c.get("g"))
            add_group(xres, 0)
            add_group(xres, 1)

            dve.wait_ge(s_fin_g, 16)
            for n in range(NT):
                r = rows_of(n)
                dve.wait_ge(s_yr, n + 1)
                if n >= 2:
                    dve.wait_ge(s_y_out[n % 2], 16 * (n // 2))
                dve.scalar_tensor_tensor(y_sb[0:r, n % 2, :].rearrange("p (b c) -> p b c", b=2), pset[n % 2][0:r, 0:2, :],
                                         stat_y[0:r, 2, n:n + 1], fin_g[0:r, :].rearrange("p (b c) -> p b c", b=2),
                                         ALU.mult, ALU.mult).then_inc(s_y, 1)

        @block.tensor
        def _(pe):
            def products(out, lhs, rhs, first=True, last=True):
                for n, (a, b) in enumerate(((0, 0), (0, 1), (1, 0))):
                    mm = pe.matmul(out, lhs[a], rhs[b], start=first and n == 0, stop=last and n == 2)
                return mm

            def wide_tile(w, n, pair, bank):
                r = rows_of(n)
                pe.wait_ge(s_vt_free, NT * w + n + 1)
                for kt in range(KT):
                    last = products(bank[0:r, 0:256], [h[:, kt, n * P:n * P + r] for h in (h_hi, h_lo)],
                                    [v[:, kt, :] for v in pair], kt == 0, kt == KT - 1)
                last.then_inc(s_vt, 1)

            pe.wait_ge(s_ident, 1)
            for n in range(NT + 2):
                if n < NT:
                    r = rows_of(n)
                    pe.wait_ge(s_xn, n + 1)
                    if n >= 2:
                        pe.wait_ge(s_h, n - 1)
                    for kt in range(KT):
                        last = pe.transpose(pset[n % 2][:, kt // 4, kt % 4 * P:kt % 4 * P + r],
                                            xn[0:r, n % 2, kt * P:kt * P + P], ident[0:r, 0:r])
                    last.then_inc(s_xnt, 1)
                if n == 2:
                    pe.wait_ge(s_wide, 1)
                if n >= 2:
                    pe.wait_ge(s_h, n - 1)
                    wide_tile(0, n - 2, (wide_hi[:, 0], wide_lo[:, 0]), v_bank(n - 2))
            pe.wait_ge(s_tab_in, 16 * 5)
            for g in range(KT):
                pe.transpose(pset[0][:, g // 4, g % 4 * P:g % 4 * P + P], ws_raw[:, g, :], ident[:])
            pe.transpose(pset[1][:, 0, 0:5 * FT], tab_rows[0:5 * FT, 0, :], ident[0:5 * FT, 0:5 * FT])
            pe.transpose(pset[1][:, 0, P:P + FT + KT], tab_rows[0:FT + KT, 1, :], ident[0:FT + KT, 0:FT + KT]).then_inc(s_tab_t, 1)
            for w in range(1, 4):
                pe.wait_ge(s_wide, w + 1)
                for n in range(NT):
                    wide_tile(w, n, (wide_hi[:, w % 2], wide_lo[:, w % 2]), v_bank(n))
            pe.wait_ge(s_ws_t, 1)

            c = Count()
            TB = [(b, b * NB, min(T, b * NB + NB)) for b in range(3)]
            PASSES = ((0, 0), (0, 1), (1, 0))
            w_pair = (w_hi, w_lo)

            def set_free():
                s = c.slot("tile")
                for e in ("act", "dve"):
                    key = ("freed", e, s)
                    pe.wait_ge(s_freed[key], c.get(key) + 1)
                return s

            def project(kind, x_pair, ready=None):
                pe.wait_ge(s_w, c.get("block") + 1)
                ws, s = c.slot(), set_free()
                for kt in range(KT):
                    if ready is not None:
                        pe.wait_ge(ready, kt + 1)
                    for n, (a, b) in enumerate(PASSES):
                        for blk, t0, t1 in TB:
                            last = pe.matmul(pset[s][:, blk, 0:t1 - t0], w_pair[a][:, ws, kt * P:kt * P + P],
                                             x_pair[b][:, kt, t0:t1], start=kt == 0 and n == 0,
                                             stop=kt == KT - 1 and n == 2)
                last.then_inc(s_tile, 1)
                c.block(kind)

            def group(ready, value):
                pe.wait_ge(s_w, c.get("block") + 1)
                pe.wait_ge(ready, value)
                ws = c.slot()
                for q in range(4):
                    s = set_free()
                    for k in range(2):
                        for n, (a, b) in enumerate(PASSES):
                            for blk, t0, t1 in TB:
                                last = pe.matmul(pset[s][:, blk, 0:t1 - t0],
                                                 w_pair[a][:, ws, 512 * k + P * q:512 * k + P * q + P],
                                                 (grp_hi, grp_lo)[b][:, k, t0:t1], start=k == 0 and n == 0,
                                                 stop=k == 1 and n == 2)
                    last.then_inc(s_tile, 1)
                    c.tile("group")
                c.add("block")

            def mix(between=None, early=0):
                pro, body, reps, epi = MIX
                for k in range(2):
                    if between and k == 1:
                        pe.wait_ge(s_vt_free, 4 * NT + 3)
                    project(pro[k], (h_hi, h_lo))
                if between:
                    between()
                with c.loop(pe, reps, body, g=1):
                    for k in range(2):
                        project("act", (h_hi, h_lo))
                        group(s_grp, c.get("g") + 1)
                    c.add("g")
                for _ in range(early):
                    project("act", (h_hi, h_lo))
                for b in range(2):
                    group(s_grp, c.get("g") + 1)
                c.add("g")

            def spatial():
                pe.wait_ge(s_ws, 1)
                for n in range(NT):
                    r, dst = rows_of(n), (pex, *pset)[n % 3]
                    if n in (1, 2):
                        key = ("freed", "act", n - 1)
                        pe.wait_ge(s_freed[key], c.get(key) + 1)
                    pe.wait_ge(s_vn, n + 1)
                    if n >= 3:
                        pe.wait_ge(s_s, n - 2)
                    for g in range(KT):
                        last = pe.matmul(dst[:, g // 4, g % 4 * P:g % 4 * P + r], gs[0:r, n, g * P:g * P + P],
                                         ws_t[0:r, g, 0:r], start=True, stop=True)
                    last.then_inc(s_mixed, 1)
                pe.wait_ge(s_s, NT - 1)

            mix(between=spatial, early=2)
            with c.loop(pe, GATE[2], GATE[1]):
                for k in range(2):
                    project("act", (h_hi, h_lo))
            for k in range(2):
                project("act", (h_hi, h_lo))

            key = ("freed", "act", 0)
            pe.wait_ge(s_freed[key], c.get(key) + 1)

            def transpose_k(n):
                r = rows_of(n) if n < NT else CACHE
                if n < NT:
                    pe.wait_ge(s_vt_free, 4 * NT + n + 1 + 3)
                else:
                    pe.wait_ge(s_cache, 32)
                if n >= 2:
                    pe.wait_ge(s_kt, n - 1)
                for p in range(2):
                    last = pe.transpose(pex[:, n % 2, p * P:p * P + r],
                                        k_tok[0:r, n % 2 if n < NT else 2, p * P:p * P + P], ident[0:r, 0:r])
                last.then_inc(s_ktr, 1)

            pe.wait_ge(s_wide, 5)
            for n in range(NT):
                wide_tile(4, n, [v[:] for v in k_pair], pset[0][:, n % 3])
                if n:
                    transpose_k(n - 1)
            pe.wait_ge(s_wide, 6)
            for n in range(NT):
                wide_tile(5, n, [v[:] for v in v_pair], pset[0][:, n % 3])
                if n < 2:
                    transpose_k(NT - 1 + n)
            pe.wait_ge(s_vt_free, 6 * NT + 3)
            pe.wait_ge(s_kt, NT + 1)

            with c.loop(pe, ATT[2], ATT[1], att=NT) as (pair, half):
                for k in range(2):
                    project("act", (h_hi, h_lo))
                for s in range(2):
                    key = ("freed", "act", s)
                    pe.wait_ge(s_freed[key], c.get(key) + 1)
                pe.wait_ge(s_now, pair * 3 + 3)
                for step in range(NT + 3):
                    if step < NT:
                        n, q0 = step, queries_of(step)[0]
                        k0, w, _ = keys_of(n)
                        dst = pex if n % 2 == 0 else pset[1]
                        if n >= 2:
                            pe.wait_ge(s_smax, c.get("att") + (n - 1))
                        for e in range(4):
                            h, k = e // 2, e % 2
                            last = pe.matmul(dst[:, h, 256 * k:256 * k + w],
                                             grp[64 * h:64 * h + 64, k, q0:q0 + P],
                                             k_now[64 * h:64 * h + 64, k0:k0 + w], start=True, stop=True)
                        last.then_inc(s_sc, 1)
                    if step >= 3:
                        n = step - 3
                        pe.wait_ge(s_pt, c.get("att") + n + 1)
                        if n >= 2:
                            pe.wait_ge(s_b, c.get("att") + (n - 1))
                        tiles = key_tiles(n)
                        for h in range(2):
                            for j, (slot, rows) in enumerate(tiles):
                                last = pe.matmul(
                                    pset[n % 2][64 * h:64 * h + 64, 2, 0:256].rearrange("p (k q) -> p k q", k=2)[:, :, :],
                                    v_now[0:rows, slot, 64 * h:64 * h + 64],
                                    pt_sb[0:rows, j, 2 * h:2 * h + 2, :],
                                    start=j == 0, stop=j == len(tiles) - 1)
                        last.then_inc(s_o, 1)
                    if 2 <= step <= NT + 1:
                        n = step - 2
                        pe.wait_ge(s_p, c.get("att") + n + 1)
                        for j, (_, rows) in enumerate(key_tiles(n)):
                            for e in range(4):
                                last = pe.transpose(pset[0][0:rows, j, e * P:e * P + P],
                                                    sc_sb[:, n % 3, e, j * P:j * P + rows], ident[:])
                        last.then_inc(s_ptr, 1)
                c.add("att", NT)
                for b in range(2):
                    group(s_b, c.get("att"))

            for s in range(2):
                key = ("freed", "dve", s)
                pe.wait_ge(s_freed[key], c.get(key) + 1)
            for n in range(NT):
                r = rows_of(n)
                pe.wait_ge(s_x2_in[n % 2], 16 * (n // 2 + 1))
                if n >= 2:
                    pe.wait_ge(s_x2, n - 1)
                for kt in range(KT):
                    last = pe.transpose(pset[n % 2][:, kt // 4, kt % 4 * P:kt % 4 * P + r],
                                        xt2[0:r, n % 2, kt * P:kt * P + P], ident[0:r, 0:r])
                last.then_inc(s_x2t, 1)
            pe.wait_ge(s_x2, NT)
            mix()

            key = ("freed", "dve", 0)
            pe.wait_ge(s_freed[key], c.get(key) + 1)
            for kt in range(KT):
                pe.wait_ge(s_sq2, kt + 1)
                for blk, t0, t1 in TB:
                    last = pe.matmul(pset[0][:, blk, 0:t1 - t0], mean_mat[:], sq[:, kt, t0:t1],
                                     start=kt == 0, stop=kt == KT - 1)
                last.then_inc(s_ms, 1)

            pro, body, reps, epi = FFN
            for n, kind in enumerate(pro):
                project(kind, (h2_hi, h2_lo), s_h2 if n == 0 else None)
            with c.loop(pe, reps, body, g=1):
                for kind in body:
                    if kind == "group":
                        group(s_grp, c.get("g") + 1)
                    else:
                        project(kind, (h2_hi, h2_lo))
                c.add("g")
            for b in range(2):
                group(s_grp, c.get("g") + 1)

            pe.wait_ge(s_tail, FT)
            for q in range(2):
                last = pe.transpose(pex[0:2 * FT, 0, q * P:q * P + P], conv_out[:, q].rearrange("p i f -> p (i f)"), ident[:])
            last.then_inc(s_tail_t, 1)
            for s in range(2):
                key = ("freed", "dve", s)
                pe.wait_ge(s_freed[key], c.get(key) + 1)
            for n in range(NT):
                r = rows_of(n)
                if n >= 2:
                    pe.wait_ge(s_y, n - 1)
                for kt in range(KT):
                    last = pe.transpose(pset[n % 2][0:r, kt // 4, kt % 4 * P:kt % 4 * P + P],
                                        xres[:, kt, n * P:n * P + r], ident[:])
                last.then_inc(s_yt, 1)


_INS = ["x_prompt", "x_sample", "cache_k", "cache_v", "cache_conv", "ln_mix_g", "w_in", "ln_v_g", "ln_v_b", "w_s",
        "b_s", "attn_sinks", "w_pa", "w_pb", "w_o", "ln_ffn_g", "w_up", "w_conv", "b_conv", "w_down", "ln_final_g"]
_OUTS = [(1, SEQ, D), (1, DEC, D), (1, 1, 128, KVH, HD), (1, 1, 128, KVH, HD), (1, 1, 2, FF),
         (1, 1, DEC, KVH, HD), (1, 1, DEC, KVH, HD), (1, 1, 2, FF), (1, 1, DEC, D)]


def kernel(**inputs):
    import numpy as _np
    import concourse.bacc as _bacc
    from concourse import mybir as _mybir
    from concourse.bass_utils import run_bass_kernel_spmd as _run

    nc = _bacc.Bacc("TRN2", target_bir_lowering=False, num_devices=1)
    arrays, args = {}, []
    for name in _INS:
        a = _np.ascontiguousarray(inputs[name])
        arrays[f"in_{name}_dram"] = a
        args.append(nc.dram_tensor(f"in_{name}_dram", a.shape, _mybir.dt.from_np(a.dtype), kind="ExternalInput").ap())
    for i, shape in enumerate(_OUTS):
        args.append(nc.dram_tensor(f"out_{i}_dram", shape, _mybir.dt.float32, kind="ExternalOutput").ap())
    args.append(nc.dram_tensor("m1_spill", (KT, P, T), _mybir.dt.float32, kind="Internal").ap())
    program(nc, *args)
    r = _run(nc, [arrays], core_ids=[0])
    return tuple(r.results[0][f"out_{i}_dram"] for i in range(len(_OUTS)))
```

```python
from contextlib import ExitStack, contextmanager

import concourse.bass as bass
from concourse import mybir

F32 = mybir.dt.float32
F32R = mybir.dt.float32r
ALU = mybir.AluOpType
ACT = mybir.ActivationFunctionType

P = 128
D = 1024
KT = D // P
SEQ, DEC = 1024, 64
T = SEQ + DEC
NT = SEQ // P + 1
CACHE = 128
HEADS, KVH, HD = 16, 4, 64
FF = 2816
FT = FF // P
EPS = 1e-6
FFN_GROUP = 8
FAR = 2.56e32
NB = 364
U0, VG0, Q0, K0, GA0, GB0 = 0, 1024, 2048, 3072, 3584, 4608
EXT = T + 4
SAMP = SEQ + 4


ATT_TILE = 48


def rows_of(n):
    return P if n < NT - 1 else DEC


def keys_of(n):
    if n == 0:
        return 0, P, P
    return ((n - 1) * P, 2 * P, 0) if n < NT - 1 else (SEQ, CACHE + DEC, P - DEC)


def queries_of(n):
    return (n * P, 0) if n < NT - 1 else (T - P, P - DEC)


def key_tiles(n):
    if n == 0:
        return [(0, P)]
    return [(n - 1, P), (n, P)] if n < NT - 1 else [(NT - 1, CACHE), (NT, DEC)]


MIX = (["act", "act"], ["act", "group", "act", "group"], 3, ["group", "group"])
GATE = (["act", "act"], ["act", "act"], KT // 2 - 2, ["act", "act"])
ATT = ([], ["act", "act", "group", "group"], (2, 2), [])
FFN = (["dve"] * 4, ["dve", "dve", "group"] * 2, FT // 2 - 1,
       ["group", "group"])


class Count:

    def __init__(self):
        self.v, self.rate, self.i = {}, {}, 0

    def get(self, key, half=1):
        r = self.rate.get(key, 0) // half
        v = self.v.get(key, 0) // half
        return v + self.i * r if r else v

    def add(self, key, n=1):
        self.v[key] = self.v.get(key, 0) + n

    def slot(self, key="block"):
        return self.v.get(key, 0) % 2

    def block(self, kind):
        for _ in range(4 if kind == "group" else 1):
            self.tile(kind)
        self.add("block")

    def tile(self, kind):
        self.add(("freed", "act" if kind == "act" else "dve", self.slot("tile")))
        self.add("tile")

    @contextmanager
    def loop(self, eng, reps, kinds, **more):
        before = dict(self.v)
        dry = Count()
        for kind in kinds:
            dry.block(kind)
        for k, n in more.items():
            dry.add(k, n)
        assert not (dry.v.get("block", 0) % 2 or dry.v.get("tile", 0) % 2 or self.slot() or self.slot("tile"))
        self.rate = dry.v
        if isinstance(reps, tuple):
            with eng.Fori(0, reps[0]) as a:
                with eng.Fori(0, reps[1]) as b:
                    self.i = a * reps[1] + b
                    yield a, b
            reps = reps[0] * reps[1]
        else:
            with eng.Fori(0, reps) as i:
                self.i = i
                yield i
        for k, n in dry.v.items():
            assert self.v.get(k, 0) - before.get(k, 0) == n, (k, n)
            self.v[k] = before.get(k, 0) + n * reps
        self.rate, self.i = {}, 0


def program(nc, x_prompt, x_sample, cache_k, cache_v, cache_conv, ln_mix_g, w_in, ln_v_g, ln_v_b, w_s, b_s,
            attn_sinks, w_pa, w_pb, w_o, ln_ffn_g, w_up, w_conv, b_conv, w_down, ln_final_g,
            y_prompt, y_sample, new_k_prompt, new_v_prompt, new_conv_prompt, new_k_sample, new_v_sample,
            new_conv_sample, new_gmlp_v_sample, m1_spill):
    with ExitStack() as ctx:
        def sem(name):
            return ctx.enter_context(nc.semaphore(name))

        cursor = (nc.sbuf_base + 63) // 64 * 64

        def region(size):
            nonlocal cursor
            at = cursor
            cursor += (size + 63) // 64 * 64
            assert cursor <= nc.sbuf_usable_end, cursor
            return [at, at + size]

        def put(reg, name, shape, dt=F32, at=None):
            size = 4
            for s in shape[1:]:
                size *= s
            start = reg[0] + (reg[2] if len(reg) > 2 else 0) if at is None else reg[0] + at
            t = nc.alloc_sbuf_tensor_at(name, shape, dt, offset=start)
            assert start + size <= reg[1], (name, start + size - reg[1])
            if at is None:
                del reg[2:]
                reg.append(start - reg[0] + (size + 31) // 32 * 32)
            return t

        def again(reg):
            return reg[:2]

        r_h = region(2 * KT * T * 4)
        r_w = region(2 * 1024 * 4 * 3)
        r_s = region(NT * D * 4)
        r_a = region(KT * T * 4)
        r_g = region(3 * 2 * T * 4)
        r_t = region(16384)
        r_c = region(4416)

        h_hi = put(r_h, "h_hi", [P, KT, T], F32R)
        h_lo = put(r_h, "h_lo", [P, KT, T], F32R)
        h2_hi, h2_lo = h_hi, h_lo

        ident = put(r_c, "ident", [P, P])
        mean_col = put(r_c, "mean_col", [P, 1])
        stat = put(r_c, "stat", [P, 3, 16])
        stat_y = put(r_c, "stat_y", [P, 3, 16])
        half_neg = put(r_c, "half_neg", [P, 1])
        ln_stats = put(r_c, "ln_stats", [P, 2, 2, 6])
        ln_mv = put(r_c, "ln_mv", [P, NT, 2])
        ln_rstd = put(r_c, "ln_rstd", [P, NT])
        slopes = put(r_c, "slopes", [P, HEADS])
        sinks = put(r_c, "sinks", [P, HEADS])
        sink_now = put(r_c, "sink_now", [P, 4])
        att_stat = put(r_c, "att_stat", [P, 2, 8, 4])
        conv_w = put(r_c, "conv_w", [P, 5, FT])
        ffn_c = put(r_c, "ffn_c", [P, FT + KT])
        conv_out = put(r_c, "conv_out", [P, 2, 2, FT])
        spare = put(r_c, "spare", [P, 4])

        r_w0 = again(r_w)
        xt_a = put(r_w0, "xt_a", [P, 2, D])
        xn = put(r_w0, "xn", [P, 2, D])
        mix_g = put(r_w0, "mix_g", [P, D])
        junk = put(r_w0, "junk", [P, D])
        raw = put(r_w, "raw", [P, 2, 1024])
        w_hi = put(r_w, "w_hi", [P, 2, 1024], F32R)
        w_lo = put(r_w, "w_lo", [P, 2, 1024], F32R)

        gs = put(r_s, "gs", [P, NT, D])
        r_v = [r_a[0], r_t[1]]
        wraw = put(r_v, "wraw", [P, KT, 256])
        wide_hi = put(r_v, "wide_hi", [P, 2, KT, 256], F32R)
        wide_lo = put(r_v, "wide_lo", [P, 2, KT, 256], F32R)
        ws_raw = put(r_v, "ws_raw", [P, KT, P])
        lnv_g = put(r_v, "lnv_g", [P, D])
        lnv_b = put(r_v, "lnv_b", [P, D])
        ws_t = put(r_v, "ws_t", [P, KT, P])
        bs = put(r_v, "bs", [P, KT, P])
        tab_rows = put(r_v, "tab_rows", [P, 2, P])
        xt_b = put(r_v, "xt_b", [P, 2, D])
        r_kw = again(r_g)
        kv_raw = put(r_kw, "kv_raw", [P, KT, 256])
        k_pair = (put(r_kw, "k_hi", [P, KT, 256], F32R), put(r_kw, "k_lo", [P, KT, 256], F32R))
        r_vw = again(r_a)
        v_pair = (put(r_vw, "v_hi", [P, KT, 256], F32R), put(r_vw, "v_lo", [P, KT, 256], F32R))

        acc = put(r_a, "acc", [P, KT, T])
        grp = put(r_g, "grp", [P, 2, T])
        grp_hi = put(r_g, "grp_hi", [P, 2, T], F32R)
        grp_lo = put(r_g, "grp_lo", [P, 2, T], F32R)
        xt2 = put(again(r_g), "xt2", [P, 2, D], at=2 * T * 4)
        gate = put(r_t, "gate", [P, 2, T])
        m1 = put(again(r_t), "m1", [P, 2, T])
        r_k = again(r_s)
        k_t = put(r_k, "k_t", [P, 2, T + CACHE])
        v_tok = put(r_k, "v_tok", [P, NT + 1, 256])
        k_now = put(r_k, "k_now", [P, T + CACHE])
        v_now = put(r_k, "v_now", [P, NT + 1, P])
        bias_now = put(r_k, "bias_now", [P, 4, 256])
        dist = put(r_k, "dist", [P, 256])
        r_t2 = again(r_t)
        sc_sb = put(r_t2, "sc_sb", [P, 3, 4, 256])
        pt_sb = put(r_t2, "pt_sb", [P, 2, 4, P])
        k_tok = put(again(r_t), "k_tok", [P, 3, 256], at=2 * T * 4)
        xres = put(again(r_s), "xres", [P, KT, T])
        r_f = again(r_a)
        a_ext = put(r_f, "a_ext", [P, 2, EXT])
        conv = put(r_f, "conv", [P, 2, EXT])
        sq = put(r_f, "sq", [P, 2, T])
        r_n = again(r_t)
        rb = put(r_n, "rb", [P, T])
        ssum = put(r_n, "ssum", [P, T], at=2 * T * 4)
        r_y = again(r_t)
        fin_g = put(r_y, "fin_g", [P, D], at=T * 4)
        r_y2 = again(r_a)
        y_sb = put(r_y2, "y_sb", [P, 4, D])
        y_junk = put(r_y2, "y_junk", [P, D])
        conv_rows = put(r_y2, "conv_rows", [2 * FT, 2, P])

        pset = [ctx.enter_context(nc.psum_tensor(f"pset{i}", [P, 3, 512], F32)) for i in range(2)]
        pex = ctx.enter_context(nc.psum_tensor("pex", [P, 2, 512], F32))

        s_ident = sem("s_ident")
        s_tab_in = sem("s_tab_in")
        s_row_in = sem("s_row_in")
        s_tab_t = sem("s_tab_t")
        s_ws_t = sem("s_ws_t")
        s_ws = sem("s_ws")
        s_dist = sem("s_dist")
        s_distf = sem("s_distf")
        s_x_in = [sem(f"s_x_in{i}") for i in range(4)]
        s_sq = sem("s_sq")
        s_var = sem("s_var")
        s_rstd = sem("s_rstd")
        s_xn = sem("s_xn")
        s_xnt = sem("s_xnt")
        s_h_hi = sem("s_h_hi")
        s_h = sem("s_h")
        s_wide_in = sem("s_wide_in")
        s_kv_w = sem("s_kv_w")
        s_wide_hi = sem("s_wide_hi")
        s_wide = sem("s_wide")
        s_vt = sem("s_vt")
        s_vt_free = sem("s_vt_free")
        s_ln = sem("s_ln")
        s_ln_mv = sem("s_ln_mv")
        s_ln_v = sem("s_ln_v")
        s_ln_r = sem("s_ln_r")
        s_ln_a = sem("s_ln_a")
        s_vn = sem("s_vn")
        s_mixed = sem("s_mixed")
        s_s = sem("s_s")
        s_out = sem("s_out")
        s_vnout = sem("s_vnout")
        s_load = [sem(f"s_load{i}") for i in range(2)]
        s_w_hi = sem("s_w_hi")
        s_w = sem("s_w")
        s_tile = sem("s_tile")
        s_freed = {("freed", e, s): sem(f"s_freed_{e}{s}") for e in ("act", "dve") for s in range(2)}
        s_zero = sem("s_zero")
        s_prod = sem("s_prod")
        s_grp_hi = sem("s_grp_hi")
        s_grp = sem("s_grp")
        s_m1 = sem("s_m1")
        s_spill = sem("s_spill")
        s_ktr = sem("s_ktr")
        s_kt = sem("s_kt")
        s_cache = sem("s_cache")
        s_kv_out = sem("s_kv_out")
        s_now = sem("s_now")
        s_bias = sem("s_bias")
        s_sc = sem("s_sc")
        s_smax = sem("s_smax")
        s_neg = sem("s_neg")
        s_exp = sem("s_exp")
        s_den = sem("s_den")
        s_p = sem("s_p")
        s_ptr = sem("s_ptr")
        s_pt = sem("s_pt")
        s_o = sem("s_o")
        s_b_hi = sem("s_b_hi")
        s_b = sem("s_b")
        s_x2_in = [sem(f"s_x2_in{i}") for i in range(2)]
        s_x2t = sem("s_x2t")
        s_x2 = sem("s_x2")
        s_m1_in = [sem(f"s_m1_in{i}") for i in range(2)]
        s_gb = sem("s_gb")
        s_sq2 = sem("s_sq2")
        s_ssum = sem("s_ssum")
        s_ms = sem("s_ms")
        s_r0 = sem("s_r0")
        s_r1 = sem("s_r1")
        s_r2 = sem("s_r2")
        s_rb = sem("s_rb")
        s_h2_hi = sem("s_h2_hi")
        s_h2 = sem("s_h2")
        s_up = sem("s_up")
        s_gr = sem("s_gr")
        s_zext = sem("s_zext")
        s_hist = sem("s_hist")
        s_c0 = sem("s_c0")
        s_c1 = sem("s_c1")
        s_conv = sem("s_conv")
        s_gelu = sem("s_gelu")
        s_tail = sem("s_tail")
        s_tail_t = sem("s_tail_t")
        s_tail_r = sem("s_tail_r")
        s_yt = sem("s_yt")
        s_ysq = sem("s_ysq")
        s_yv = sem("s_yv")
        s_yr = sem("s_yr")
        s_y = sem("s_y")
        s_y_out = [sem(f"s_y_out{i}") for i in range(4)]
        s_fin_g = sem("s_fin_g")

        def k_tiles(w):
            return w[0].rearrange("(k p) c -> p k c", p=P)

        w_in_v, w_up_v = k_tiles(w_in), k_tiles(w_up)
        w_pb_v = w_pb[0].rearrange("(h r) c -> r h c", r=HD)

        def token_rows(n):
            return x_prompt[0, n * P:(n + 1) * P, :] if n < NT - 1 else x_sample[0]

        def x_slot(n):
            return (xt_a, xt_b)[n % 4 // 2][0:rows_of(n), n % 2, :]

        def v_bank(n):
            return (pex[:, 0], pex[:, 1], pset[1][:, 2])[n % 3]

        def halves(t):
            return t[:, 0:2 * NB].rearrange("p (b n) -> p b n", b=2), t[:, 2 * NB:T]

        def pieces(s):
            return pset[s][:, 0:2, 0:NB], pset[s][:, 2, 0:T - 2 * NB]

        def row128(v):
            return v.rearrange("(a n) -> a n", a=1).broadcast_to([P, v.shape[0]])

        block = ctx.enter_context(nc.Block())

        @block.sync
        def _(sp):
            def wide(w, c0):
                if w:
                    sp.wait_ge(s_wide, w)
                sp.dma_start(wraw[:], w_in_v[:, :, bass.ds(c0, 256)]).then_inc(s_wide_in, 16)

            def load_x(n):
                if n >= 4:
                    sp.wait_ge(s_xn, n - 3)
                sp.dma_start(x_slot(n), token_rows(n)).then_inc(s_x_in[n % 4], 16)

            load_x(0)
            sp.dma_start(mix_g[:], row128(ln_mix_g[0])).then_inc(s_row_in, 16)
            load_x(1)
            load_x(2)
            wide(0, VG0)
            for n in range(3, NT):
                load_x(n)
            sp.dma_start(tab_rows[0:3 * FT, 0, :], w_conv[0].rearrange("i (f p) -> (i f) p", p=P)).then_inc(s_tab_in, 16)
            sp.dma_start(tab_rows[3 * FT:5 * FT, 0, :], cache_conv[0, 0].rearrange("i (f p) -> (i f) p", p=P)).then_inc(s_tab_in, 16)
            sp.dma_start(tab_rows[0:FT, 1, :], b_conv[0].rearrange("(f p) -> f p", p=P)).then_inc(s_tab_in, 16)
            sp.dma_start(tab_rows[FT:FT + KT, 1, :], ln_ffn_g[0].rearrange("(f p) -> f p", p=P)).then_inc(s_tab_in, 16)
            sp.dma_start(ws_raw[:], w_s[0].rearrange("g t s -> t g s")).then_inc(s_tab_in, 16)
            wide(1, VG0 + 256)
            sp.dma_start(lnv_g[:], row128(ln_v_g[0])).then_inc(s_row_in, 16)
            sp.dma_start(lnv_b[:], row128(ln_v_b[0])).then_inc(s_row_in, 16)
            sp.dma_start(bs[:], b_s.rearrange("a g t -> a (g t)").broadcast_to([P, D])).then_inc(s_row_in, 16)
            sp.dma_start(sinks[:], attn_sinks.broadcast_to([P, HEADS])).then_inc(s_row_in, 16)
            for w in range(2, 4):
                wide(w, VG0 + 256 * w)

            c = Count()

            def load(srcs):
                s = c.slot()
                if c.v.get("block", 0) >= 2 or c.rate:
                    sp.wait_ge(s_w, c.get("block") - 1)
                else:
                    sp.wait_ge(s_h, NT)
                for place, src in srcs:
                    sp.dma_start(place(raw[:, s, :]), src).then_inc(s_load[s], 16)

            def part(h, k):
                return lambda slot: slot[64 * h:64 * h + 64].rearrange("p (k c) -> p k c", k=k)

            def proj(view, c0):
                load([(part(h, KT), view[64 * h:64 * h + 64, :, bass.ds(c0, P)]) for h in range(2)])

            def group(w, j, b):
                view = k_tiles(w)
                load([(part(h, 2), view[64 * h:64 * h + 64, bass.ds(2 * j, 2), 512 * b:512 * b + 512])
                      for h in range(2)])

            def load_m1(m, k):
                if not isinstance(m, int):
                    sp.wait_ge(s_prod, m + (KT - 1))
                sp.dma_start(m1[:, k, :], m1_spill[bass.ds(m, 1)].rearrange("a p t -> (a p) t"))\
                  .then_inc(s_m1_in[k], 16)

            def load_residual():
                sp.wait_ge(s_tile, c.get("tile") - 1)
                for n in range(NT):
                    if n == 2:
                        for k in range(2):
                            load_m1(k, k)
                    if n >= 2:
                        sp.wait_ge(s_x2t, n - 1)
                    sp.dma_start(xt2[0:rows_of(n), n % 2, :], token_rows(n)).then_inc(s_x2_in[n % 2], 16)

            def mix(c0, w, with_m1, early=()):
                pro, body, reps, epi = MIX
                for k in range(2):
                    proj(w_in_v, c0 + P * k)
                    if k == 1 and with_m1:
                        load_residual()
                    c.block(pro[k])
                with c.loop(sp, reps, body) as i:
                    for k in range(2):
                        if with_m1:
                            load_m1(i * 2 + (2 + k), k)
                        proj(w_in_v, i * 256 + (c0 + 256 + P * k))
                        c.block(body[2 * k])
                        group(w, i, k)
                        c.block(body[2 * k + 1])
                for c1 in early:
                    proj(w_in_v, c1)
                    c.block("act")
                for b in range(2):
                    group(w, reps, b)
                    c.block(epi[b])

            mix(U0, w_pa, False, early=(GA0, GA0 + P))
            with c.loop(sp, GATE[2], GATE[1]) as i:
                for k in range(2):
                    proj(w_in_v, i * 256 + (GA0 + P * (2 + k)))
                    c.block("act")
            for k in range(2):
                proj(w_in_v, GA0 + P * (KT - 2 + k))
                c.block("act")
            with c.loop(sp, ATT[2], ATT[1]) as (pair, half):
                for k in range(2):
                    load([(lambda slot, h=h: slot.rearrange("p (k c) -> p k c", k=KT)[:, :, 64 * h:64 * h + 64],
                           w_in_v[:, :, bass.ds(pair * 512 + half * 128 + (Q0 + 256 * h + 64 * k), HD)])
                          for h in range(2)])
                    c.block("act")
                for b in range(2):
                    load([(part(h, 2), w_pb_v[:, bass.ds(pair * 8 + half * 2 + 4 * h, 2), 512 * b:512 * b + 512])
                          for h in range(2)])
                    c.block("group")
            mix(GB0, w_o, True)
            pro, body, reps, epi = FFN
            for k in range(2):
                proj(w_up_v, P * k)
                c.block(pro[0])
                proj(w_up_v, FF + P * k)
                c.block(pro[1])
            with c.loop(sp, reps, body) as i:
                for k in range(2):
                    proj(w_up_v, i * 256 + (256 + P * k))
                    c.block(body[0])
                    proj(w_up_v, i * 256 + (FF + 256 + P * k))
                    c.block(body[1])
                    group(w_down, i, k)
                    c.block(body[2])
            for b in range(2):
                group(w_down, reps, b)
                c.block(epi[b])
            sp.dma_start(fin_g[:], row128(ln_final_g)).then_inc(s_fin_g, 16)
            sp.wait_ge(s_tail_r, 2)
            for q, out in enumerate((new_conv_prompt, new_conv_sample)):
                sp.dma_start(out[0, 0].rearrange("i (f p) -> (i f) p", p=P), conv_rows[:, q, :]).then_inc(s_out, 16)
            for n in range(NT):
                sp.wait_ge(s_y, n + 1)
                dst = y_prompt[0, n * P:(n + 1) * P, :] if n < NT - 1 else y_sample[0]
                sp.dma_start(dst, y_sb[0:rows_of(n), n % 4, :]).then_inc(s_y_out[n % 4], 16)
            sp.wait_ge(s_out, 32)
            for k in range(4):
                sp.wait_ge(s_y_out[k], 16 * len(range(k, NT, 4)))
            sp.wait_ge(s_vnout, 16)
            sp.wait_ge(s_kv_out, 64)
            sp.wait_ge(s_spill, 16 * KT)

        @block.gpsimd
        def _(pool):
            pool.memset(ident[:], 0.0).then_inc(s_zero, 1)
            pool.memset(half_neg[:], -0.5).then_inc(s_zero, 1)
            pool.memset(mean_col[:], 1.0 / D).then_inc(s_zero, 1)
            for i in range(HEADS):
                last = pool.memset(slopes[:, i:i + 1], -2.0 ** (-8.0 * (i + 1) / HEADS))
            last.then_inc(s_zero, 1)
            pool.wait_ge(s_zero, 4)
            pool.affine_select(out=ident[:], in_=ident[:], compare_op=ALU.not_equal, fill=1.0, base=0,
                               pattern=[[-1, P]], channel_multiplier=1).then_inc(s_ident, 1)

            def rstd(n, table, s_in, s_mid, s_end, done):
                r = rows_of(n)
                pool.wait_ge(s_in, n + 1)
                pool.tensor_scalar(table[0:r, 1, n:n + 1], table[0:r, 0, n:n + 1], 1.0 / D, EPS, ALU.mult,
                                   ALU.add).then_inc(s_mid, 1)
                pool.wait_ge(s_mid, n + 1)
                pool.tensor_tensor(table[0:r, 2, n:n + 1], table[0:r, 1, n:n + 1], half_neg[0:r, :],
                                   ALU.pow).then_inc(s_end, 1)

            for n in range(NT):
                rstd(n, stat, s_sq, s_var, s_rstd, n)

            for n in range(NT):
                r = rows_of(n)
                pool.wait_ge(s_ln_mv, n + 1)
                pool.tensor_scalar(ln_rstd[0:r, n:n + 1], ln_mv[0:r, n, 1:2], 1.0, EPS, ALU.mult,
                                   ALU.add).then_inc(s_ln_v, 1)
                pool.wait_ge(s_ln_v, n + 1)
                pool.tensor_tensor(ln_rstd[0:r, n:n + 1], ln_rstd[0:r, n:n + 1], half_neg[0:r, :],
                                   ALU.pow).then_inc(s_ln_r, 1)
            pool.wait_ge(s_tile, 1)
            pool.memset(acc[:], 0.0).then_inc(s_zero, 1)

            pool.wait_ge(s_tile, ATT_TILE - KT + 2)
            pool.wait_ge(s_prod, 2 * 4)
            pool.dma_start(kv_raw[:], w_in_v[:, :, K0:K0 + 256]).then_inc(s_kv_w, 16)
            pool.dma_start(k_tok[:, 2, :], cache_k[0, 0].rearrange("t h d -> t (h d)")).then_inc(s_cache, 16)
            pool.dma_start(v_tok[:, NT - 1, :], cache_v[0, 0].rearrange("t h d -> t (h d)")).then_inc(s_cache, 16)

            for half in range(2):
                with pool.Fori(0, KT // 2) as i:
                    pool.wait_ge(s_m1, i + (3 + half * KT // 2))
                    pool.dma_start(m1_spill[bass.ds(i + half * KT // 2, 1)].rearrange("a p t -> (a p) t"),
                                   acc[:, bass.ds(i + half * KT // 2, 1), :].rearrange("p a t -> p (a t)"))\
                        .then_inc(s_spill, 16)
                pool.wait_ge(s_spill, 16 * (half + 1) * KT // 2)
                if half == 0:
                    pool.wait_ge(s_wide, 5)
                    pool.dma_start(kv_raw[:], w_in_v[:, :, K0 + 256:K0 + 512]).then_inc(s_kv_w, 16)

            pool.wait_ge(s_grp, 2 * 4)
            pool.wait_ge(s_prod, 2 * 4)
            pool.iota(dist[:].bitcast(mybir.dt.int32), [[-1, 256]], base=P, channel_multiplier=1).then_inc(s_dist, 1)
            pool.wait_ge(s_distf, 2)
            pool.affine_select(out=dist[0:64, :], in_=dist[0:64, :], compare_op=ALU.is_ge, fill=FAR, base=191,
                               pattern=[[-1, 256]], channel_multiplier=0).then_inc(s_dist, 1)
            pool.affine_select(out=dist[64:P, :], in_=dist[64:P, :], compare_op=ALU.is_ge, fill=FAR, base=-64,
                               pattern=[[1, 256]], channel_multiplier=0).then_inc(s_dist, 1)
            pool.wait_ge(s_dist, 3)
            pool.wait_ge(s_vt, 6 * NT)
            pool.memset(acc[:], 0.0).then_inc(s_zero, 1)
            pool.wait_ge(s_kt, NT + 1)
            pool.wait_ge(s_vt_free, 6 * NT + 3)
            pool.wait_ge(s_cache, 32)
            with pool.Fori(0, 2) as pair:
                pool.wait_ge(s_tile, pair * 20 + ATT_TILE)
                pool.tensor_copy(k_now[:], k_t[:, bass.ds(pair, 1), :].rearrange("p a c -> p (a c)")).then_inc(s_now, 1)
                pool.tensor_copy(v_now[:, 0:NT, :], v_tok[:, 0:NT, bass.ds(pair * P, P)]).then_inc(s_now, 1)
                pool.tensor_copy(v_now[0:DEC, NT, :], v_tok[0:DEC, NT, bass.ds(pair * P, P)]).then_inc(s_now, 1)

            for kt in range(1, KT):
                pool.wait_ge(s_sq2, kt + 1)
                if kt >= 2:
                    pool.wait_ge(s_ssum, kt - 1)
                pool.tensor_tensor(ssum[:], ssum[:], sq[:, kt % 2, :], ALU.add).then_inc(s_ssum, 1)

            pool.wait_ge(s_h2, KT)
            pool.memset(a_ext[:, :, 0:2], 0.0).then_inc(s_zext, 1)
            pool.wait_ge(s_r0, 1)
            pool.tensor_tensor(stat[:, 2, 0:NT - 1], stat[:, 1, 0:NT - 1], half_neg[:].broadcast_to([P, NT - 1]), ALU.pow)
            pool.tensor_tensor(stat[0:DEC, 2, NT - 1:NT], stat[0:DEC, 1, NT - 1:NT], half_neg[0:DEC, :],
                               ALU.pow).then_inc(s_r1, 1)

            def keep_tail(f, k):
                src = a_ext[:, k, :]
                at = bass.ds(f, 1)
                pool.tensor_copy(conv_out[:, 0, :, at], src[:, SEQ:SEQ + 2].unsqueeze(2))
                pool.tensor_copy(conv_out[:, 1, :, at], src[:, EXT - 2:EXT].unsqueeze(2)).then_inc(s_tail, 1)

            for k in range(2):
                pool.wait_ge(s_c0, k + 1)
                keep_tail(k, k)
            with pool.Fori(0, FFN[2]) as i:
                for k in range(2):
                    pool.wait_ge(s_c0, i * 2 + (k + 3))
                    keep_tail(i * 2 + (k + 2), k)
            for n in range(NT):
                rstd(n, stat_y, s_ysq, s_yv, s_yr, n)

        @block.scalar
        def _(act):
            copy = ACT.Copy
            act.sem_inc(s_freed["freed", "act", 0], 1)
            act.sem_inc(s_freed["freed", "act", 1], 1)
            act.sem_inc(s_vt_free, 3)

            def h_hi_part(n):
                r = rows_of(n)
                act.wait_ge(s_xnt, n + 1)
                for b in range(2):
                    last = act.activation(h_hi[:, 4 * b:4 * b + 4, n * P:n * P + r],
                                          pset[n % 2][:, b, :].rearrange("p (k t) -> p k t", k=4)[:, :, 0:r], copy)
                last.then_inc(s_h_hi, 1)

            def wide_hi_part(w, dst, src=wraw, arrived=s_wide_in, before=0):
                act.wait_ge(arrived, (w - before) * 16 + 16)
                act.activation(dst, src[:], copy).then_inc(s_wide_hi, 1)

            def vg(w, n):
                r = rows_of(n)
                act.wait_ge(s_vt, w * NT + n + 1)
                act.activation(gs[0:r, n, 256 * w:256 * w + 256], v_bank(n)[0:r, 0:256],
                               ACT.Gelu_apprx_tanh).then_inc(s_vt_free, 1)

            for n in range(NT + 3):
                if n < NT:
                    r = rows_of(n)
                    act.wait_ge(s_x_in[n % 4], 16 * (n // 4 + 1))
                    if n >= 1:
                        act.wait_ge(s_sq, n)
                    act.activation(junk[0:r, :], x_slot(n), ACT.Square,
                                   accum_out=stat[0:r, 0, n:n + 1]).then_inc(s_sq, 1)
                if 1 <= n <= NT:
                    h_hi_part(n - 1)
                if n == 2:
                    wide_hi_part(0, wide_hi[:, 0])
                if n == NT - 2:
                    wide_hi_part(1, wide_hi[:, 1])
                if n >= 3:
                    vg(0, n - 3)
            act.wait_ge(s_tab_t, 1)
            act.activation(conv_w[:].rearrange("p i f -> p (i f)"), pset[1][:, 0, 0:5 * FT], copy)
            act.activation(ffn_c[:], pset[1][:, 0, P:P + FT + KT], copy)
            for b in range(2):
                last = act.activation(ws_t[:, 4 * b:4 * b + 4, :], pset[0][:, b, :].rearrange("p (k t) -> p k t", k=4), copy)
            last.then_inc(s_ws_t, 1)

            c = Count()

            def split_hi(ahead=1):
                s = (c.slot() + ahead) % 2
                act.wait_ge(s_load[s], c.get("block", 2) * 32 + ((c.slot() + ahead) // 2 * 32 + 32))
                if c.v.get("tile", 0):
                    act.wait_ge(s_tile, c.get("tile"))
                act.activation(w_hi[:, s, :], raw[:, s, :], copy).then_inc(s_w_hi, 1)

            def group_hi(g):
                act.wait_ge(s_tile, c.get("tile"))
                for k in range(2):
                    act.wait_ge(s_prod, g * 2 + (k + 1))
                    act.activation(grp_hi[:, k, :], grp[:, k, :], copy).then_inc(s_grp_hi, 1)

            def evacuate(dst, func, **kw):
                act.wait_ge(s_tile, c.get("tile") + 1)
                s = c.slot("tile")
                for d, q in zip(halves(dst), pieces(s)):
                    last = act.activation(d, q, func, **kw)
                last.then_inc(s_freed["freed", "act", s], 1)

            def mix(project, between=None, after=None, early=None, first=1, pre=None):
                pro, body, reps, epi = MIX
                for k in range(2):
                    if pre and k == 1:
                        pre(1)
                    if k >= 1 - first:
                        split_hi()
                    if pre and k == 0:
                        pre(0)
                    project(k)
                    c.block(pro[k])
                if between:
                    between()
                with c.loop(act, reps, body, g=1):
                    for k in range(2):
                        split_hi()
                        if k == 0:
                            group_hi(c.get("g"))
                            act.wait_ge(s_grp, c.get("g") * 2 + 2)
                        project(k)
                        c.block("act")
                        split_hi()
                        c.block("group")
                    c.add("g")
                split_hi()
                group_hi(c.get("g"))
                if early:
                    for k in range(2):
                        early(k)
                        c.block("act")
                        split_hi()
                if after:
                    after(0)
                c.block("group")
                c.add("g")
                split_hi()
                if after:
                    after(1)
                c.block("group")

            def values_out():
                act.wait_ge(s_vn, NT)
                act.dma_start(new_gmlp_v_sample[0, 0], gs[0:DEC, NT - 1, :]).then_inc(s_vnout, 16)

            for w in range(1, 4):
                if w < 3:
                    wide_hi_part(w + 1, wide_hi[:, (w + 1) % 2])
                else:
                    split_hi(0)
                    split_hi(1)
                for n in range(NT):
                    vg(w, n)
            c.v["m"] = 0

            def gate_a(k):
                act.wait_ge(s_m1, c.get("m") + 1)
                evacuate(gate[:, k, :], ACT.Sigmoid)
                c.add("m")

            mix(lambda k: evacuate(grp[:, k, :], ACT.Gelu_apprx_tanh), between=values_out, early=gate_a, first=0)

            with c.loop(act, GATE[2], GATE[1], m=2):
                for k in range(2):
                    split_hi()
                    gate_a(k)
                    c.block("act")
            wide_hi_part(4, k_pair[0][:], kv_raw, s_kv_w, 4)
            for k in range(2):
                split_hi()
                gate_a(k)
                c.block("act")
                if k == 0:
                    wide_hi_part(5, v_pair[0][:], kv_raw, s_kv_w, 4)

            for n in range(NT):
                r = rows_of(n)
                act.wait_ge(s_vt, 4 * NT + n + 1)
                if n >= 2:
                    act.wait_ge(s_ktr, n - 1)
                act.activation(k_tok[0:r, n % 2, :], pset[0][0:r, n % 3, 0:256], copy).then_inc(s_vt_free, 1)
            for n in range(NT):
                r, slot = rows_of(n), n if n < NT - 1 else NT
                act.wait_ge(s_vt, 5 * NT + n + 1)
                act.activation(v_tok[0:r, slot, :], pset[0][0:r, n % 3, 0:256], copy).then_inc(s_vt_free, 1)
            act.wait_ge(s_vt_free, 6 * NT + 3)
            for dst, src in ((new_k_prompt, k_tok[:, (NT - 2) % 2, :]), (new_k_sample, k_tok[0:DEC, (NT - 1) % 2, :]),
                             (new_v_prompt, v_tok[:, NT - 2, :]), (new_v_sample, v_tok[0:DEC, NT, :])):
                act.dma_start(dst[0, 0].rearrange("t h d -> t (h d)"), src).then_inc(s_kv_out, 16)

            with c.loop(act, ATT[2], ATT[1], att=NT):
                for k in range(2):
                    split_hi()
                    evacuate(grp[:, k, :], copy, scale=HD ** -0.5)
                    c.block("act")
                for step in range(NT + 3):
                    if step >= 3:
                        n, r, q0 = step - 3, rows_of(step - 3), queries_of(step - 3)[1]
                        act.wait_ge(s_o, c.get("att") + n + 1)
                        act.activation(grp_hi[:, :, n * P:n * P + r],
                                       pset[n % 2][:, 2, 0:256].rearrange("p (k q) -> p k q", k=2)[:, :, q0:P],
                                       copy).then_inc(s_b_hi, 1)
                    if 2 <= step <= NT + 1:
                        n = step - 2
                        act.wait_ge(s_ptr, c.get("att") + n + 1)
                        for j, (_, rows) in enumerate(key_tiles(n)):
                            last = act.activation(pt_sb[0:rows, j, :, :],
                                                  pex[0:rows, j, :].rearrange("p (e q) -> p e q", e=4), copy)
                        last.then_inc(s_pt, 1)
                    if step < NT:
                        n, a = step, att_stat[:, step % 2]
                        w = keys_of(n)[1]
                        act.wait_ge(s_neg, c.get("att") + n + 1)
                        for e in range(4):
                            act.activation(sc_sb[:, n % 3, e, 0:w], sc_sb[:, n % 3, e, 0:w], ACT.Exp,
                                           bias=a[:, 1, e:e + 1], accum_out=a[:, 3, e:e + 1])
                        act.activation(a[:, 4, :], a[:, 2, :], ACT.Exp).then_inc(s_exp, 1)
                c.add("att", NT)
                for b in range(2):
                    split_hi()
                    c.block("group")

            def residual(k):
                for n in (range(5), range(5, NT))[k]:
                    r = rows_of(n)
                    act.wait_ge(s_x2t, n + 1)
                    for b in range(2):
                        last = act.activation(xres[:, 4 * b:4 * b + 4, n * P:n * P + r],
                                              pex[:, b, :].rearrange("p (k t) -> p k t", k=4)[:, :, 0:r], copy)
                    last.then_inc(s_x2, 1)

            def finished(b):
                for q in range(4):
                    kt, key = 4 * b + q, ("freed", "dve", q % 2)
                    act.wait_ge(s_freed[key], c.get(key) + q // 2 + 2)
                    act.activation(h2_hi[:, kt, :], xres[:, kt, :], copy,
                                   scale=ffn_c[:, FT + kt:FT + kt + 1]).then_inc(s_h2_hi, 1)
                    if kt >= 3:
                        act.wait_ge(s_ssum, kt - 2)
                    act.activation(ssum[:] if kt == 0 else sq[:, kt % 2, :], xres[:, kt, :],
                                   ACT.Square).then_inc(s_sq2, 1)

            mix(lambda k: evacuate(grp[:, k, :], ACT.Sigmoid), after=finished, pre=residual)

            def up_gate(k, first):
                f = c.get("f")
                if not first:
                    act.wait_ge(s_conv, f - 1)
                    act.wait_ge(s_tail, f - 1)
                at = bass.ds(f, 1)
                act.activation(a_ext[:, k, SEQ + 2:SEQ + 4], conv_w[:, 3:5, at].rearrange("p i f -> p (i f)"),
                               copy).then_inc(s_hist, 1)
                act.wait_ge(s_hist, f + 1)
                act.wait_ge(s_up, f + 1)
                act.wait_ge(s_prod, f + (2 * FFN_GROUP - 1) if not first else 2 * FFN_GROUP)
                act.activation(conv[:, k, 2:EXT], a_ext[:, k, 2:EXT], ACT.Identity, bias=ffn_c[:, at],
                               scale=conv_w[:, 2, at]).then_inc(s_c0, 1)

            def up_value():
                f = c.get("f")
                act.wait_ge(s_conv, f + 1)
                k = c.slot("f")
                act.activation(conv[:, k, 2:EXT], conv[:, k, 2:EXT], ACT.Gelu_apprx_tanh).then_inc(s_gelu, 1)

            pro, body, reps, epi = FFN
            for k in range(2):
                split_hi()
                up_gate(k, True)
                c.block("dve")
                split_hi()
                up_value()
                c.block("dve")
                c.add("f")
            with c.loop(act, reps, body, g=1, f=2):
                for k in range(2):
                    split_hi()
                    if k == 0:
                        group_hi(c.get("g"))
                    up_gate(k, False)
                    c.block("dve")
                    split_hi()
                    up_value()
                    c.block("dve")
                    split_hi()
                    c.block("group")
                    c.add("f")
                c.add("g")
            split_hi()
            group_hi(c.get("g"))
            c.block("group")
            c.block("group")

            act.wait_ge(s_tail_t, 1)
            act.activation(conv_rows[:].rearrange("r q p -> r (q p)"), pex[0:2 * FT, 0, 0:2 * P], copy).then_inc(s_tail_r, 2)
            for n in range(NT):
                r = rows_of(n)
                act.wait_ge(s_yt, n + 1)
                if n >= 1:
                    act.wait_ge(s_ysq, n)
                act.activation(y_junk[0:r, :].rearrange("p (b c) -> p b c", b=2), (pex, *pset)[n % 3][0:r, 0:2, :], ACT.Square,
                               accum_out=stat_y[0:r, 0, n:n + 1]).then_inc(s_ysq, 1)

        @block.vector
        def _(dve):
            for key, n in ((s_freed["freed", "dve", 0], 1), (s_freed["freed", "dve", 1], 1), (s_m1, 2)):
                dve.sem_inc(key, n)

            def h_lo_part(n):
                r = rows_of(n)
                dve.wait_ge(s_h_hi, n + 1)
                for b in range(2):
                    at = (slice(None), slice(4 * b, 4 * b + 4), slice(n * P, n * P + r))
                    last = dve.tensor_tensor(h_lo[at], pset[n % 2][:, b, :].rearrange("p (k t) -> p k t", k=4)[:, :, 0:r],
                                             h_hi[at].bitcast(F32), ALU.subtract)
                last.then_inc(s_h, 1)

            dve.wait_ge(s_row_in, 16)
            def wide_lo_part(w, dst, hi, src=wraw):
                dve.wait_ge(s_wide_hi, w + 1)
                dve.tensor_tensor(dst, src[:], hi.bitcast(F32), ALU.subtract).then_inc(s_wide, 1)

            for n in range(NT):
                r = rows_of(n)
                dve.wait_ge(s_rstd, n + 1)
                dve.wait_ge(s_x_in[n % 4], 16 * (n // 4 + 1))
                if n >= 2:
                    dve.wait_ge(s_xnt, n - 1)
                dve.scalar_tensor_tensor(xn[0:r, n % 2, :], x_slot(n), stat[0:r, 2, n:n + 1], mix_g[0:r, :],
                                         ALU.mult, ALU.mult).then_inc(s_xn, 1)
                if n >= 1:
                    h_lo_part(n - 1)
                if n == 2:
                    wide_lo_part(0, wide_lo[:, 0], wide_hi[:, 0])
                if n == NT - 2:
                    wide_lo_part(1, wide_lo[:, 1], wide_hi[:, 1])
            h_lo_part(NT - 1)
            dve.wait_ge(s_ws_t, 1)
            dve.memset(ws_t[64:P, :, 0:64], 0.0).then_inc(s_ws, 1)
            for w in range(2, 4):
                wide_lo_part(w, wide_lo[:, w % 2], wide_hi[:, w % 2])

            c = Count()

            def split_lo(ahead=1):
                s = (c.slot() + ahead) % 2
                dve.wait_ge(s_w_hi, c.get("block") + (ahead + 1))
                dve.tensor_tensor(w_lo[:, s, :], raw[:, s, :], w_hi[:, s, :].bitcast(F32), ALU.subtract).then_inc(s_w, 1)

            def group_lo(g):
                for k in range(2):
                    dve.wait_ge(s_grp_hi, g * 2 + (k + 1))
                    dve.tensor_tensor(grp_lo[:, k, :], grp[:, k, :], grp_hi[:, k, :].bitcast(F32),
                                      ALU.subtract).then_inc(s_grp, 1)

            def add_group(dst, b, after=None, split=True):
                for q in range(4):
                    if q == 2 and split:
                        split_lo()
                    dve.wait_ge(s_tile, c.get("tile") + 1)
                    s = c.slot("tile")
                    for d, v in zip(halves(dst[:, 4 * b + q, :]), pieces(s)):
                        last = dve.tensor_tensor(d, v, d, ALU.add)
                    last.then_inc(s_freed["freed", "dve", s], 1)
                    c.tile("group")
                    if after:
                        after(4 * b + q)
                c.add("block")

            def evacuated(k):
                key = ("freed", "act", c.slot("tile"))
                dve.wait_ge(s_freed[key], c.get(key) + 2)

            def mix(project, dst, between=None, early=None, first=1, after=None):
                pro, body, reps, epi = MIX
                for k in range(2):
                    if k >= 1 - first:
                        split_lo()
                    if not between:
                        project(k)
                    c.block(pro[k])
                    c.add("kt")
                if between:
                    between()
                with c.loop(dve, reps, body, g=1, kt=2):
                    for k in range(2):
                        split_lo()
                        if k == 0:
                            group_lo(c.get("g"))
                        project(k)
                        c.block("act")
                        c.add("kt")
                        add_group(dst, k)
                    c.add("g")
                if early:
                    split_lo()
                group_lo(c.get("g"))
                if early:
                    for k in range(2):
                        early(k)
                        c.block("act")
                        if k == 0:
                            split_lo()
                add_group(dst, 0, after)
                c.add("g")
                add_group(dst, 1, after)

            def values():
                dve.wait_ge(s_row_in, 16 * 5)
                for n in range(NT):
                    r = rows_of(n)
                    dve.wait_ge(s_vt_free, 3 * NT + n + 1 + 3)
                    if n >= 1:
                        dve.wait_ge(s_ln_mv, n)
                    for b in range(2):
                        last = dve.bn_stats(ln_stats[0:r, 0, b, :], gs[0:r, n, 512 * b:512 * b + 512])
                    last.then_inc(s_ln, 1)
                    dve.wait_ge(s_ln, n + 1)
                    dve.bn_aggr(ln_mv[0:r, n, :], ln_stats[0:r, 0]).then_inc(s_ln_mv, 1)
                    dve.wait_ge(s_ln_mv, n + 1)
                    dve.scalar_tensor_tensor(gs[0:r, n, :], gs[0:r, n, :], ln_mv[0:r, n, 0:1], lnv_g[0:r, :],
                                             ALU.subtract, ALU.mult).then_inc(s_ln_a, 1)
                    dve.wait_ge(s_ln_a, n + 1)
                    dve.wait_ge(s_ln_r, n + 1)
                    dve.scalar_tensor_tensor(gs[0:r, n, :], gs[0:r, n, :], ln_rstd[0:r, n:n + 1], lnv_b[0:r, :],
                                             ALU.mult, ALU.add).then_inc(s_vn, 1)

            def mixed():
                for n in range(NT):
                    r = rows_of(n)
                    src = (pex, *pset)[n % 3]
                    dve.wait_ge(s_mixed, n + 1)
                    if n == NT - 1:
                        dve.wait_ge(s_vnout, 16)
                    for b in range(2):
                        last = dve.tensor_tensor(
                            gs[:, n, 512 * b:512 * b + 512].rearrange("p (g t) -> p g t", g=4)[:, :, 0:r],
                            src[:, b, :].rearrange("p (g t) -> p g t", g=4)[:, :, 0:r],
                            bs[:, 4 * b:4 * b + 4, 0:r], ALU.add)
                    last.then_inc(s_s, 1)
                dve.wait_ge(s_s, NT)
                for k in range(2):
                    product(k, k)
                dve.wait_ge(s_zero, 5)

            def product(k, kt):
                at = kt * P
                p = grp[:, k, 0:SEQ].rearrange("p (n t) -> p n t", t=P)
                dve.tensor_tensor(p, p, gs[:, 0:NT - 1, bass.ds(at, P)], ALU.mult)
                p = grp[:, k, SEQ:T]
                dve.tensor_tensor(p, p, gs[:, NT - 1, bass.ds(at, DEC)], ALU.mult).then_inc(s_prod, 1)

            def project_u(k):
                evacuated(k)
                product(k, c.get("kt"))

            split_lo(0)
            split_lo(1)
            values()
            gate_in = []

            def gate_early(k):
                key = ("freed", "act", c.slot("tile"))
                gate_in.append((s_freed[key], c.get(key) + 2))

            mix(project_u, acc, between=mixed, early=gate_early, first=0)

            def gated(m, k):
                a = acc[:, bass.ds(m, 1), :].rearrange("p a t -> p (a t)")
                dve.tensor_tensor(a, a, gate[:, k, :], ALU.mult).then_inc(s_m1, 1)

            for k, (key, value) in enumerate(gate_in):
                dve.wait_ge(key, value)
                gated(k, k)
            c.v["m"] = 2
            with c.loop(dve, GATE[2], GATE[1], m=2):
                for k in range(2):
                    split_lo()
                    evacuated(k)
                    gated(c.get("m"), k)
                    c.block("act")
                    c.add("m")
            wide_lo_part(4, k_pair[1][:], k_pair[0][:], kv_raw)
            for k in range(2):
                split_lo()
                evacuated(k)
                gated(c.get("m"), k)
                c.block("act")
                c.add("m")
                if k == 0:
                    wide_lo_part(5, v_pair[1][:], v_pair[0][:], kv_raw)

            for n in range(NT + 1):
                r = (rows_of(n) if n < NT else CACHE)
                col = n * P if n < NT - 1 else (SEQ + CACHE if n == NT - 1 else SEQ)
                dve.wait_ge(s_ktr, n + 1)
                dve.tensor_copy(k_t[:, :, col:col + r],
                                pex[:, n % 2, 0:256].rearrange("p (k t) -> p k t", k=2)[:, :, 0:r]).then_inc(s_kt, 1)
            dve.wait_ge(s_dist, 1)
            dve.tensor_copy(bias_now[:, 0, :], dist[:].bitcast(mybir.dt.int32)).then_inc(s_distf, 1)
            dve.wait_ge(s_distf, 1)
            dve.scalar_tensor_tensor(dist[:], bias_now[:, 0, :], -1.0, bias_now[:, 0, :], ALU.mult,
                                     ALU.max).then_inc(s_distf, 1)

            dve.wait_ge(s_dist, 3)
            dve.wait_ge(s_zero, 6)
            dve.wait_ge(s_kv_out, 64)
            with c.loop(dve, ATT[2], ATT[1], att=NT, den=2 * NT) as (pair, half):
                for k in range(2):
                    split_lo()
                    c.block("act")
                for e in range(4):
                    at = bass.ds(pair * 8 + half * 2 + (4 * (e // 2) + e % 2), 1)
                    dve.tensor_scalar(bias_now[:, e, :], dist[:], slopes[:, at], None, ALU.mult)
                    last = dve.tensor_copy(sink_now[:, e:e + 1], sinks[:, at])
                last.then_inc(s_bias, 1)
                dve.wait_ge(s_bias, c.i + 1)
                for step in range(NT + 4):
                    if step < NT:
                        n, a = step, att_stat[:, step % 2]
                        w, b0 = keys_of(n)[1], keys_of(n)[2]
                        src = pset[n % 2]
                        if n >= 3:
                            dve.wait_ge(s_ptr, c.get("att") + (n - 2))
                        dve.wait_ge(s_sc, c.get("att") + n + 1)
                        dve.tensor_copy(spare[:, 3:4], sink_now[:, 0:1])
                        for e in range(4):
                            last = dve.tensor_tensor_reduce(
                                sc_sb[:, n % 3, e, 0:w], src[:, e // 2, 256 * (e % 2):256 * (e % 2) + w],
                                bias_now[:, e, b0:b0 + w], 1.0, sink_now[:, e:e + 1], ALU.add, ALU.max,
                                a[:, 0, e:e + 1])
                        last.then_inc(s_smax, 1)
                        dve.wait_ge(s_smax, c.get("att") + n + 1)
                        dve.tensor_scalar(a[:, 1, :], a[:, 0, :], -1.0, None, ALU.mult)
                        dve.tensor_tensor(a[:, 2, :], sink_now[:, :], a[:, 0, :], ALU.subtract).then_inc(s_neg, 1)
                    if 1 <= step <= NT:
                        n, a = step - 1, att_stat[:, (step - 1) % 2]
                        w = keys_of(n)[1]
                        dve.wait_ge(s_exp, c.get("att") + n + 1)
                        dve.tensor_tensor(a[:, 5, :], a[:, 3, :], a[:, 4, :], ALU.add).then_inc(s_den, 1)
                        dve.wait_ge(s_den, c.get("den") + 1)
                        dve.reciprocal(a[:, 6, :], a[:, 5, :]).then_inc(s_den, 1)
                        dve.wait_ge(s_den, c.get("den") + 2)
                        c.add("den", 2)
                        for e in range(4):
                            p = sc_sb[:, n % 3, e, 0:w]
                            last = dve.tensor_scalar(p, p, a[:, 6, e:e + 1], None, ALU.mult)
                        last.then_inc(s_p, 1)
                    if step >= 4:
                        n, r, q0 = step - 4, rows_of(step - 4), queries_of(step - 4)[1]
                        dve.wait_ge(s_b_hi, c.get("att") + n + 1)
                        at = (slice(None), slice(None), slice(n * P, n * P + r))
                        dve.tensor_tensor(grp_lo[at], pset[n % 2][:, 2, 0:256].rearrange("p (k q) -> p k q", k=2)[:, :, q0:P],
                                          grp_hi[at].bitcast(F32), ALU.subtract).then_inc(s_b, 1)
                c.add("att", NT)
                for b in range(2):
                    add_group(acc, b)

            c.v["kt"] = 0

            def merge(k):
                evacuated(k)
                a = acc[:, bass.ds(c.get("kt"), 1), :].rearrange("p a t -> p (a t)")
                dve.tensor_tensor(grp[:, k, :], grp[:, k, :], a, ALU.mult).then_inc(s_gb, 1)
                dve.wait_ge(s_gb, c.get("kt") + 1)
                dve.wait_ge(s_m1_in[k], c.get("kt", 2) * 16 + 16)
                dve.tensor_tensor(grp[:, k, :], grp[:, k, :], m1[:, k, :], ALU.add).then_inc(s_prod, 1)

            def h2_lo_part(kt):
                dve.wait_ge(s_h2_hi, kt + 1)
                dve.scalar_tensor_tensor(h2_lo[:, kt, :], xres[:, kt, :], ffn_c[:, FT + kt:FT + kt + 1],
                                         h2_hi[:, kt, :].bitcast(F32), ALU.mult, ALU.subtract).then_inc(s_h2, 1)

            mix(merge, xres, after=lambda kt: h2_lo_part(kt - 1) if kt else None)
            h2_lo_part(KT - 1)

            def norm_factor():
                dve.wait_ge(s_ms, 1)
                dve.tensor_scalar(stat[:, 1, 0:NT - 1], pex[:, 0, 0:NT - 1], 1.0, EPS, ALU.mult, ALU.add)
                dve.tensor_scalar(stat[0:DEC, 1, NT - 1:NT], pex[0:DEC, 0, NT - 1:NT], 1.0, EPS, ALU.mult,
                                  ALU.add).then_inc(s_r0, 1)
                dve.wait_ge(s_r2, 1)
                dve.tensor_copy(rb[:, 0:SEQ].rearrange("p (b n) -> p b n", b=2), pset[1][:, 0:2, :])
                dve.tensor_copy(rb[:, SEQ:T], pset[1][:, 2, 0:DEC]).then_inc(s_rb, 1)
                dve.wait_ge(s_rb, 1)

            def ext_pieces(t, s):
                p0, p1 = pieces(s)
                cut = SEQ - 2 * NB
                return ((t[:, 2:2 + 2 * NB].rearrange("p (b n) -> p b n", b=2), p0, halves(rb[:])[0]),
                        (t[:, 2 + 2 * NB:2 + SEQ], p1[:, 0:cut], rb[:, 2 * NB:SEQ]),
                        (t[:, SAMP:EXT], p1[:, cut:], rb[:, SEQ:T]))

            def up_gate(k, first=False):
                f, s = c.get("f"), c.slot("tile")
                at = bass.ds(f, 1)
                dve.wait_ge(s_tile, c.get("tile") + 1)
                if not first:
                    dve.wait_ge(s_tail, f - 1)
                for d, v, m in ext_pieces(a_ext[:, k], s):
                    last = dve.tensor_tensor(d, v, m, ALU.mult)
                last.then_inc(s_freed["freed", "dve", s], 1)
                dve.tensor_copy(spare[:, 2:3], half_neg[:]).then_inc(s_up, 1)
                dve.wait_ge(s_c0, f + 1)
                cv = conv[:, k, 2:EXT]
                dve.scalar_tensor_tensor(cv, a_ext[:, k, 1:EXT - 1], conv_w[:, 1, at], cv, ALU.mult, ALU.add).then_inc(s_c1, 1)
                dve.wait_ge(s_c1, f + 1)
                dve.scalar_tensor_tensor(cv, a_ext[:, k, 0:EXT - 2], conv_w[:, 0, at], cv, ALU.mult, ALU.add).then_inc(s_conv, 1)

            def up_value(k):
                f, s = c.get("f"), c.slot("tile")
                dve.wait_ge(s_gelu, f + 1)
                (d0, p0, r0), (d1, p1, r1), (d2, p2, r2) = ext_pieces(conv[:, k], s)
                for d, r in ((d0, r0), (d1, r1), (d2, r2)):
                    last = dve.tensor_tensor(d, d, r, ALU.mult)
                last.then_inc(s_gr, 1)
                dve.wait_ge(s_gr, f + 1)
                dve.wait_ge(s_tile, c.get("tile") + 1)
                g = grp[:, k, :]
                dve.tensor_tensor(halves(g)[0], p0, d0, ALU.mult)
                dve.tensor_tensor(g[:, 2 * NB:SEQ], p1, d1, ALU.mult)
                dve.tensor_tensor(g[:, SEQ:T], p2, d2, ALU.mult).then_inc(s_freed["freed", "dve", s], 1)
                dve.tensor_copy(spare[:, 3:4], half_neg[:]).then_inc(s_prod, 1)

            dve.wait_ge(s_zext, 1)
            pro, body, reps, epi = FFN
            for k in range(2):
                split_lo()
                if k == 0:
                    norm_factor()
                up_gate(k, True)
                c.block("dve")
                split_lo()
                up_value(k)
                c.block("dve")
                c.add("f")
            with c.loop(dve, reps, body, g=1, f=2):
                for k in range(2):
                    split_lo()
                    if k == 0:
                        group_lo(c.get("g"))
                    up_gate(k)
                    c.block("dve")
                    split_lo()
                    up_value(k)
                    c.block("dve")
                    add_group(xres, k)
                    c.add("f")
                c.add("g")
            group_lo(c.get("g"))
            add_group(xres, 0)
            add_group(xres, 1, split=False)

            dve.wait_ge(s_fin_g, 16)
            for n in range(NT):
                r = rows_of(n)
                dve.wait_ge(s_yr, n + 1)
                if n >= 4:
                    dve.wait_ge(s_y_out[n % 4], 16 * (n // 4))
                dve.scalar_tensor_tensor(y_sb[0:r, n % 4, :].rearrange("p (b c) -> p b c", b=2), (pex, *pset)[n % 3][0:r, 0:2, :],
                                         stat_y[0:r, 2, n:n + 1], fin_g[0:r, :].rearrange("p (b c) -> p b c", b=2),
                                         ALU.mult, ALU.mult).then_inc(s_y, 1)

        @block.tensor
        def _(pe):
            def products(out, lhs, rhs, first=True, last=True):
                for n, (a, b) in enumerate(((0, 0), (0, 1), (1, 0))):
                    mm = pe.matmul(out, lhs[a], rhs[b], start=first and n == 0, stop=last and n == 2)
                return mm

            def wide_tile(w, n, pair, bank):
                r = rows_of(n)
                pe.wait_ge(s_vt_free, NT * w + n + 1)
                for kt in range(KT):
                    last = products(bank[0:r, 0:256], [h[:, kt, n * P:n * P + r] for h in (h_hi, h_lo)],
                                    [v[:, kt, :] for v in pair], kt == 0, kt == KT - 1)
                last.then_inc(s_vt, 1)

            pe.wait_ge(s_ident, 1)
            for n in range(NT + 2):
                if n < NT:
                    r = rows_of(n)
                    pe.wait_ge(s_xn, n + 1)
                    if n >= 2:
                        pe.wait_ge(s_h, n - 1)
                    for kt in range(KT):
                        last = pe.transpose(pset[n % 2][:, kt // 4, kt % 4 * P:kt % 4 * P + r],
                                            xn[0:r, n % 2, kt * P:kt * P + P], ident[0:r, 0:r])
                    last.then_inc(s_xnt, 1)
                if n == 2:
                    pe.wait_ge(s_wide, 1)
                if n >= 2:
                    pe.wait_ge(s_h, n - 1)
                    wide_tile(0, n - 2, (wide_hi[:, 0], wide_lo[:, 0]), v_bank(n - 2))
            pe.wait_ge(s_tab_in, 16 * 5)
            for g in range(KT):
                pe.transpose(pset[0][:, g // 4, g % 4 * P:g % 4 * P + P], ws_raw[:, g, :], ident[:])
            pe.transpose(pset[1][:, 0, 0:5 * FT], tab_rows[0:5 * FT, 0, :], ident[0:5 * FT, 0:5 * FT])
            pe.transpose(pset[1][:, 0, P:P + FT + KT], tab_rows[0:FT + KT, 1, :], ident[0:FT + KT, 0:FT + KT]).then_inc(s_tab_t, 1)
            for w in range(1, 4):
                pe.wait_ge(s_wide, w + 1)
                for n in range(NT):
                    wide_tile(w, n, (wide_hi[:, w % 2], wide_lo[:, w % 2]), v_bank(n))
            pe.wait_ge(s_ws_t, 1)

            c = Count()
            TB = [(b, b * NB, min(T, b * NB + NB)) for b in range(3)]
            PASSES = ((0, 0), (0, 1), (1, 0))
            w_pair = (w_hi, w_lo)

            def set_free():
                s = c.slot("tile")
                for e in ("act", "dve"):
                    key = ("freed", e, s)
                    pe.wait_ge(s_freed[key], c.get(key) + 1)
                return s

            def project(kind, x_pair, ready=None, after=None):
                pe.wait_ge(s_w, c.get("block") + 1)
                ws, s = c.slot(), set_free()
                for kt in range(KT):
                    if ready is not None:
                        pe.wait_ge(ready, kt + 1)
                    for n, (a, b) in enumerate(PASSES):
                        for blk, t0, t1 in TB:
                            last = pe.matmul(pset[s][:, blk, 0:t1 - t0], w_pair[a][:, ws, kt * P:kt * P + P],
                                             x_pair[b][:, kt, t0:t1], start=kt == 0 and n == 0,
                                             stop=kt == KT - 1 and n == 2)
                    if kt == KT - 1:
                        last.then_inc(s_tile, 1)
                    if after:
                        after(kt)
                c.block(kind)

            ALL = [(k, n) for k in range(2) for n in range(3)]

            def group_tile(ws, q, s, ks_passes, first=True, last=True, blks=(0, 1, 2)):
                for i, (k, n) in enumerate(ks_passes):
                    a, b = PASSES[n]
                    for blk, t0, t1 in [TB[x] for x in blks]:
                        mm = pe.matmul(pset[s][:, blk, 0:t1 - t0],
                                       w_pair[a][:, ws, 512 * k + P * q:512 * k + P * q + P],
                                       (grp_hi, grp_lo)[b][:, k, t0:t1], start=first and i == 0,
                                       stop=last and i == len(ks_passes) - 1)
                return mm

            def group(g=None, att=None, begun=0):
                pe.wait_ge(s_w, c.get("block") + 1)
                if att is not None:
                    pe.wait_ge(s_b, att)
                ws = c.slot()
                for q in range(4):
                    s = set_free()
                    if q or g is None:
                        last = group_tile(ws, q, s, ALL, blks=(2,) if q < begun else (0, 1, 2))
                    else:
                        for k in range(2):
                            pe.wait_ge(s_grp_hi, g * 2 + (k + 1))
                            group_tile(ws, q, s, [(k, 0), (k, 2)], k == 0, False)
                        for k in range(2):
                            pe.wait_ge(s_grp, g * 2 + (k + 1))
                            last = group_tile(ws, q, s, [(k, 1)], False, k == 1)
                    last.then_inc(s_tile, 1)
                    c.tile("group")
                c.add("block")

            def mix(between=None, early=0, after=None):
                pro, body, reps, epi = MIX
                for k in range(2):
                    if between and k == 1:
                        pe.wait_ge(s_vt_free, 4 * NT + 3)
                    project(pro[k], (h_hi, h_lo), after=after and (lambda kt, k=k: after(k, kt)))
                if between:
                    between()
                with c.loop(pe, reps, body, g=1):
                    for k in range(2):
                        project("act", (h_hi, h_lo))
                        group(c.get("g"))
                    c.add("g")
                for _ in range(early):
                    project("act", (h_hi, h_lo))
                for b in range(2):
                    group(c.get("g"))
                c.add("g")

            def spatial():
                pe.wait_ge(s_ws, 1)
                for n in range(NT):
                    r, dst = rows_of(n), (pex, *pset)[n % 3]
                    if n in (1, 2):
                        key = ("freed", "act", n - 1)
                        pe.wait_ge(s_freed[key], c.get(key) + 1)
                    pe.wait_ge(s_vn, n + 1)
                    if n >= 3:
                        pe.wait_ge(s_s, n - 2)
                    for g in range(KT):
                        last = pe.matmul(dst[:, g // 4, g % 4 * P:g % 4 * P + r], gs[0:r, n, g * P:g * P + P],
                                         ws_t[0:r, g, 0:r], start=True, stop=True)
                    last.then_inc(s_mixed, 1)
                pe.wait_ge(s_s, NT - 1)

            mix(between=spatial, early=2)
            with c.loop(pe, GATE[2], GATE[1]):
                for k in range(2):
                    project("act", (h_hi, h_lo))
            for k in range(2):
                project("act", (h_hi, h_lo))

            key = ("freed", "act", 0)
            pe.wait_ge(s_freed[key], c.get(key) + 1)

            def transpose_k(n):
                r = rows_of(n) if n < NT else CACHE
                if n < NT:
                    pe.wait_ge(s_vt_free, 4 * NT + n + 1 + 3)
                else:
                    pe.wait_ge(s_cache, 32)
                if n >= 2:
                    pe.wait_ge(s_kt, n - 1)
                for p in range(2):
                    last = pe.transpose(pex[:, n % 2, p * P:p * P + r],
                                        k_tok[0:r, n % 2 if n < NT else 2, p * P:p * P + P], ident[0:r, 0:r])
                last.then_inc(s_ktr, 1)

            pe.wait_ge(s_wide, 5)
            for n in range(NT):
                wide_tile(4, n, [v[:] for v in k_pair], pset[0][:, n % 3])
                if n:
                    transpose_k(n - 1)
            pe.wait_ge(s_wide, 6)
            for n in range(NT):
                wide_tile(5, n, [v[:] for v in v_pair], pset[0][:, n % 3])
                if n < 2:
                    transpose_k(NT - 1 + n)
            pe.wait_ge(s_vt_free, 6 * NT + 3)
            pe.wait_ge(s_kt, NT + 1)

            with c.loop(pe, ATT[2], ATT[1], att=NT) as (pair, half):
                for k in range(2):
                    project("act", (h_hi, h_lo))
                pe.wait_ge(s_now, pair * 3 + 3)
                for step in range(NT + 3):
                    if step == NT:
                        pe.wait_ge(s_w, c.get("block") + 1)
                        pe.wait_ge(s_smax, c.get("att") + NT)
                        pe.wait_ge(s_b, c.get("att") + 3)
                        for q in range(2):
                            group_tile(c.slot(), q, q, ALL, blks=(0,))
                    if step > NT:
                        pe.wait_ge(s_b, c.get("att") + 6)
                        group_tile(c.slot(), step - NT - 1, step - NT - 1, ALL, blks=(1,))
                    if step < NT:
                        n, q0 = step, queries_of(step)[0]
                        k0, w, _ = keys_of(n)
                        dst = pset[n % 2]
                        if n >= 2:
                            pe.wait_ge(s_smax, c.get("att") + (n - 1))
                        for k in range(2):
                            if n == 0:
                                key = ("freed", "act", k)
                                pe.wait_ge(s_freed[key], c.get(key) + 1)
                            for h in range(2):
                                last = pe.matmul(dst[:, h, 256 * k:256 * k + w],
                                                 grp[64 * h:64 * h + 64, k, q0:q0 + P],
                                                 k_now[64 * h:64 * h + 64, k0:k0 + w], start=True, stop=True)
                        last.then_inc(s_sc, 1)
                    if step >= 3:
                        n = step - 3
                        pe.wait_ge(s_pt, c.get("att") + n + 1)
                        if n >= 2:
                            pe.wait_ge(s_b, c.get("att") + (n - 1))
                        tiles = key_tiles(n)
                        for h in range(2):
                            for j, (slot, rows) in enumerate(tiles):
                                last = pe.matmul(
                                    pset[n % 2][64 * h:64 * h + 64, 2, 0:256].rearrange("p (k q) -> p k q", k=2)[:, :, :],
                                    v_now[0:rows, slot, 64 * h:64 * h + 64],
                                    pt_sb[0:rows, j, 2 * h:2 * h + 2, :],
                                    start=j == 0, stop=j == len(tiles) - 1)
                        last.then_inc(s_o, 1)
                    if 2 <= step <= NT + 1:
                        n = step - 2
                        pe.wait_ge(s_p, c.get("att") + n + 1)
                        for j, (_, rows) in enumerate(key_tiles(n)):
                            for e in range(4):
                                last = pe.transpose(pex[0:rows, j, e * P:e * P + P],
                                                    sc_sb[:, n % 3, e, j * P:j * P + rows], ident[:])
                        last.then_inc(s_ptr, 1)
                c.add("att", NT)
                for b in range(2):
                    group(att=c.get("att"), begun=2 if b == 0 else 0)

            def residual(k, kt):
                n = kt - 3 if k == 0 else kt + 5
                if not (0 <= n < 5 if k == 0 else n < NT):
                    return
                r = rows_of(n)
                pe.wait_ge(s_x2_in[n % 2], 16 * (n // 2 + 1))
                if n >= 1:
                    pe.wait_ge(s_x2, n)
                for q in range(KT):
                    last = pe.transpose(pex[:, q // 4, q % 4 * P:q % 4 * P + r],
                                        xt2[0:r, n % 2, q * P:q * P + P], ident[0:r, 0:r])
                last.then_inc(s_x2t, 1)

            mix(after=residual)

            def mean_squares(kt):
                if kt == KT - 3:
                    pe.wait_ge(s_ssum, KT - 1)
                    for n in range(NT):
                        last = pe.matmul(pex[0:rows_of(n), 0, n:n + 1], ssum[:, n * P:n * P + rows_of(n)], mean_col[:],
                                         start=True, stop=True)
                    last.then_inc(s_ms, 1)
                if kt == KT - 2:
                    key = ("freed", "dve", 1)
                    pe.wait_ge(s_freed[key], c.get(key) + 1)
                    pe.wait_ge(s_r1, 1)
                    for n in range(NT):
                        r = rows_of(n)
                        last = pe.matmul(pset[1][:, n // 4, n % 4 * P:n % 4 * P + r],
                                         stat[0:r, 2, n:n + 1].broadcast_to([r, P]), ident[0:r, 0:r], start=True, stop=True)
                    last.then_inc(s_r2, 1)

            pro, body, reps, epi = FFN
            for n, kind in enumerate(pro):
                if n == 0:
                    project(kind, (h2_hi, h2_lo), s_h2, mean_squares)
                    pe.wait_ge(s_rb, 1)
                else:
                    project(kind, (h2_hi, h2_lo))
            with c.loop(pe, reps, body, g=1):
                for kind in body:
                    if kind == "group":
                        group(c.get("g"))
                    else:
                        project(kind, (h2_hi, h2_lo))
                c.add("g")
            for b in range(2):
                group(c.get("g"))
                if b == 0:
                    pe.wait_ge(s_tail, FT)
                    for q in range(2):
                        last = pe.transpose(pex[0:2 * FT, 0, q * P:q * P + P], conv_out[:, q].rearrange("p i f -> p (i f)"), ident[:])
                    last.then_inc(s_tail_t, 1)

            pe.wait_ge(s_tail_r, 2)
            key = ("freed", "dve", 0)
            pe.wait_ge(s_freed[key], c.get(key) + 1)
            for n in range(NT):
                r = rows_of(n)
                if n >= 3:
                    pe.wait_ge(s_y, n - 2)
                for kt in range(KT):
                    if n == 0 and kt == KT - 1:
                        key = ("freed", "dve", 1)
                        pe.wait_ge(s_freed[key], c.get(key) + 1)
                    last = pe.transpose((pex, *pset)[n % 3][0:r, kt // 4, kt % 4 * P:kt % 4 * P + P],
                                        xres[:, kt, n * P:n * P + r], ident[:])
                last.then_inc(s_yt, 1)


_INS = ["x_prompt", "x_sample", "cache_k", "cache_v", "cache_conv", "ln_mix_g", "w_in", "ln_v_g", "ln_v_b", "w_s",
        "b_s", "attn_sinks", "w_pa", "w_pb", "w_o", "ln_ffn_g", "w_up", "w_conv", "b_conv", "w_down", "ln_final_g"]
_OUTS = [(1, SEQ, D), (1, DEC, D), (1, 1, 128, KVH, HD), (1, 1, 128, KVH, HD), (1, 1, 2, FF),
         (1, 1, DEC, KVH, HD), (1, 1, DEC, KVH, HD), (1, 1, 2, FF), (1, 1, DEC, D)]


def kernel(**inputs):
    import numpy as _np
    import concourse.bacc as _bacc
    from concourse import mybir as _mybir
    from concourse.bass_utils import run_bass_kernel_spmd as _run

    nc = _bacc.Bacc("TRN2", target_bir_lowering=False, num_devices=1)
    arrays, args = {}, []
    for name in _INS:
        a = _np.ascontiguousarray(inputs[name])
        arrays[f"in_{name}_dram"] = a
        args.append(nc.dram_tensor(f"in_{name}_dram", a.shape, _mybir.dt.from_np(a.dtype), kind="ExternalInput").ap())
    for i, shape in enumerate(_OUTS):
        args.append(nc.dram_tensor(f"out_{i}_dram", shape, _mybir.dt.float32, kind="ExternalOutput").ap())
    args.append(nc.dram_tensor("m1_spill", (KT, P, T), _mybir.dt.float32, kind="Internal").ap())
    program(nc, *args)
    r = _run(nc, [arrays], core_ids=[0])
    return tuple(r.results[0][f"out_{i}_dram"] for i in range(len(_OUTS)))
```
